# Optimizing a Trainium2 kernel written in Bass

```python
import math
import jax, jax.numpy as jnp
from jax import lax
import numpy as np

D_MODEL = 2048
BATCH = 1
SEQ = 256
DEPTH = 2

MEM_LEN = 256
DN_HEADS = 8
DN_HEAD_DIM = 128
DN_WIDTH = DN_HEADS * DN_HEAD_DIM
DN_CONV = 4
DN_CHUNK = 64
CV_WIDTH = D_MODEL // 2
CV_KERNEL = 31
SB_HEADS = 16
SB_HEAD_DIM = D_MODEL // SB_HEADS
SB_WIDTH = SB_HEADS * SB_HEAD_DIM
SB_BLOCK = 128
MEM_HEADS = 4
MEM_HEAD_DIM = D_MODEL // 8
MEM_WIDTH = MEM_HEADS * MEM_HEAD_DIM

N_EVEN = (DEPTH + 1) // 2
N_ODD = DEPTH // 2
EVEN_IN = 3 * DN_WIDTH + DN_WIDTH + 2 * DN_HEADS + 2 * CV_WIDTH + CV_WIDTH + 2 * MEM_WIDTH
EVEN_MIX = DN_WIDTH + CV_WIDTH + MEM_WIDTH
ODD_IN = 3 * SB_WIDTH + SB_WIDTH + 2 * MEM_WIDTH
ODD_MIX = SB_WIDTH + MEM_WIDTH
EPS = 1e-6

kernel_name = "hybrid_deltanet_conformer_stickbreak_memory"

def rms_norm(x, g):
    xf = x.astype(jnp.float32)
    y = xf * lax.rsqrt(jnp.mean(xf * xf, axis=-1, keepdims=True) + EPS)
    return (y * g.astype(jnp.float32)).astype(x.dtype)

def layer_norm(x, g, b):
    xf = x.astype(jnp.float32)
    mu = jnp.mean(xf, axis=-1, keepdims=True)
    xc = xf - mu
    y = xc * lax.rsqrt(jnp.mean(xc * xc, axis=-1, keepdims=True) + EPS)
    return (y * g.astype(jnp.float32) + b.astype(jnp.float32)).astype(x.dtype)

def l2_norm(x):
    return x * lax.rsqrt(jnp.sum(x * x, axis=-1, keepdims=True) + EPS)

def causal_depthwise_conv(x, w):
    ksz, ch = w.shape
    return lax.conv_general_dilated(
        x, w.astype(x.dtype)[:, None, :], window_strides=(1,), padding=[(ksz - 1, 0)],
        dimension_numbers=("NWC", "WIO", "NWC"), feature_group_count=ch)

def gated_delta_rule(q, k, v, beta, g):
    bsz, seq, nh, dk = q.shape
    dv = v.shape[-1]
    n_chunks = seq // DN_CHUNK

    def chunk(t):
        t = t.reshape((bsz, n_chunks, DN_CHUNK, nh) + t.shape[3:])
        return jnp.moveaxis(t, 3, 1)

    q, k, v, beta, g = chunk(q), chunk(k), chunk(v), chunk(beta), chunk(g)
    gc = jnp.cumsum(g, axis=-1)
    idx = jnp.arange(DN_CHUNK)
    causal = idx[:, None] >= idx[None, :]
    strict = idx[:, None] > idx[None, :]
    decay = jnp.exp(jnp.where(causal, gc[..., :, None] - gc[..., None, :], -jnp.inf))
    kb = k * beta[..., None]
    a_mat = jnp.where(strict, jnp.einsum('bhnid,bhnjd->bhnij', kb, k) * decay, 0.0)
    eye = jnp.eye(DN_CHUNK, dtype=q.dtype)
    rhs = jnp.concatenate([v * beta[..., None], kb * jnp.exp(gc)[..., None]], axis=-1)
    sol = lax.linalg.triangular_solve(eye + a_mat, rhs, left_side=True, lower=True,
                                      unit_diagonal=True)
    u_val, w_key = sol[..., :dv], sol[..., dv:]
    qk = jnp.einsum('bhnid,bhnjd->bhnij', q, k) * decay

    def to_scan(t):
        return jnp.moveaxis(t, 2, 0)

    def step(state, inp):
        q_c, k_c, u_c, w_c, qk_c, gc_c = inp
        v_new = u_c - jnp.einsum('bhcd,bhde->bhce', w_c, state)
        o = (jnp.einsum('bhcd,bhde->bhce', q_c * jnp.exp(gc_c)[..., None], state)
             + jnp.einsum('bhcs,bhse->bhce', qk_c, v_new))
        g_last = gc_c[..., -1:]
        state = (state * jnp.exp(g_last)[..., None]
                 + jnp.einsum('bhcd,bhce->bhde', k_c * jnp.exp(g_last - gc_c)[..., None], v_new))
        return state, o

    state0 = jnp.zeros((bsz, nh, dk, dv), q.dtype)
    _, o = lax.scan(step, state0, (to_scan(q), to_scan(k), to_scan(u_val), to_scan(w_key),
                                   to_scan(qk), to_scan(gc)))
    o = jnp.transpose(o, (1, 0, 3, 2, 4))
    return o.reshape(bsz, seq, nh, dv)

def stick_breaking_attention(q, k, v):
    bsz, seq, nh, hd = q.shape
    scale = hd ** -0.5
    outs = []
    for blk in range(seq // SB_BLOCK):
        t0 = blk * SB_BLOCK
        t1 = t0 + SB_BLOCK
        z = jnp.einsum('bthd,bshd->bhts', q[:, t0:t1], k[:, :t1]) * scale
        t_pos = t0 + jnp.arange(SB_BLOCK)
        s_pos = jnp.arange(t1)
        mask = s_pos[None, :] < t_pos[:, None]
        log_keep = jnp.where(mask, jax.nn.log_sigmoid(-z), 0.0)
        rest = lax.cumsum(log_keep, axis=3, reverse=True) - log_keep
        weights = jnp.where(mask, jnp.exp(jax.nn.log_sigmoid(z) + rest), 0.0)
        outs.append(jnp.einsum('bhts,bshd->bthd', weights, v[:, :t1]))
    return jnp.concatenate(outs, axis=1)

def memory_attend(q_m, z_m, q_norm_g, mem_k, mem_v):
    bsz, seq, _ = q_m.shape
    q = rms_norm(q_m.reshape(bsz, seq, MEM_HEADS, MEM_HEAD_DIM).astype(jnp.float32), q_norm_g)
    s = jnp.einsum('bshd,bmhd->bhsm', q, mem_k.astype(jnp.float32)) * (MEM_HEAD_DIM ** -0.5)
    p = jax.nn.softmax(s, axis=-1)
    o = jnp.einsum('bhsm,bmhd->bshd', p, mem_v.astype(jnp.float32)).reshape(bsz, seq, MEM_WIDTH)
    return (o * jax.nn.silu(z_m.astype(jnp.float32))).astype(q_m.dtype)

def even_layer(h, norm_g, w_in, conv_qkv, a_log, dt_bias, dn_norm_g, dw_w, dw_b,
               ln_g, ln_b, q_norm_m, w_out, mem_k, mem_v):
    bsz, seq, _ = h.shape
    f32 = jnp.float32
    p = rms_norm(h, norm_g) @ w_in
    cuts = [3 * DN_WIDTH, 4 * DN_WIDTH, 4 * DN_WIDTH + DN_HEADS, 4 * DN_WIDTH + 2 * DN_HEADS]
    cuts += [cuts[-1] + 2 * CV_WIDTH, cuts[-1] + 3 * CV_WIDTH, cuts[-1] + 3 * CV_WIDTH + MEM_WIDTH]
    qkv_a, z_a, b_a, a_a, glu_b, z_b, q_m, z_m = jnp.split(p, cuts, axis=-1)

    qkv = jax.nn.silu(causal_depthwise_conv(qkv_a, conv_qkv)).astype(f32)
    q, k, v = [t.reshape(bsz, seq, DN_HEADS, DN_HEAD_DIM) for t in jnp.split(qkv, 3, axis=-1)]
    q = l2_norm(q) * (DN_HEAD_DIM ** -0.5)
    k = l2_norm(k)
    beta = jax.nn.sigmoid(b_a.astype(f32))
    g = -jnp.exp(a_log.astype(f32)) * jax.nn.softplus(a_a.astype(f32) + dt_bias.astype(f32))
    o = gated_delta_rule(q, k, v, beta, g)
    gate_a = jax.nn.silu(z_a.astype(f32)).reshape(bsz, seq, DN_HEADS, DN_HEAD_DIM)
    o_a = (rms_norm(o, dn_norm_g) * gate_a).reshape(bsz, seq, DN_WIDTH).astype(h.dtype)

    glu = glu_b[..., :CV_WIDTH] * jax.nn.sigmoid(glu_b[..., CV_WIDTH:])
    c = causal_depthwise_conv(glu, dw_w) + dw_b.astype(glu.dtype)
    c = layer_norm(c, ln_g, ln_b)
    o_b = (jax.nn.silu(c.astype(f32)) * jax.nn.silu(z_b.astype(f32))).astype(h.dtype)

    o_m = memory_attend(q_m, z_m, q_norm_m, mem_k, mem_v)
    return jnp.concatenate([o_a, o_b, o_m], axis=-1) @ w_out

def odd_layer(h, norm_g, w_in, q_norm_c, k_norm_c, q_norm_m, w_out, mem_k, mem_v):
    bsz, seq, _ = h.shape
    f32 = jnp.float32
    p = rms_norm(h, norm_g) @ w_in
    cuts = [SB_WIDTH, 2 * SB_WIDTH, 3 * SB_WIDTH, 4 * SB_WIDTH, 4 * SB_WIDTH + MEM_WIDTH]
    q_c, k_c, v_c, z_c, q_m, z_m = jnp.split(p, cuts, axis=-1)
    heads = lambda t: t.reshape(bsz, seq, SB_HEADS, SB_HEAD_DIM).astype(f32)
    q = rms_norm(heads(q_c), q_norm_c)
    k = rms_norm(heads(k_c), k_norm_c)
    o = stick_breaking_attention(q, k, heads(v_c)).reshape(bsz, seq, SB_WIDTH)
    o_c = (o * jax.nn.silu(z_c.astype(f32))).astype(h.dtype)
    o_m = memory_attend(q_m, z_m, q_norm_m, mem_k, mem_v)
    return jnp.concatenate([o_c, o_m], axis=-1) @ w_out

def setup_inputs(seed: int = 0) -> dict:
    key = jax.random.key(seed)
    ks = jax.random.split(key, 24)
    f32 = jnp.float32
    nrm = lambda k, shape, scale: jax.random.normal(k, shape, f32) * scale
    gain = lambda k, shape: 1.0 + 0.05 * jax.random.normal(k, shape, f32)
    dt = jnp.exp(jax.random.uniform(ks[9], (N_EVEN, DN_HEADS), f32,
                                    math.log(1e-3), math.log(1e-1)))
    return {
        "x": nrm(ks[0], (BATCH, SEQ, D_MODEL), 1.0),
        "mem": nrm(ks[1], (BATCH, MEM_LEN, D_MODEL), 1.0),
        "mem_norm_g": gain(ks[2], (D_MODEL,)),
        "w_mem_kv": nrm(ks[3], (D_MODEL, 2 * MEM_WIDTH), D_MODEL ** -0.5),
        "mem_k_norm_g": gain(ks[4], (MEM_HEAD_DIM,)),
        "ev_norm_g": gain(ks[5], (N_EVEN, D_MODEL)),
        "ev_w_in": nrm(ks[6], (N_EVEN, D_MODEL, EVEN_IN), D_MODEL ** -0.5),
        "ev_conv_qkv": nrm(ks[7], (N_EVEN, DN_CONV, 3 * DN_WIDTH), DN_CONV ** -0.5),
        "ev_a_log": jnp.log(jax.random.uniform(ks[8], (N_EVEN, DN_HEADS), f32, 1.0, 16.0)),
        "ev_dt_bias": dt + jnp.log(-jnp.expm1(-dt)),
        "ev_dn_norm_g": gain(ks[10], (N_EVEN, DN_HEAD_DIM)),
        "ev_dw_w": nrm(ks[11], (N_EVEN, CV_KERNEL, CV_WIDTH), CV_KERNEL ** -0.5),
        "ev_dw_b": nrm(ks[12], (N_EVEN, CV_WIDTH), 0.02),
        "ev_ln_g": gain(ks[13], (N_EVEN, CV_WIDTH)),
        "ev_ln_b": nrm(ks[14], (N_EVEN, CV_WIDTH), 0.02),
        "ev_q_norm_m": gain(ks[15], (N_EVEN, MEM_HEAD_DIM)),
        "ev_w_out": nrm(ks[16], (N_EVEN, EVEN_MIX, D_MODEL), EVEN_MIX ** -0.5),
        "od_norm_g": gain(ks[17], (N_ODD, D_MODEL)),
        "od_w_in": nrm(ks[18], (N_ODD, D_MODEL, ODD_IN), D_MODEL ** -0.5),
        "od_q_norm_c": gain(ks[19], (N_ODD, SB_HEAD_DIM)),
        "od_k_norm_c": gain(ks[20], (N_ODD, SB_HEAD_DIM)),
        "od_q_norm_m": gain(ks[21], (N_ODD, MEM_HEAD_DIM)),
        "od_w_out": nrm(ks[22], (N_ODD, ODD_MIX, D_MODEL), ODD_MIX ** -0.5),
    }

def reference(x, mem, mem_norm_g, w_mem_kv, mem_k_norm_g,
              ev_norm_g, ev_w_in, ev_conv_qkv, ev_a_log, ev_dt_bias, ev_dn_norm_g,
              ev_dw_w, ev_dw_b, ev_ln_g, ev_ln_b, ev_q_norm_m, ev_w_out,
              od_norm_g, od_w_in, od_q_norm_c, od_k_norm_c, od_q_norm_m, od_w_out):
    bsz, mlen, _ = mem.shape
    mkv = (rms_norm(mem, mem_norm_g) @ w_mem_kv).reshape(bsz, mlen, 2, MEM_HEADS, MEM_HEAD_DIM)
    mem_k = rms_norm(mkv[:, :, 0], mem_k_norm_g)
    mem_v = mkv[:, :, 1]
    h = x
    for layer in range(DEPTH):
        j = layer // 2
        if layer % 2 == 0:
            h = h + even_layer(h, ev_norm_g[j], ev_w_in[j], ev_conv_qkv[j], ev_a_log[j],
                               ev_dt_bias[j], ev_dn_norm_g[j], ev_dw_w[j], ev_dw_b[j],
                               ev_ln_g[j], ev_ln_b[j], ev_q_norm_m[j], ev_w_out[j],
                               mem_k, mem_v)
        else:
            h = h + odd_layer(h, od_norm_g[j], od_w_in[j], od_q_norm_c[j], od_k_norm_c[j],
                              od_q_norm_m[j], od_w_out[j], mem_k, mem_v)
    return h


_drawn_inputs = setup_inputs


def setup_inputs(seed=0):
    import zlib

    import numpy as np

    out = dict(_drawn_inputs(seed))
    spreads = {}
    factors = {'mem_norm_g': 8.0,
     'mem_k_norm_g': 8.0,
     'ev_dn_norm_g': 2.912,
     'ev_dw_b': 6.547,
     'ev_ln_g': 4.456,
     'ev_ln_b': 8.0,
     'ev_q_norm_m': 8.0,
     'od_q_norm_c': 25.932,
     'od_k_norm_c': 24.667,
     'od_q_norm_m': 8.0}
    for name, (base, spread) in spreads.items():
        noise = np.random.default_rng([zlib.crc32(name.encode()), seed]).standard_normal(out[name].shape)
        drawn = base * np.exp(spread * noise) if base else spread * noise
        out[name] = __import__('jax').numpy.asarray(drawn.astype(out[name].dtype))
    for name, factor in factors.items():
        out[name] = (out[name] * factor).astype(out[name].dtype)
    return out
```

```python
import math

import concourse.bass as bass
from concourse import mybir
from contextlib import ExitStack

F32 = mybir.dt.float32
F32R = mybir.dt.float32r
ALU = mybir.AluOpType
ACT = mybir.ActivationFunctionType
AX = mybir.AxisListType

D = 2048
S = 256
T = 2
KT = D // 128
DNW, CVW, MW, SBW = 1024, 1024, 1024, 2048
H_DN, H_MEM, H_SB = 8, 4, 16
EPS = 1e-6
NEG = -1.0e30
CONV, TAPS = 4, 31

Q0, K0, V0, ZA0, BA0 = 0, DNW, 2 * DNW, 3 * DNW, 4 * DNW
GA0 = BA0 + 2 * H_DN
GB0 = GA0 + CVW
ZB0 = GB0 + CVW
QM0 = ZB0 + CVW
ZM0 = QM0 + MW
JOBS = []


def _jobs():
    for g in range(2):
        for base in (Q0, K0, V0, ZA0):
            JOBS.append(("ev_in", 0, base + 512 * g, KT, 0))
    for c0 in (GA0, GB0, GA0 + 512, GB0 + 512, ZB0, ZB0 + 512, QM0, QM0 + 512, ZM0, ZM0 + 512):
        JOBS.append(("ev_in", 0, c0, KT, 0))
    for b in range(4):
        JOBS.append(("mem", 0, 512 * b, KT, 16))
    for part in range(3):
        for b in range(4):
            JOBS.append(("ev_out", 1024 * part, 512 * b, 8, 32 + 8 * part))
    for g in range(4):
        for base in (0, SBW, 2 * SBW, 3 * SBW):
            JOBS.append(("od_in", 0, base + 512 * g, KT, 56))
    for b in range(4):
        JOBS.append(("od_in", 0, 4 * SBW + 512 * b, KT, 56))
    for part in range(3):
        for b in range(4):
            JOBS.append(("od_out", 1024 * part, 512 * b, 8, 72 + 8 * part))


_jobs()
J_MEM, J_EVOUT, J_ODIN, J_ODOUT = 18, 22, 34, 54
CH0 = []
_n = 0
for _j in JOBS:
    CH0.append(_n)
    _n += _j[3] // 2
CH0.append(_n)
NCH = _n
JOB_OF = [j for j in range(len(JOBS)) for _ in range(JOBS[j][3] // 2)]

SLOT = ([k for k in range(16)] + [k for k in range(16)] + list(range(8)) + list(range(8, 16)) + list(range(8))
        + [(k + 8) % 16 for k in range(16)] + list(range(8, 16)) + list(range(8)) + list(range(8, 16)))
NFILL = len(SLOT)


def fills_of(j):
    return range(JOBS[j][4], JOBS[j][4] + JOBS[j][3])


LAST_CHUNK = {}
for _j in range(len(JOBS)):
    for _i, _f in enumerate(fills_of(_j)):
        LAST_CHUNK[_f] = CH0[_j] + _i // 2 + 1


def chunks_before_fill(n):
    before = [m for m in range(n) if SLOT[m] == SLOT[n]]
    return LAST_CHUNK[before[-1]] if before else 0


VEC = [("mem_norm_g", 16), ("ev_norm_g", 16), ("od_norm_g", 16), ("mem_k_norm_g", 2), ("ev_q_norm_m", 2),
       ("od_q_norm_m", 2), ("ev_dn_norm_g", 1), ("od_q_norm_c", 1), ("od_k_norm_c", 1), ("ev_dw_b", 8),
       ("ev_ln_g", 8), ("ev_ln_b", 8)]
VCOL = {}
_n = 0
for _name, _c in VEC:
    VCOL[_name] = _n
    _n += _c
NVEC = _n
V_CONV = 128
V_DW = 256
NV = 512

RAWS, RING, AHEAD = 4, 8, 6


PSLOT = {j: j % 4 for j in range(18)}
PSLOT.update({18: 0, 19: 1})
PSLOT.update({j: (j - J_ODIN) % 4 for j in range(J_ODIN, J_ODOUT)})


def make_plan(last_job):
    seq = []

    def add(steps, at=0, by=10 ** 9, rate=2.0):
        for s in steps:
            seq.append((at, by, rate, s))

    def after(j):
        return CH0[j + 1] + 2

    def deltanet(g):
        heads = range(4 * g, 4 * g + 4)
        s = []
        for h in heads:
            s += [("dnT", h), ("dnC", h), ("dnB", h)]
        s += [("za", g), ("dnV", g)] + [("dnG", h) for h in heads]
        a, b = 2 * g, 2 * g + 1
        s += [("d4x", 7 * a)]
        for l in range(7):
            s += [("d4y", 7 * a + l), ("d4x", 7 * b + l)]
            s += [("d4y", 7 * b + l)] + ([("d4x", 7 * a + l + 1)] if l < 6 else [])
        tail = []
        for h in heads:
            tail += [("d5a", h), ("d5b", h), ("d5c", h), ("d5d", h), ("d5e", h)]
        return s, tail + [("d6", g)] + [("d7", h) for h in heads]

    add([("xt", n) for n in range(16)] + [("rstd", 0), ("ba", 0)], rate=1000)
    s, tail = deltanet(0)
    add(s + tail, after(3), rate=2.7)
    s, tail = deltanet(1)
    add(s[:12], after(6), CH0[9] + 1)
    add(s[12:], after(7))
    add([("glu", 0)] + [("gT", ct) for ct in range(4)], after(9))
    add(tail, after(7))
    add([("mload", 0)])
    add([("glu", 1)] + [("gT", ct) for ct in range(4, 8)], after(11))
    add([("zT", n) for n in range(8)], after(13))
    for pr in range(4):
        add([("conv", 8 * pr + q) for q in range(8)], rate=1.5)
    add([("zT", n) for n in range(8, 12)], after(16), CH0[18], 1000)
    add([("zT", n) for n in range(12, 16)], after(17), CH0[18] + 4, 1000)
    add([("lnm", 0)] + [("lnv", ct) for ct in range(8)] + [("lnr", 0)] + [("lno", ct) for ct in range(8)])
    add([("mqs", i) for i in range(2)] + [("mqT", dt) for dt in range(8)], after(15))
    add([("mks", 0)] + [("mkT", dt) for dt in range(4)], after(18))
    add([("mks", 1)] + [("mkT", dt) for dt in range(4, 8)], after(19))
    att = []
    for n in range(4):
        att += [("mas", n), ("mat", n), ("mao", 2 * n), ("mao", 2 * n + 1)]
    add(att, after(21), rate=1.0)
    add([("mf", n) for n in range(48, 56)], CH0[26], CH0[30])
    for g in range(4):
        add([("sbn", g)] + [("zT", 16 + 4 * g + q) for q in range(4)], after(J_ODIN + 4 * g + 3))
        add([("tab", g)], 0, rate=1000)
        add([("sbT", h) for h in range(4 * g, 4 * g + 4)])
        for h in range(4 * g, 4 * g + 4):
            add([("sbz", h), ("sbc", h), ("sbo", h)], rate=1.5)
    add([("zT", n) for n in range(32, 40)], after(J_ODOUT - 1))
    add([("mf", n) for n in range(80, 88)], CH0[J_ODOUT] + 1, CH0[J_ODOUT + 4])
    add([("mqs", 2), ("mqs", 3)] + [("mqT", dt) for dt in range(8, 16)], after(J_ODOUT - 1))
    att = []
    for n in range(4, 8):
        att += [("mas", n), ("mat", n), ("mao", 2 * n), ("mao", 2 * n + 1)]
    add(att, after(J_ODOUT - 1))
    add([("mf", n) for n in range(88, 96)], CH0[J_ODOUT + 4], CH0[J_ODOUT + 8])

    fixed = {}
    for j in range(len(JOBS)):
        fixed.setdefault(CH0[j + 1] + 1, []).append(("evac", j))
    for i in range(8):
        fixed.setdefault(CH0[17] + i + 2, []).extend([("xt", 16 + 2 * i), ("xt", 17 + 2 * i)])
    fixed.setdefault(CH0[18] + 1, []).append(("rstd", 1))
    for k in range(8):
        fixed.setdefault(CH0[21] + k // 2 + 2, []).append(("mf", 32 + k))
        fixed.setdefault(CH0[22] + k // 2 + 1, []).append(("mf", 40 + k))
        fixed.setdefault(CH0[53] + k // 2 + 2, []).append(("mf", 72 + k))
    fixed.setdefault(CH0[22] - 4, []).append(("xload", 0))
    for b in range(4):
        at = CH0[31 + b] + (1 if b < 3 else 0)
        fixed.setdefault(at, []).extend([("xt", 56 + 4 * b + q) for q in range(4)])
    fixed[CH0[34] + 1].remove(("evac", 33))
    fixed[CH0[34]].insert(0, ("evac", 33))
    fixed[CH0[34]].append(("rstd", 2))

    plan, at, due = [], 0, 0.0
    for c in range(NCH + 3):
        plan += fixed.get(c, [])
        while at < len(seq) and (seq[at][1] <= c or any(q[1] <= c for q in seq[at:]) or
                                 (seq[at][0] <= c and due <= c + 1)):
            due = max(due, c) + 1.0 / seq[at][2]
            plan.append(seq[at][3])
            at += 1
        if c < NCH:
            plan.append(("chunk", c))
    plan += [q[3] for q in seq[at:]]
    if last_job < len(JOBS):
        stop = plan.index(("evac", last_job - 1)) + 1
        plan = [p for p in plan[:stop] if not (p[0] == "chunk" and p[1] >= CH0[last_job])
                and not (p[0] == "xt" and p[1] >= 56)]
    return plan


def prog(nc, x, mem, vecs, w, a_log, dt_bias, out, last_job=len(JOBS)):
    plan = make_plan(last_job)
    jobs = JOBS[:last_job]
    nch = CH0[last_job]
    ctx = ExitStack()
    with ctx:
        def sb(name, shape, dt=F32):
            return ctx.enter_context(nc.sbuf_tensor(name, shape, dt))

        def sem(name):
            return ctx.enter_context(nc.semaphore(name))

        raw = sb("raw", [128, RAWS, 2, 512])
        whi = sb("whi", [128, RING, 2, 512], F32R)
        wlo = sb("wlo", [128, RING, 2, 512], F32R)
        xhi = sb("xhi", [128, 16, S], F32R)
        xlo = sb("xlo", [128, 16, S], F32R)
        hid = sb("hid", [128, T, D])
        proj = sb("proj", [128, 4, T, 512])
        reg = sb("reg", [128, 4096])
        cvr = sb("cvr", [128, 10, S])
        mix = sb("mix", [128, 24, S])
        scr = sb("scr", [128, 1024])
        ident = sb("ident", [128, 128])
        ones = sb("ones", [128, 128])
        negones = sb("negones", [128, 128])
        upto = sb("upto", [128, 128])
        negfrom = sb("negfrom", [128, 128])
        after01 = sb("after01", [128, 128])
        shut = sb("shut", [128, 2, 128])
        vt = sb("vt", [128, NV])
        qgain = sb("qgain", [128, 1])
        rows = sb("rows", [24, 2, 128])
        ssq = sb("ssq", [128, 3, T])
        rstd = sb("rstd", [128, 3, T])
        mhalf = sb("mhalf", [128, 16])
        ba = sb("ba", [128, T, 2 * H_DN])
        alog = sb("alog", [128, H_DN])
        dtb = sb("dtb", [128, H_DN])
        beta = sb("beta", [128, T, H_DN])
        halfb = sb("halfb", [128, T, H_DN])
        lnb = sb("lnb", [128, T, H_DN])
        gu = sb("gu", [128, T, H_DN])
        ge = sb("ge", [128, T, H_DN])
        gl_in = sb("gl_in", [128, T, H_DN])
        gcl = sb("gcl", [128, 2, T, H_DN])
        nrm = sb("nrm", [128, H_DN, 4])
        hln = sb("hln", [128, 2, 4, 4])
        cc = sb("cc", [128, 2, 4, T])
        ei = sb("ei", [128, 2, 4, 8])
        ex = sb("ex", [128, 2, 4, 8])
        nks = sb("nks", [128, 2, 8])
        oss = sb("oss", [128, 2, 8])
        oms = sb("oms", [128, 2, 8])
        ofac = sb("ofac", [128, 2, 8])
        qss = sb("qss", [128, 6, 4])
        qrs = sb("qrs", [128, 6, 4])
        smx = sb("smx", [128, 8, T])
        snb = sb("snb", [128, 8, T])
        ssm = sb("ssm", [128, 8, T])
        srs = sb("srs", [128, 8, T])
        bss = sb("bss", [128, 4, 16])
        brs = sb("brs", [128, 4, 16])

        flat = hid[:, :, :].rearrange("p t d -> p (t d)")
        pflat = proj[:, :, :, :].rearrange("p a t n -> p (a t n)")
        cflat = cvr[:, :, :].rearrange("p a s -> p (a s)")
        mflat = mix[:, :, :].rearrange("p a s -> p (a s)")
        ykqv = reg[:, 0:3072].rearrange("p (h c s) -> p h c s", h=4, c=3)
        ofx = reg[:, 3072:4096].rearrange("p (a m n) -> p a m n", a=2, m=4)
        tok = flat[:, 0:1536].rearrange("p (h c n) -> p h c n", h=4, c=3)
        aq = flat[:, 1536:3584].rearrange("p (m c n) -> p m c n", m=8, c=2)
        dw = flat[:, 3584:4096].rearrange("p (c n) -> p c n", c=4)
        tinv = cflat[:, 0:1024].rearrange("p (a m n) -> p a m n", a=2, m=4)
        tinvt = cflat[:, 1024:2048].rearrange("p (a m n) -> p a m n", a=2, m=4)
        za = mflat[:, 16 * S:24 * S].rearrange("p (t n) -> p t n", t=T)
        level = mflat[:, 8 * S:8 * S + 896].rearrange("p (l n) -> p l n", l=7)
        memx = reg[:, :].rearrange("p (t d) -> p t d", t=T)
        kmt = reg[:, 0:2048].rearrange("p (a s) -> p a s", a=8)
        vm = reg[:, 2048:4096].rearrange("p (t n) -> p t n", t=T)
        qmt = cflat[:, 0:2048].rearrange("p (a s) -> p a s", a=8)
        prob = scr[:, 0:512].rearrange("p (t m) -> p t m", t=T)
        probt = scr[:, 512:1024].rearrange("p (m s) -> p m s", m=2)
        qk = cflat[:, 0:2048].rearrange("p (a c s) -> p a c s", a=4, c=2)
        wts = cflat[:, 2048:2432]
        absz = scr[:, 0:384]
        spz = scr[:, 512:896]
        vrow = pflat[:, 0:512].rearrange("p (a n) -> p a n", a=4)
        wba = reg[:, 0:256].rearrange("p (k n) -> p k n", k=16)
        bah = whi[:, RING - 1, 0, 0:256].rearrange("p (k n) -> p k n", k=16)
        bal = wlo[:, RING - 1, 0, 0:256].rearrange("p (k n) -> p k n", k=16)

        def psum(name):
            return ctx.enter_context(nc.psum_tensor(name, [128, 512], F32))

        pj = [[psum(f"job{a}{t}") for t in range(T)] for a in range(2)]
        M = [psum(f"mixer{i}") for i in range(4)]

        s_vrow = sem("vector_rows_loaded")
        s_small = sem("small_inputs_loaded")
        s_xin = sem("x_loaded")
        s_min = sem("mem_loaded")
        s_xre = sem("x_loaded_again")
        s_raw = [sem(f"raw_chunk_loaded{i}") for i in range(RAWS)]
        s_out = sem("output_stored")
        s_hi = sem("chunk_high_parts")
        s_lo = sem("chunk_remainders")
        s_pe = sem("chunks_multiplied")
        s_evA = sem("job_results_copied")
        s_evD = sem("job_results_added")
        s_xp = sem("rows_transposed")
        s_xh = sem("fill_high_parts")
        s_xl = sem("fill_remainders")
        s_const = sem("constants_made")
        s_vp = sem("vectors_transposed")
        s_vt = sem("vectors_copied")
        s_ss = sem("row_squares_summed")
        s_ms = sem("row_mean_squares")
        s_rstd = sem("row_rstd")
        s_wbh = sem("ba_weights_high")
        s_wbl = sem("ba_weights_low")
        s_bap = sem("ba_multiplied")
        s_ba = sem("ba_copied")
        s_baA = sem("ba_scalar_steps")
        s_baD = sem("ba_vector_steps")
        s_gcp = sem("decays_summed")
        s_gc = sem("decays_copied")
        s_zat = sem("za_tanh")
        s_za = sem("za_gates")
        s_dnT = sem("dn_qkv_transposed")
        s_cv4 = sem("dn_conv_ops")
        s_th = sem("dn_tanh")
        s_silu = sem("dn_silu")
        s_sq = sem("dn_squares")
        s_back = sem("dn_kv_transposed_back")
        s_tok = sem("dn_kv_by_token")
        s_np = sem("dn_norms_summed")
        s_nrm = sem("dn_norms_copied")
        s_lnq = sem("dn_log_norms")
        s_ei = sem("dn_exponents")
        s_ex = sem("dn_factors")
        s_rp = sem("dn_rows_transposed")
        s_rows = sem("dn_rows_copied")
        s_tks = sem("dn_kv_scaled")
        s_gp = sem("dn_products")
        s_eq = sem("dn_decays")
        s_aq = sem("dn_matrices")
        s_of = [sem(f"inv_masked{i}") for i in range(2)]
        s_x1p = [sem(f"inv_first_product{i}") for i in range(2)]
        s_x1 = [sem(f"inv_first_copied{i}") for i in range(2)]
        s_x2p = [sem(f"inv_second_products{i}") for i in range(2)]
        s_t = [sem(f"inv_updated{i}") for i in range(2)]
        s_5ap = sem("dn_v0_product")
        s_5a = sem("dn_v0_copied")
        s_5bp = sem("dn_state_products")
        s_5b = sem("dn_state_copied")
        s_5cp = sem("dn_state_read")
        s_5cA = sem("dn_q_state_copied")
        s_5c = sem("dn_second_rhs")
        s_5dp = sem("dn_v1_product")
        s_5d = sem("dn_v1_copied")
        s_5ep = sem("dn_o1_product")
        s_5e = sem("dn_o1_added")
        s_oss = sem("dn_out_squares")
        s_oms = sem("dn_out_mean_squares")
        s_opw = sem("dn_out_rstd")
        s_of6 = sem("dn_out_factors")
        s_ow = sem("dn_out_gated")
        s_owp = sem("dn_out_transposed")
        s_mixa = sem("dn_out_stored")
        s_glt = sem("glu_tanh")
        s_glu = sem("glu_products")
        s_gtp = sem("glu_transposed")
        s_gt = sem("glu_stored")
        s_cv = sem("conv_taps")
        s_mup = sem("ln_sum")
        s_mu = sem("ln_mean")
        s_xc = sem("ln_centred")
        s_lsq = sem("ln_squares")
        s_lvp = sem("ln_square_sums")
        s_var = sem("ln_variance")
        s_std = sem("ln_std")
        s_xn = sem("ln_normalised")
        s_ly = sem("ln_affine")
        s_lt = sem("ln_tanh")
        s_mixb = sem("conv_out_stored")
        s_zp = sem("gates_transposed")
        s_zc = sem("gates_tanh")
        s_z = sem("gates_stored")
        s_mqs = sem("mq_squares")
        s_mqm = sem("mq_mean_squares")
        s_mqr = sem("mq_rstd")
        s_mqk = sem("mq_scales")
        s_mks = sem("mk_scaled")
        s_mqp = sem("mq_transposed")
        s_mqT = sem("mq_stored")
        s_mkp = sem("mk_transposed")
        s_mkT = sem("mk_stored")
        s_scp = sem("mem_scores")
        s_nb = sem("mem_score_maxima")
        s_exp = sem("mem_exps")
        s_pr = sem("mem_probs")
        s_ptp = sem("mem_probs_transposed")
        s_pt = sem("mem_probs_stored")
        s_maop = sem("mem_out_products")
        s_mao = sem("mem_out_stored")
        s_sbs = sem("sb_squares")
        s_sbr = sem("sb_square_sums")
        s_sbm = sem("sb_mean_squares")
        s_sbw = sem("sb_rstd")
        s_sbn = sem("sb_normalised")
        s_sbtp = sem("sb_qk_transposed")
        s_sbT = sem("sb_qk_stored")
        s_sbzp = sem("sb_scores")
        s_sbA = sem("sb_log_terms")
        s_sbsp = sem("sb_softplus")
        s_sbmk = sem("sb_softplus_masked")
        s_sbcp = sem("sb_sums")
        s_sbW = sem("sb_weights")
        s_sbop = sem("sb_out_products")
        s_sbo = sem("sb_out_stored")
        s_actq = sem("scalar_own_steps")
        s_dveq = sem("vector_own_steps")
        s_poolq = sem("gpsimd_own_steps")

        def evac_done(j):
            if j < J_EVOUT:
                return s_evA, j + 1
            if j < J_ODIN:
                return s_evD, j - J_EVOUT + 1
            if j < J_ODOUT:
                return s_evA, j - J_ODIN + J_EVOUT + 1
            return s_evD, j - J_ODOUT + (J_ODIN - J_EVOUT) + 1

        def banks(step, i):
            if step == "xt":
                return [i % 4] if i < 16 else [2 + i % 2]
            if step in ("mqT", "mkT"):
                return [i % 2]
            if step == "d4y":
                return [] if i % 7 == 0 else ([1, 2] if i % 7 < 6 else [2])
            if step == "lnv":
                return [1] if i == 0 else []
            return {"vec": [0], "ba": [0, 1], "dnT": [0, 1], "dnB": [2], "dnV": [1], "dnG": [0, 1], "d4x": [0],
                    "d5a": [0], "d5b": [1], "d5c": [2], "d5d": [0], "d5e": [1], "d7": [2], "gT": [3], "zT": [3],
                    "lnm": [0], "mas": [0], "mat": [1], "mao": [2], "sbT": [0], "sbz": [1], "sbo": [2]}.get(step, [])

        def inv_count(i):
            return 7 * (i // 14) + i % 7 + 1

        def read(step, i):
            par = (i // 7) % 2
            return {"vec": (s_vt, 1), "xt": (s_xl, i + 1), "ba": (s_gc, 1), "dnT": (s_nrm, i + 1),
                    "dnB": (s_tok, i + 1), "dnV": (s_rows, i + 1), "dnG": (s_aq, i + 1),
                    "d4x": (s_t[par], inv_count(i)) if i % 7 == 0 else (s_x1[par], 6 * (i // 14) + i % 7),
                    "d4y": (s_t[par], inv_count(i)), "d5a": (s_5a, i + 1), "d5b": (s_5b, i + 1),
                    "d5c": (s_5c, i + 1), "d5d": (s_5d, i + 1), "d5e": (s_5e, i + 1), "d7": (s_mixa, i + 1),
                    "gT": (s_gt, i + 1), "zT": (s_z, i + 1), "lnm": (s_mu, 1), "lnv": (s_var, 1),
                    "mqT": (s_mqT, i + 1), "mkT": (s_mkT, i + 1), "mas": (s_exp, i + 1), "mat": (s_pt, i + 1),
                    "mao": (s_mao, i + 1), "sbT": (s_sbT, i + 1), "sbz": (s_sbW, i + 1),
                    "sbo": (s_sbo, i + 1)}[step]

        last_user, bank_free = {}, {}
        for st, i in [("vec", 0)] + plan:
            bank_free[st, i] = [read(*last_user[b]) for b in banks(st, i) if b in last_user]
            for b in banks(st, i):
                last_user[b] = (st, i)

        def slot_jobs(j):
            before = [q for q in PSLOT if q < j and PSLOT[q] == PSLOT[j]]
            if not before:
                return [(s_ss, 1), (s_vp, 1)]
            q = max(before)
            if q < 8:
                return [(s_za, q // 4 + 1)] if q % 4 == 3 else [(s_dnT, 4 * (q // 4) + 4)]
            if q < 12:
                return [(s_glu, (q - 8) // 2 + 1)] if q % 2 else [(s_gtp, 4 * ((q - 8) // 2) + 4)]
            if q < 14:
                return [(s_zp, 4 * (q - 12) + 4)]
            if q < 16:
                return [(s_mqp, 4 * (q - 14) + 4)]
            if q < 18:
                return [(s_zp, 8 + 4 * (q - 16) + 4)]
            if q < 20:
                return [(s_mkp, 4 * (q - 18) + 4)]
            g, c = divmod(q - J_ODIN, 4)
            if q >= J_ODIN + 16:
                return []
            return [[(s_sbtp, 4 * g + 4)], [(s_sbtp, 4 * g + 4)], [(s_sbop, 4 * g + 4)], [(s_zp, 16 + 4 * g + 4)]][c]

        def zsource(n):
            if n < 8:
                return 12 + n // 4, n // 4, n % 4, 8 + n
            if n < 16:
                return 16 + (n - 8) // 4, (n - 8) // 4, n % 4, 16 + n - 8
            if n < 32:
                return J_ODIN + 4 * ((n - 16) // 4) + 3, 3, n % 4, n - 16
            return 52 + (n - 32) // 4, 2 + (n - 32) // 4, n % 4, 16 + n - 32

        def gain(name, c):
            return vt[:, VCOL[name] + c:VCOL[name] + c + 1]

        def xt_gain(n):
            return gain("ev_norm_g", n) if n < 16 else gain("mem_norm_g", n - 16) if n < 32 else gain("od_norm_g", n - 56)

        def source_ready(src):
            return [(s_xin, 16), (s_min, 16), (s_evD, J_ODIN - J_EVOUT)][src]

        def mix_ready(n):
            kt, odd = (n - 32, 0) if n < 56 else (n - 72, 1)
            if odd and kt < 16:
                return s_sbo, kt + 1
            if kt < 8:
                return s_mixa, kt + 1
            if kt < 16:
                return s_mixb, kt - 7
            return s_mao, 8 * odd + kt - 15

        mm = nc.tensor.matmul
        act = nc.scalar.activation
        vec = nc.vector
        MQJOB = [14, 15, 50, 51, 18, 19]
        MQSLOT = [2, 3, 0, 1, 0, 1]
        order = {0: 1, 1: 2, 4: 3, 5: 4, 2: 5, 3: 6}

        block = ctx.enter_context(nc.Block())

        @block.sync
        def _(sp):
            sp.dma_start(hid[:, :, :], x.rearrange("(t p) d -> p t d", p=128)).then_inc(s_xin, 16)
            for a, (dst, src) in enumerate(vecs(vrow)):
                sp.dma_start(dst, src).then_inc(s_vrow, 16)
            sp.dma_start(wba, w["ev_in"][:, BA0:BA0 + 16].rearrange("(k p) n -> p k n", p=128),
                         allow_slow_non_contiguous=True).then_inc(s_small, 16)
            sp.dma_start(alog[:, :], a_log.partition_broadcast(128)).then_inc(s_small, 16)
            sp.dma_start(dtb[:, :], dt_bias.partition_broadcast(128)).then_inc(s_small, 16)
            for c in range(nch):
                j = JOB_OF[c]
                name, r0, c0, _, _ = JOBS[j]
                r = r0 + 256 * (c - CH0[j])
                if c >= RAWS:
                    sp.wait_ge(s_lo, c - RAWS + 1)
                sp.dma_start(raw[:, c % RAWS, :, :], w[name][r:r + 256, c0:c0 + 512].rearrange("(k p) n -> p k n", p=128)
                             ).then_inc(s_raw[c % RAWS], 16)
            stores = 0
            for b in range(4):
                j = last_job - 4 + b
                sp.wait_ge(*evac_done(j))
                sp.dma_start(out[:, 512 * b:512 * b + 512].rearrange("(t p) d -> p t d", p=128),
                             hid[:, :, 512 * b:512 * b + 512]).then_inc(s_out, 16)
                stores += 16
            sp.wait_ge(s_out, stores)

        @block.gpsimd
        def _(gp):
            own = [0]

            def link(ins):
                own[0] += 1
                ins.then_inc(s_poolq, 1)
                gp.wait_ge(s_poolq, own[0])

            def keep(t, pattern, base, mult, op, fill):
                link(nc.gpsimd.affine_select(out=t, in_=t, compare_op=op, fill=fill, base=base,
                                             pattern=pattern, channel_multiplier=mult))

            for t, v in ((ident, 0.0), (ones, 1.0), (negones, -1.0), (upto, 1.0), (negfrom, -1.0), (after01, 1.0),
                         (mhalf, -0.5)):
                link(nc.gpsimd.memset(t[:, :], v))
            link(nc.gpsimd.memset(shut[:, :, :], 0.0))
            link(nc.gpsimd.memset(level, 0.0))
            keep(ident[:, :], [[-1, 128]], 0, 1, ALU.not_equal, 1.0)
            keep(upto[:, :], [[1, 128]], 0, -1, ALU.is_ge, 0.0)
            keep(negfrom[:, :], [[-1, 128]], 0, 1, ALU.is_ge, 0.0)
            keep(after01[:, :], [[1, 128]], 0, -1, ALU.is_gt, 0.0)
            keep(shut[:, 0, :], [[1, 128]], 0, -1, ALU.is_gt, NEG)
            keep(shut[:, 1, :], [[1, 128]], 0, -1, ALU.is_ge, NEG)
            for l in range(7):
                h = 1 << l
                nb = 64 // h
                v = level[:, l, :].rearrange("p (b c r) -> p b c r", b=nb, c=2)[:, :, 1, :]
                link(nc.gpsimd.memset(v, 1.0))
                keep(v, [[-2 * h, nb], [0, h]], 0, 1, ALU.is_ge, 0.0)
                keep(v, [[2 * h, nb], [0, h]], h - 1, -1, ALU.is_ge, 0.0)
            nc.gpsimd.memset(qgain[:, :], 0.0).then_inc(s_const, 1)

            def power(out_, in_, n, done):
                nc.gpsimd.tensor_tensor(out_, in_, mhalf[:, 0:n], ALU.pow).then_inc(done, 1)

            def do_rstd(src):
                gp.wait_ge(s_ms, src + 1)
                power(rstd[:, src, :], ssq[:, src, :], T, s_rstd)

            def do_dnB(h):
                gp.wait_ge(s_silu, 2 * h + 2)
                if h:
                    gp.wait_ge(s_np, h)
                k = ykqv[:, h % 4, 0:2, :]
                nc.gpsimd.tensor_tensor(scr[:, 0:512].rearrange("p (c s) -> p c s", c=2), k, k, ALU.mult).then_inc(s_sq, 1)

            def do_dnG(h):
                g, hl = h // 4, h % 4
                gp.wait_ge(s_tok, h + 1)
                gp.wait_ge(s_ex, g + 1)
                gp.wait_ge(s_baD, 2)
                for c, f in ((0, ex[:, g, 1, 2 * hl:2 * hl + 1]), (1, halfb[:, 0, h:h + 1]), (2, halfb[:, 1, h:h + 1])):
                    ins = nc.gpsimd.tensor_scalar(tok[:, hl, c, :], tok[:, hl, c, :], f, 1.0, ALU.mult, ALU.mult)
                ins.then_inc(s_tks, 1)

            def do_d4x(i):
                pr, l = divmod(i, 7)
                g, par = divmod(pr, 2)
                if l == 0:
                    gp.wait_ge(s_aq, 4 * g + 2 * par + 2)
                    if g:
                        gp.wait_ge(s_5dp, 4 * (g - 1) + 2 * par + 2)
                else:
                    gp.wait_ge(s_t[par], 7 * g + l)
                nc.gpsimd.tensor_tensor(ofx[:, par, :, :], aq[:, 4 * par:4 * par + 4, 0, :],
                                        level[:, l, :].unsqueeze(1).broadcast_to([128, 4, 128]), ALU.mult
                                        ).then_inc(s_of[par], 1)

            def do_d6(g):
                gp.wait_ge(s_oms, g + 1)
                power(oms[:, g, :], oms[:, g, :], 8, s_opw)

            def mq_power(i, n):
                gp.wait_ge(s_mqm, n)
                power(qss[:, i, :], qss[:, i, :], 4, s_mqr)

            def do_sbn(g):
                gp.wait_ge(s_sbm, g + 1)
                power(brs[:, g, :], bss[:, g, :], 16, s_sbw)
                gp.wait_ge(s_sbw, g + 1)
                for c in range(2):
                    v = pflat[:, 1024 * c:1024 * c + 1024].rearrange("p (a n) -> p a n", n=128)
                    nc.gpsimd.tensor_tensor(v, v, brs[:, g, 8 * c:8 * c + 8].unsqueeze(2).broadcast_to([128, 8, 128]),
                                            ALU.mult).then_inc(s_sbn, 1)

            def do_sbz(h):
                gp.wait_ge(s_sbsp, h + 1)
                v = spz.rearrange("p (a n) -> p a n", a=3)[:, 0:3:2, :]
                nc.gpsimd.tensor_tensor(v, v, after01[:, :].unsqueeze(1).broadcast_to([128, 2, 128]), ALU.mult
                                        ).then_inc(s_sbmk, 1)

            steps = {"rstd": do_rstd, "dnB": do_dnB, "dnG": do_dnG, "d4x": do_d4x, "d6": do_d6, "sbn": do_sbn,
                     "sbz": do_sbz, "mqs": lambda i: mq_power(i, order[i]), "mks": lambda i: mq_power(4 + i, order[4 + i])}
            for st, i in plan:
                if st in steps:
                    steps[st](i)

        @block.scalar
        def _(sc):
            own = [0]

            def link(ins):
                own[0] += 1
                ins.then_inc(s_actq, 1)
                sc.wait_ge(s_actq, own[0])

            def split(c):
                sc.wait_ge(s_raw[c % RAWS], 16 * (c // RAWS + 1))
                if c >= RING:
                    sc.wait_ge(s_pe, c - RING + 1)
                if c == RING - 1:
                    sc.wait_ge(s_bap, 1)
                act(whi[:, c % RING, :, :], raw[:, c % RAWS, :, :], ACT.Copy).then_inc(s_hi, 1)

            def do_chunk(c):
                if c + AHEAD < nch:
                    split(c + AHEAD)

            def do_evac(j):
                if not (j < J_EVOUT or J_ODIN <= j < J_ODOUT):
                    return
                src = 0 if j < J_MEM else 1 if j < J_EVOUT else 2
                sc.wait_ge(s_rstd, src + 1)
                sc.wait_ge(s_pe, CH0[j + 1])
                for t in range(T):
                    if j in PSLOT:
                        if t == 0:
                            for q in slot_jobs(j):
                                sc.wait_ge(*q)
                        dst = proj[:, PSLOT[j], t, :]
                    else:
                        dst = vm[:, t, 512 * (j - 20):512 * (j - 20) + 512]
                    ins = act(dst, pj[j % 2][t][:, :], ACT.Copy, scale=rstd[:, src, t:t + 1])
                ins.then_inc(evac_done(j)[0], 1)

            def fill_wait(n):
                if chunks_before_fill(n):
                    sc.wait_ge(s_pe, chunks_before_fill(n))

            def do_xt(n):
                sc.wait_ge(s_xp, (n if n < 32 else n - 24) + 1)
                fill_wait(n)
                act(xhi[:, SLOT[n], :], M[banks("xt", n)[0]][:, 0:S], ACT.Copy, scale=xt_gain(n)).then_inc(s_xh, 1)

            def do_mf(n):
                sc.wait_ge(*mix_ready(n))
                fill_wait(n)
                act(xhi[:, SLOT[n], :], mix[:, n - 32 if n < 56 else n - 72, :], ACT.Copy).then_inc(s_xh, 1)

            def do_rstd(src):
                sc.wait_ge(*source_ready(src))
                for t in range(T):
                    if src == 1:
                        sc.wait_ge(s_mixa, 8)
                        ins = act(flat[:, 2048 * t:2048 * t + 2048], memx[:, t, :], ACT.Square, accum_out=ssq[:, 1, t:t + 1])
                    else:
                        ins = act(pflat[:, 2048 * t:2048 * t + 2048], hid[:, t, :], ACT.Square, accum_out=ssq[:, src, t:t + 1])
                ins.then_inc(s_ss, 1)

            def do_ba(_):
                sc.wait_ge(s_bap, 1)
                sc.wait_ge(s_rstd, 1)
                for t in range(T):
                    ins = act(ba[:, t, :], M[0][:, 16 * t:16 * t + 16], ACT.Copy, scale=rstd[:, 0, t:t + 1])
                ins.then_inc(s_ba, 1)
                sc.wait_ge(s_ba, 1)
                act(beta[:, :, :], ba[:, :, 0:H_DN], ACT.Tanh, scale=0.5).then_inc(s_baA, 1)
                link(act(alog[:, :], alog[:, :], ACT.Exp))
                sc.wait_ge(s_baD, 1)
                link(act(ge[:, :, :], gu[:, :, :], ACT.Abs))
                link(act(ge[:, :, :], ge[:, :, :], ACT.Exp, scale=-1.0))
                sc.wait_ge(s_baD, 2)
                act(ge[:, :, :], ge[:, :, :], ACT.Ln, bias=1.0)
                act(lnb[:, :, :], beta[:, :, :], ACT.Ln).then_inc(s_baA, 1)

            def do_za(g):
                sc.wait_ge(*evac_done(4 * g + 3))
                act(za[:, :, 512 * g:512 * g + 512], proj[:, 3, :, :], ACT.Tanh, scale=0.5).then_inc(s_zat, 1)

            def do_dnC(h):
                sc.wait_ge(s_cv4, 12 * h + 12)
                y = ykqv[:, h % 4, :, :]
                act(M[0][:, :].rearrange("p (c s) -> p c s", c=2), y[:, 0:2, :], ACT.Tanh, scale=0.5)
                act(M[1][:, 0:S], y[:, 2, :], ACT.Tanh, scale=0.5).then_inc(s_th, 1)

            def do_dnB(h):
                sc.wait_ge(s_back, h + 1)
                if h >= 4:
                    sc.wait_ge(s_owp, h - 3)
                sc.wait_ge(s_ss, 1)
                act(tok[:, h % 4, :, :], M[2][:, 0:384].rearrange("p (c n) -> p c n", c=3), ACT.Copy).then_inc(s_tok, 1)

            def do_dnV(g):
                sc.wait_ge(s_lnq, 2 * g + 1)
                act(hln[:, g, :, :], hln[:, g, :, :], ACT.Ln).then_inc(s_lnq, 1)
                sc.wait_ge(s_ei, g + 1)
                act(ex[:, g, :, :], ei[:, g, :, :], ACT.Exp).then_inc(s_ex, 1)

            def do_dnG(h):
                g, hl = h // 4, h % 4
                sc.wait_ge(s_gp, h + 1)
                if h >= 4:
                    sc.wait_ge(s_5ep, h - 3)
                for t in range(T):
                    ins = act(aq[:, 2 * hl + t, :, :], M[1][:, 256 * t:256 * t + 256].rearrange("p (c n) -> p c n", c=2),
                              ACT.Exp, bias=cc[:, g, hl, t:t + 1])
                ins.then_inc(s_eq, 1)

            def do_d4x(i):
                pr, l = divmod(i, 7)
                g, par = divmod(pr, 2)
                if l:
                    sc.wait_ge(s_x1p[par], 7 * g + l + 1)
                    act(ofx[:, par, :, :], M[0][:, :].rearrange("p (m n) -> p m n", m=4), ACT.Copy).then_inc(s_x1[par], 1)

            def do_d5a(h):
                sc.wait_ge(s_5ap, h + 1)
                act(dw[:, 0, :], M[0][:, 0:128], ACT.Copy).then_inc(s_5a, 1)

            def do_d5b(h):
                sc.wait_ge(s_5bp, h + 1)
                if h:
                    sc.wait_ge(s_oss, h)
                act(dw[:, 1, :], M[1][:, 0:128], ACT.Copy)
                act(tok[:, h % 4, 0, :], M[1][:, 128:256], ACT.Copy).then_inc(s_5b, 1)

            def do_d5c(h):
                g, hl = h // 4, h % 4
                sc.wait_ge(s_5cp, h + 1)
                if h:
                    sc.wait_ge(s_5e, h)
                act(dw[:, 3, :], M[2][:, 128:256], ACT.Copy, scale=ex[:, g, 2, 2 * hl + 1:2 * hl + 2]).then_inc(s_5cA, 1)

            def do_d5d(h):
                sc.wait_ge(s_5dp, h + 1)
                act(dw[:, 2, :], M[0][:, 0:128], ACT.Copy).then_inc(s_5d, 1)

            def do_d5e(h):
                g, hl = h // 4, h % 4
                sc.wait_ge(s_5e, h + 1)
                for t in range(T):
                    ins = act(dw[:, 1 + t, :], tok[:, hl, t, :], ACT.Square, accum_out=oss[:, g, 2 * hl + t:2 * hl + t + 1])
                ins.then_inc(s_oss, 1)

            def do_d7(h):
                sc.wait_ge(s_owp, h + 1)
                act(mix[:, h, :], M[2][:, 0:S], ACT.Copy, scale=gain("ev_dn_norm_g", 0)).then_inc(s_mixa, 1)

            def do_glu(i):
                sc.wait_ge(*evac_done(9 + 2 * i))
                act(proj[:, 2 * i + 1, :, :], proj[:, 2 * i + 1, :, :], ACT.Tanh, scale=0.5).then_inc(s_glt, 1)

            def do_gT(ct):
                sc.wait_ge(s_gtp, ct + 1)
                sc.wait_ge(s_t[0], 14)
                sc.wait_ge(s_t[1], 14)
                act(cvr[:, ct + 2, :], M[3][:, 0:S], ACT.Copy, scale=0.5).then_inc(s_gt, 1)

            def do_lnm(_):
                sc.wait_ge(s_mup, 1)
                act(scr[:, 0:S], M[0][:, 0:S], ACT.Copy, scale=1.0 / CVW).then_inc(s_mu, 1)

            def do_lnv(ct):
                sc.wait_ge(s_xc, 1)
                if ct >= 2:
                    sc.wait_ge(s_lvp, ct - 1)
                act(cvr[:, 8 + ct % 2, :], cvr[:, ct, :], ACT.Square).then_inc(s_lsq, 1)

            def do_lnr(_):
                sc.wait_ge(s_var, 1)
                act(scr[:, S:2 * S], scr[:, S:2 * S], ACT.Sqrt).then_inc(s_std, 1)

            def do_lno(ct):
                sc.wait_ge(s_ly, ct + 1)
                if ct >= 2:
                    sc.wait_ge(s_mixb, ct - 1)
                act(cvr[:, 8 + ct % 2, :], cvr[:, ct, :], ACT.Tanh, scale=0.5).then_inc(s_lt, 1)

            def do_zT(n):
                kt = zsource(n)[3]
                sc.wait_ge(s_zp, n + 1)
                if n < 8:
                    sc.wait_ge(s_t[0], 14)
                    sc.wait_ge(s_t[1], 14)
                elif n < 16:
                    sc.wait_ge(s_ow, 16)
                elif n == 16:
                    sc.wait_ge(s_xl, 48)
                elif n == 32:
                    sc.wait_ge(s_xl, 56)
                act(mix[:, kt, :], M[3][:, 0:S], ACT.Copy)
                act(M[3][:, S:2 * S], M[3][:, 0:S], ACT.Tanh, scale=0.5).then_inc(s_zc, 1)

            def squares(i):
                sc.wait_ge(*evac_done(MQJOB[i]))
                if i < 2:
                    sc.wait_ge(s_mixb, 8)
                if i == 2:
                    sc.wait_ge(s_sbcp, 16)
                if order[i] > 1:
                    sc.wait_ge(s_mqs, order[i] - 1)
                for t in range(T):
                    for hd in range(2):
                        ins = act(scr[:, 256 * (2 * t + hd):256 * (2 * t + hd) + 256],
                                  proj[:, MQSLOT[i], t, 256 * hd:256 * hd + 256], ACT.Square,
                                  accum_out=qss[:, i, 2 * t + hd:2 * t + hd + 1])
                ins.then_inc(s_mqs, 1)

            def do_mqT(dt):
                sc.wait_ge(s_mqp, dt + 1)
                sc.wait_ge(*((s_mixb, 8) if dt < 8 else (s_sbop, 16)))
                act(qmt[:, dt % 8, :], M[dt % 2][:, 0:S], ACT.Copy,
                    scale=gain("ev_q_norm_m" if dt < 8 else "od_q_norm_m", dt % 2)).then_inc(s_mqT, 1)

            def do_mkT(dt):
                sc.wait_ge(s_mkp, dt + 1)
                sc.wait_ge(s_ss, 2)
                act(kmt[:, dt, :], M[dt % 2][:, 0:S], ACT.Copy, scale=gain("mem_k_norm_g", dt % 2)).then_inc(s_mkT, 1)

            def do_mas(n):
                i, hd2 = 2 * (n // 4) + (n % 4) // 2, n % 2
                sc.wait_ge(s_nb, n + 1)
                if n:
                    sc.wait_ge(s_ptp, n)
                for t in range(T):
                    ins = act(prob[:, t, :], M[0][:, 256 * t:256 * t + 256], ACT.Exp, bias=snb[:, n, t:t + 1],
                              scale=qrs[:, i, 2 * t + hd2:2 * t + hd2 + 1], accum_out=ssm[:, n, t:t + 1])
                ins.then_inc(s_exp, 1)

            def do_mat(n):
                sc.wait_ge(s_ptp, n + 1)
                if n:
                    sc.wait_ge(s_maop, 2 * n)
                act(probt, M[1][:, :].rearrange("p (m s) -> p m s", m=2), ACT.Copy).then_inc(s_pt, 1)

            def do_sbn(g):
                for c in range(2):
                    sc.wait_ge(*evac_done(J_ODIN + 4 * g + c))
                    if 2 * g + c:
                        sc.wait_ge(s_sbr, 2 * g + c)
                    else:
                        sc.wait_ge(s_maop, 8)
                    if g:
                        sc.wait_ge(s_sbcp, 4 * g)
                    act(scr[:, :], pflat[:, 1024 * c:1024 * c + 1024], ACT.Square).then_inc(s_sbs, 1)

            def do_tab(_):
                sc.preload_act_table_set("natural_log_exp_and_others")

            def do_sbT(h):
                sc.wait_ge(s_sbtp, h + 1)
                if h >= 4:
                    sc.wait_ge(s_sbzp, h - 3)
                else:
                    sc.wait_ge(s_scp, 4)
                act(qk[:, h % 4, 0, :], M[0][:, 0:S], ACT.Copy, scale=qgain[:, 0:1])
                act(qk[:, h % 4, 1, :], M[0][:, S:2 * S], ACT.Copy, scale=gain("od_k_norm_c", 0)).then_inc(s_sbT, 1)

            def do_sbz(h):
                sc.wait_ge(s_sbzp, h + 1)
                sc.wait_ge(s_sbr, 2 * (h // 4) + 2)
                if h:
                    sc.wait_ge(s_sbsp, h)
                link(act(absz, M[1][:, 0:384], ACT.Abs))
                link(act(absz, absz, ACT.Exp, scale=-1.0))
                act(absz, absz, ACT.Ln, bias=1.0).then_inc(s_sbA, 1)

            def do_sbc(h):
                sc.wait_ge(s_sbcp, h + 1)
                if h:
                    sc.wait_ge(s_sbop, h)
                act(wts, M[1][:, 0:384], ACT.Exp).then_inc(s_sbW, 1)

            def do_mload(_):
                sc.wait_ge(s_5cp, 8)
                sc.wait_ge(s_5dp, 8)
                sc.dma_start(memx, mem.rearrange("(t p) d -> p t d", p=128)).then_inc(s_min, 16)

            def do_xload(_):
                sc.wait_ge(s_mixa, 8)
                sc.wait_ge(s_ss, 2)
                sc.dma_start(hid[:, :, :], x.rearrange("(t p) d -> p t d", p=128)).then_inc(s_xre, 16)

            steps = {"chunk": do_chunk, "evac": do_evac, "xt": do_xt, "mf": do_mf, "rstd": do_rstd, "ba": do_ba,
                     "za": do_za, "dnC": do_dnC, "dnB": do_dnB, "dnV": do_dnV, "dnG": do_dnG, "d4x": do_d4x,
                     "d5a": do_d5a, "d5b": do_d5b, "d5c": do_d5c, "d5d": do_d5d, "d5e": do_d5e, "d7": do_d7,
                     "glu": do_glu, "gT": do_gT, "lnm": do_lnm, "lnv": do_lnv, "lnr": do_lnr, "lno": do_lno,
                     "zT": do_zT, "mqs": squares, "mks": lambda i: squares(4 + i), "mqT": do_mqT, "mkT": do_mkT,
                     "mas": do_mas, "mat": do_mat, "sbn": do_sbn, "tab": do_tab, "sbT": do_sbT, "sbz": do_sbz,
                     "sbc": do_sbc, "mload": do_mload, "xload": do_xload}
            sc.wait_ge(s_vp, 1)
            for a, n in enumerate((NVEC, 96, 128, 120)):
                ins = act(vt[:, 128 * a:128 * a + n], M[0][:, 128 * a:128 * a + n], ACT.Copy)
            ins.then_inc(s_vt, 1)
            sc.wait_ge(s_vt, 1)
            sc.wait_ge(s_const, 1)
            act(qgain[:, :], gain("od_q_norm_c", 0), ACT.Copy, scale=128.0 ** -0.5)
            sc.wait_ge(s_small, 48)
            act(bah, wba, ACT.Copy).then_inc(s_wbh, 1)
            for c in range(AHEAD):
                split(c)
            for st, i in plan:
                if st in steps:
                    steps[st](i)

        @block.vector
        def _(ve):
            own = [0]

            def link(ins):
                own[0] += 1
                ins.then_inc(s_dveq, 1)
                ve.wait_ge(s_dveq, own[0])

            def split(c):
                ve.wait_ge(s_hi, c + 1)
                if c == RING - 1:
                    ve.wait_ge(s_bap, 1)
                vec.tensor_tensor(wlo[:, c % RING, :, :], raw[:, c % RAWS, :, :], whi[:, c % RING, :, :].bitcast(F32),
                                  ALU.subtract).then_inc(s_lo, 1)

            def do_chunk(c):
                if c + AHEAD < nch:
                    split(c + AHEAD)

            def do_evac(j):
                if j < J_EVOUT or J_ODIN <= j < J_ODOUT:
                    return
                b = (j - J_EVOUT) % 4 if j < J_ODIN else (j - J_ODOUT) % 4
                ve.wait_ge(s_pe, CH0[j + 1])
                ve.wait_ge(s_xre, 16)
                if evac_done(j)[1] > 1:
                    ve.wait_ge(s_evD, evac_done(j)[1] - 1)
                if j == J_ODOUT:
                    ve.wait_ge(s_xp, 48)
                    ve.wait_ge(s_ss, 3)
                for t in range(T):
                    v = hid[:, t, 512 * b:512 * b + 512]
                    ins = vec.tensor_tensor(v, v, pj[j % 2][t][:, :], ALU.add)
                ins.then_inc(s_evD, 1)

            def do_xt(n):
                ve.wait_ge(s_xh, n + 1)
                vec.scalar_tensor_tensor(out=xlo[:, SLOT[n], :], in0=M[banks("xt", n)[0]][:, 0:S], scalar=xt_gain(n),
                                         in1=xhi[:, SLOT[n], :].bitcast(F32), op0=ALU.mult, op1=ALU.subtract
                                         ).then_inc(s_xl, 1)

            def do_mf(n):
                ve.wait_ge(s_xh, n + 1)
                vec.tensor_tensor(xlo[:, SLOT[n], :], mix[:, n - 32 if n < 56 else n - 72, :],
                                  xhi[:, SLOT[n], :].bitcast(F32), ALU.subtract).then_inc(s_xl, 1)

            def do_rstd(src):
                ve.wait_ge(s_ss, src + 1)
                vec.tensor_scalar(ssq[:, src, :], ssq[:, src, :], 1.0 / D, EPS, ALU.mult, ALU.add).then_inc(s_ms, 1)

            def do_ba(_):
                ve.wait_ge(s_ba, 1)
                ve.wait_ge(s_small, 48)
                vec.tensor_tensor(gu[:, :, :], ba[:, :, H_DN:2 * H_DN],
                                  dtb[:, :].unsqueeze(1).broadcast_to([128, T, H_DN]), ALU.add).then_inc(s_baD, 1)
                ve.wait_ge(s_baA, 1)
                link(vec.tensor_scalar(beta[:, :, :], beta[:, :, :], 0.5, 0.5, ALU.mult, ALU.add))
                link(vec.tensor_scalar(beta[:, :, :], beta[:, :, :], 1e-18, None, ALU.max))
                vec.tensor_scalar(halfb[:, :, :], beta[:, :, :], 0.5, None, ALU.mult).then_inc(s_baD, 1)
                ve.wait_ge(s_baA, 2)
                link(vec.scalar_tensor_tensor(out=ge[:, :, :], in0=gu[:, :, :], scalar=0.0, in1=ge[:, :, :],
                                              op0=ALU.max, op1=ALU.add))
                vec.scalar_tensor_tensor(out=gl_in[:, :, :], in0=ge[:, :, :], scalar=-1.0,
                                         in1=alog[:, :].unsqueeze(1).broadcast_to([128, T, H_DN]),
                                         op0=ALU.mult, op1=ALU.mult).then_inc(s_baD, 1)
                ve.wait_ge(s_gcp, 1)
                vec.tensor_copy(gcl[:, :, :, :].rearrange("p a t h -> p (a t h)"), M[1][:, 0:32]).then_inc(s_gc, 1)

            def do_za(g):
                ve.wait_ge(s_zat, g + 1)
                v = za[:, :, 512 * g:512 * g + 512]
                vec.scalar_tensor_tensor(out=v, in0=v, scalar=1.0, in1=proj[:, 3, :, :], op0=ALU.add, op1=ALU.mult
                                         ).then_inc(s_za, 1)

            def do_dnC(h):
                ve.wait_ge(s_dnT, h + 1)
                if h >= 4:
                    ve.wait_ge(s_5cp, h - 3)
                src = [M[0][:, S:2 * S], M[0][:, 0:S], M[1][:, 0:S]]
                tile = [8 + h, h, 16 + h]
                n = 12 * h
                for r in range(CONV):
                    for c in range(3):
                        y = ykqv[:, h % 4, c, :]
                        col = V_CONV + 24 * (CONV - 1 - r) + tile[c]
                        wc = vt[:, col:col + 1]
                        if r == 0:
                            ins = vec.tensor_scalar(y, src[c], wc, None, ALU.mult)
                        else:
                            ve.wait_ge(s_cv4, n + 1 - 3)
                            ins = vec.scalar_tensor_tensor(out=y[:, r:], in0=src[c][:, 0:S - r], scalar=wc,
                                                           in1=y[:, r:], op0=ALU.mult, op1=ALU.add)
                        ins.then_inc(s_cv4, 1)
                        n += 1
                ve.wait_ge(s_th, h + 1)
                y = ykqv[:, h % 4, :, :]
                vec.scalar_tensor_tensor(out=y[:, 0:2, :], in0=M[0][:, :].rearrange("p (c s) -> p c s", c=2), scalar=1.0,
                                         in1=y[:, 0:2, :], op0=ALU.add, op1=ALU.mult).then_inc(s_silu, 1)
                vec.scalar_tensor_tensor(out=y[:, 2, :], in0=M[1][:, 0:S], scalar=1.0, in1=y[:, 2, :],
                                         op0=ALU.add, op1=ALU.mult).then_inc(s_silu, 1)

            def do_dnB(h):
                ve.wait_ge(s_np, h + 1)
                vec.tensor_copy(nrm[:, h, :], M[0][:, 0:4]).then_inc(s_nrm, 1)

            def do_dnV(g):
                hs = slice(4 * g, 4 * g + 4)
                ve.wait_ge(s_nrm, 4 * g + 4)
                vec.tensor_scalar(hln[:, g, :, :], nrm[:, hs, :], 4 * EPS, None, ALU.add).then_inc(s_lnq, 1)
                ve.wait_ge(s_lnq, 2 * g + 2)
                ve.wait_ge(s_gc, 1)
                ve.wait_ge(s_baA, 2)
                link(vec.tensor_scalar(hln[:, g, :, :], hln[:, g, :, :], -0.5, None, ALU.mult))
                lk, lq = hln[:, g, :, 0:2], hln[:, g, :, 2:4]
                gc = gcl[:, 0, :, hs].rearrange("p t h -> p h t")
                gl = gcl[:, 1, :, hs].rearrange("p t h -> p h t")
                lb = lnb[:, :, hs].rearrange("p t h -> p h t")

                def e(a):
                    return ei[:, g, a, :].rearrange("p (h t) -> p h t", h=4)
                vec.tensor_tensor(cc[:, g, :, :], lk, gc, ALU.subtract)
                link(vec.tensor_tensor(e(0), lk, gc, ALU.add))
                vec.tensor_tensor(e(0), e(0), lb, ALU.add)
                vec.tensor_tensor(e(1), cc[:, g, :, :], gl, ALU.add)
                vec.tensor_copy(e(2), gc)
                vec.tensor_scalar(e(3), lq, -0.5 * math.log(128.0), None, ALU.add).then_inc(s_ei, 1)
                ve.wait_ge(s_rp, g + 1)
                vec.tensor_copy(rows[:, g, :], M[1][0:24, 0:128]).then_inc(s_rows, 1)
                ve.wait_ge(s_ex, g + 1)
                link(vec.tensor_scalar(nks[:, g, :], ex[:, g, 0, :], -1.0, None, ALU.mult))

            def do_dnG(h):
                ve.wait_ge(s_eq, h + 1)
                v = aq[:, 2 * (h % 4):2 * (h % 4) + 2, :, :].rearrange("p m c n -> p (m c n)")
                vec.tensor_tensor(v, M[0][:, :], v, ALU.mult).then_inc(s_aq, 1)

            def do_d4x(i):
                pr, l = divmod(i, 7)
                g, par = divmod(pr, 2)
                if l == 0:
                    ve.wait_ge(s_x1p[par], 7 * g + 1)
                    eye = ident[:, :].unsqueeze(1).broadcast_to([128, 4, 128])
                    vec.tensor_tensor(tinv[:, par, :, :], eye, M[0][:, :].rearrange("p (m n) -> p m n", m=4), ALU.subtract)
                    vec.tensor_tensor(tinvt[:, par, :, :], eye, ofx[:, par, :, :], ALU.subtract).then_inc(s_t[par], 1)

            def do_d4y(i):
                pr, l = divmod(i, 7)
                g, par = divmod(pr, 2)
                if l == 0:
                    return
                ve.wait_ge(s_x2p[par], 6 * g + l)
                ve.wait_ge(s_t[par], 7 * g + l)
                m1, m2 = (M[b][:, :].rearrange("p (m n) -> p m n", m=4) for b in (1, 2))
                if l < 6:
                    vec.tensor_tensor(tinv[:, par, :, :], tinv[:, par, :, :], m1, ALU.subtract)
                    vec.tensor_tensor(tinvt[:, par, :, :], tinvt[:, par, :, :], m2, ALU.subtract).then_inc(s_t[par], 1)
                else:
                    vec.tensor_tensor(ofx[:, par, :, :], tinvt[:, par, :, :], m2, ALU.subtract).then_inc(s_t[par], 1)

            def do_d5c(h):
                g, hl = h // 4, h % 4
                ve.wait_ge(s_5cA, h + 1)
                ve.wait_ge(s_tks, h + 1)
                vec.scalar_tensor_tensor(out=tok[:, hl, 2, :], in0=M[2][:, 0:128], scalar=nks[:, g, 2 * hl + 1:2 * hl + 2],
                                         in1=tok[:, hl, 2, :], op0=ALU.mult, op1=ALU.add).then_inc(s_5c, 1)

            def do_d5e(h):
                ve.wait_ge(s_5ep, h + 1)
                vec.tensor_tensor(tok[:, h % 4, 1, :], dw[:, 3, :], M[1][:, 0:128], ALU.add).then_inc(s_5e, 1)

            def do_d6(g):
                ve.wait_ge(s_oss, 4 * g + 4)
                sq = ex[:, g, 3, :]
                link(vec.tensor_tensor(oms[:, g, :], oss[:, g, :], sq, ALU.mult))
                link(vec.tensor_tensor(oms[:, g, :], oms[:, g, :], sq, ALU.mult))
                vec.tensor_scalar(oms[:, g, :], oms[:, g, :], 1.0 / 128, EPS, ALU.mult, ALU.add).then_inc(s_oms, 1)
                ve.wait_ge(s_opw, g + 1)
                vec.scalar_tensor_tensor(out=ofac[:, g, :], in0=oms[:, g, :], scalar=0.5, in1=sq, op0=ALU.mult,
                                         op1=ALU.mult).then_inc(s_of6, 1)

            def do_d7(h):
                g, hl = h // 4, h % 4
                ve.wait_ge(s_of6, g + 1)
                ve.wait_ge(s_za, g + 1)
                for t in range(T):
                    v = tok[:, hl, t, :]
                    vec.scalar_tensor_tensor(out=v, in0=v, scalar=ofac[:, g, 2 * hl + t:2 * hl + t + 1],
                                             in1=za[:, t, 128 * h:128 * h + 128], op0=ALU.mult, op1=ALU.mult
                                             ).then_inc(s_ow, 1)

            def do_glu(i):
                ve.wait_ge(s_glt, i + 1)
                a = proj[:, 2 * i, :, :]
                vec.scalar_tensor_tensor(out=a, in0=proj[:, 2 * i + 1, :, :], scalar=1.0, in1=a, op0=ALU.add,
                                         op1=ALU.mult).then_inc(s_glu, 1)

            def do_conv(i):
                pr, q = divmod(i, 8)
                for k in range(8 * q, min(8 * q + 8, 2 * TAPS)):
                    d, which = divmod(k, 2)
                    ct = 2 * pr + which
                    n = 2 * TAPS * pr + k
                    c, gsrc = cvr[:, ct, :], cvr[:, ct + 2, :]
                    col = V_DW + 8 * (TAPS - 1 - d) + ct
                    if d == 0:
                        if n:
                            ve.wait_ge(s_cv, 2 * TAPS * pr if which == 0 else 2 * TAPS * pr)
                        ve.wait_ge(s_gt, ct + 1)
                        ins = vec.tensor_scalar(c, gsrc, vt[:, col:col + 1], gain("ev_dw_b", ct), ALU.mult, ALU.add)
                    else:
                        ve.wait_ge(s_cv, n - 1)
                        ins = vec.scalar_tensor_tensor(out=c[:, d:], in0=gsrc[:, 0:S - d], scalar=vt[:, col:col + 1],
                                                       in1=c[:, d:], op0=ALU.mult, op1=ALU.add)
                    ins.then_inc(s_cv, 1)

            def do_lnm(_):
                ve.wait_ge(s_mu, 1)
                v = cvr[:, 0:8, :]
                vec.tensor_tensor(v, v, scr[:, 0:S].unsqueeze(1).broadcast_to([128, 8, S]), ALU.subtract).then_inc(s_xc, 1)

            def do_lnr(_):
                ve.wait_ge(s_lvp, 8)
                r = scr[:, S:2 * S]
                vec.tensor_scalar(r, M[1][:, 0:S], 1.0 / CVW, EPS, ALU.mult, ALU.add).then_inc(s_var, 1)
                ve.wait_ge(s_std, 1)
                link(vec.reciprocal(r, r))
                v = cvr[:, 0:8, :]
                vec.tensor_tensor(v, v, r.unsqueeze(1).broadcast_to([128, 8, S]), ALU.mult).then_inc(s_xn, 1)

            def do_lno(ct):
                ve.wait_ge(s_xn, 1)
                c = cvr[:, ct, :]
                vec.tensor_scalar(c, c, gain("ev_ln_g", ct), gain("ev_ln_b", ct), ALU.mult, ALU.add).then_inc(s_ly, 1)
                ve.wait_ge(s_lt, ct + 1)
                ve.wait_ge(s_z, ct + 1)
                link(vec.scalar_tensor_tensor(out=c, in0=cvr[:, 8 + ct % 2, :], scalar=1.0, in1=c, op0=ALU.add, op1=ALU.mult))
                v = mix[:, 8 + ct, :]
                vec.scalar_tensor_tensor(out=v, in0=c, scalar=0.25, in1=v, op0=ALU.mult, op1=ALU.mult).then_inc(s_mixb, 1)

            def do_zT(n):
                ve.wait_ge(s_zc, n + 1)
                v = mix[:, zsource(n)[3], :]
                vec.scalar_tensor_tensor(out=v, in0=M[3][:, S:2 * S], scalar=1.0, in1=v, op0=ALU.add, op1=ALU.mult
                                         ).then_inc(s_z, 1)

            mq_n = [0]

            def mean_squares(i):
                mq_n[0] += 1
                n = mq_n[0]
                ve.wait_ge(s_mqs, n)
                vec.tensor_scalar(qss[:, i, :], qss[:, i, :], 1.0 / 256, EPS, ALU.mult, ALU.add).then_inc(s_mqm, 1)
                ve.wait_ge(s_mqr, n)

            def do_mqs(i):
                mean_squares(i)
                vec.tensor_scalar(qrs[:, i, :], qss[:, i, :], 1.0 / 16, None, ALU.mult).then_inc(s_mqk, 1)

            def do_mks(i):
                mean_squares(4 + i)
                for t in range(T):
                    for hd in range(2):
                        v = proj[:, MQSLOT[4 + i], t, 256 * hd:256 * hd + 256]
                        ins = vec.tensor_scalar(v, v, qss[:, 4 + i, 2 * t + hd:2 * t + hd + 1], None, ALU.mult)
                ins.then_inc(s_mks, 1)

            def do_mas(n):
                i, hd2 = 2 * (n // 4) + (n % 4) // 2, n % 2
                ve.wait_ge(s_scp, n + 1)
                ve.wait_ge(s_mqk, i + 1)
                link(vec.tensor_reduce(smx[:, n, :], M[0][:, :].rearrange("p (t m) -> p t m", t=T), AX.X, ALU.max))
                vec.scalar_tensor_tensor(out=snb[:, n, :], in0=smx[:, n, :], scalar=-1.0, in1=qrs[:, i, hd2:4:2],
                                         op0=ALU.mult, op1=ALU.mult).then_inc(s_nb, 1)
                ve.wait_ge(s_exp, n + 1)
                link(vec.reciprocal(srs[:, n, :], ssm[:, n, :]))
                for t in range(T):
                    ins = vec.tensor_scalar(prob[:, t, :], prob[:, t, :], srs[:, n, t:t + 1], None, ALU.mult)
                ins.then_inc(s_pr, 1)

            def do_mao(m):
                ve.wait_ge(s_maop, m + 1)
                ve.wait_ge(s_z, (8 if m < 8 else 32) + m % 8 + 1)
                v = mix[:, 16 + m % 8, :]
                vec.scalar_tensor_tensor(out=v, in0=M[2][:, 0:S], scalar=0.5, in1=v, op0=ALU.mult, op1=ALU.mult
                                         ).then_inc(s_mao, 1)

            def do_sbn(g):
                for c in range(2):
                    ve.wait_ge(s_sbs, 2 * g + c + 1)
                    vec.tensor_reduce(bss[:, g, 8 * c:8 * c + 8], scr[:, :].rearrange("p (a n) -> p a n", n=128),
                                      AX.X, ALU.add).then_inc(s_sbr, 1)
                ve.wait_ge(s_sbr, 2 * g + 2)
                vec.tensor_scalar(bss[:, g, :], bss[:, g, :], 1.0 / 128, EPS, ALU.mult, ALU.add).then_inc(s_sbm, 1)

            def do_sbz(h):
                ve.wait_ge(s_sbA, h + 1)
                if h:
                    ve.wait_ge(s_sbcp, h)
                vec.scalar_tensor_tensor(out=spz, in0=M[1][:, 0:384], scalar=0.0, in1=absz, op0=ALU.max, op1=ALU.add
                                         ).then_inc(s_sbsp, 1)

            def do_sbo(h):
                ve.wait_ge(s_sbop, h + 1)
                ve.wait_ge(s_z, 16 + h + 1)
                v = mix[:, h, :]
                vec.scalar_tensor_tensor(out=v, in0=M[2][:, 0:S], scalar=0.5, in1=v, op0=ALU.mult, op1=ALU.mult
                                         ).then_inc(s_sbo, 1)

            steps = {"chunk": do_chunk, "evac": do_evac, "xt": do_xt, "mf": do_mf, "rstd": do_rstd, "ba": do_ba,
                     "za": do_za, "dnC": do_dnC, "dnB": do_dnB, "dnV": do_dnV, "dnG": do_dnG, "d4x": do_d4x,
                     "d4y": do_d4y, "d5c": do_d5c, "d5e": do_d5e, "d6": do_d6, "d7": do_d7, "glu": do_glu,
                     "conv": do_conv, "lnm": do_lnm, "lnr": do_lnr, "lno": do_lno, "zT": do_zT, "mqs": do_mqs,
                     "mks": do_mks, "mas": do_mas, "mao": do_mao, "sbn": do_sbn, "sbz": do_sbz, "sbo": do_sbo}
            ve.wait_ge(s_vt, 1)
            ve.wait_ge(s_wbh, 1)
            vec.tensor_tensor(bal, wba, bah.bitcast(F32), ALU.subtract).then_inc(s_wbl, 1)
            for c in range(AHEAD):
                split(c)
            for st, i in plan:
                if st in steps:
                    steps[st](i)

        @block.tensor
        def _(pe):
            def take(st, i):
                for q in bank_free[st, i]:
                    pe.wait_ge(*q)

            def three(out_, k, t, hi, lo, first, last):
                xh, xl = xhi[:, k, 128 * t:128 * t + 128], xlo[:, k, 128 * t:128 * t + 128]
                mm(out_, xh, hi, start=first, stop=False)
                mm(out_, xh, lo, start=False, stop=False)
                return mm(out_, xl, hi, start=False, stop=last)

            def do_chunk(c):
                j = JOB_OF[c]
                kts, fill = JOBS[j][3], JOBS[j][4]
                i = c - CH0[j]
                if i == 0 and j >= 2:
                    pe.wait_ge(*evac_done(j - 2))
                pe.wait_ge(s_xl, fill + 2 * i + 2)
                pe.wait_ge(s_lo, c + 1)
                for k in (2 * i, 2 * i + 1):
                    for t in range(T):
                        ins = three(pj[j % 2][t][:, :], SLOT[fill + k], t, whi[:, c % RING, k % 2, :],
                                    wlo[:, c % RING, k % 2, :], k == 0, k == kts - 1)
                ins.then_inc(s_pe, 1)

            def turn(dst, src):
                return nc.tensor.transpose(dst, src, ident[:, :])

            def do_xt(n):
                src, k = (hid, n) if n < 16 else (memx, n - 16) if n < 32 else (hid, n - 56)
                if n < 56:
                    pe.wait_ge(*((s_xin, 16) if n < 16 else (s_min, 16)))
                else:
                    pe.wait_ge(*evac_done(30 + k // 4))
                take("xt", n)
                for t in range(T):
                    ins = turn(M[banks("xt", n)[0]][:, 128 * t:128 * t + 128], src[:, t, 128 * k:128 * k + 128])
                ins.then_inc(s_xp, 1)

            def do_ba(_):
                pe.wait_ge(s_wbl, 1)
                pe.wait_ge(s_xl, 16)
                take("ba", 0)
                for t in range(T):
                    for k in range(KT):
                        ins = three(M[0][:, 16 * t:16 * t + 16], k, t, bah[:, k, :], bal[:, k, :], k == 0, k == KT - 1)
                ins.then_inc(s_bap, 1)
                pe.wait_ge(s_baD, 3)
                g = gl_in[:, :, :].rearrange("p t h -> p (t h)")
                mm(M[1][:, 0:16], upto[:, :], g, start=True, stop=True)
                mm(M[1][:, 16:32], ones[:, :], g, start=True, stop=True).then_inc(s_gcp, 1)

            def do_dnT(h):
                for c in range(3):
                    pe.wait_ge(*evac_done(4 * (h // 4) + c))
                take("dnT", h)
                for c in range(3):
                    for t in range(T):
                        o = 256 * (c % 2) + 128 * t
                        ins = turn(M[c // 2][:, o:o + 128], proj[:, c, t, 128 * (h % 4):128 * (h % 4) + 128])
                ins.then_inc(s_dnT, 1)

            def do_dnB(h):
                pe.wait_ge(s_silu, 2 * h + 2)
                take("dnB", h)
                y = ykqv[:, h % 4, :, :]
                turn(M[2][:, 0:128], y[:, 0, 0:128])
                turn(M[2][:, 128:256], y[:, 2, 0:128])
                turn(M[2][:, 256:384], y[:, 2, 128:256]).then_inc(s_back, 1)
                pe.wait_ge(s_sq, h + 1)
                for a in range(4):
                    ins = mm(M[0][:, a:a + 1], scr[:, 128 * a:128 * a + 128], ones[:, 0:1], start=True, stop=True)
                ins.then_inc(s_np, 1)

            def do_dnV(g):
                pe.wait_ge(s_ei, g + 1)
                take("dnV", g)
                turn(M[1][0:24, 0:128], ei[:, g, 0:3, :].rearrange("p a m -> p (a m)")).then_inc(s_rp, 1)

            def do_dnG(h):
                g, hl = h // 4, h % 4
                pe.wait_ge(s_rows, g + 1)
                take("dnG", h)
                for t in range(T):
                    tc = slice(128 * t, 128 * t + 128)
                    mm(M[0][:, 256 * t:256 * t + 256].rearrange("p (c n) -> p c n", c=2), ykqv[:, hl, 0, tc],
                       ykqv[:, hl, 0:2, tc], start=True, stop=True)
                for t in range(T):
                    mm(M[1][:, 256 * t:256 * t + 256], ident[:, :], shut[:, :, :].rearrange("p c n -> p (c n)"),
                       start=(t == 0), stop=False, skip_group_check=True)
                    for c in range(2):
                        o = 256 * t + 128 * c
                        r = 16 * c + 2 * hl + t
                        ins = mm(M[1][:, o:o + 128], ident[0:24, r:r + 1].broadcast_to([24, 128]), rows[:, g, :],
                                 start=False, stop=True, skip_group_check=True)
                ins.then_inc(s_gp, 1)

            def do_d4x(i):
                pr, l = divmod(i, 7)
                g, par = divmod(pr, 2)
                pe.wait_ge(s_of[par], 7 * g + l + 1)
                if l:
                    pe.wait_ge(s_t[par], 7 * g + l)
                take("d4x", i)
                for m in range(4):
                    ins = mm(M[0][:, 128 * m:128 * m + 128], ofx[:, par, m, :], tinv[:, par, m, :] if l else ident[:, :],
                             start=True, stop=True)
                ins.then_inc(s_x1p[par], 1)

            def do_d4y(i):
                pr, l = divmod(i, 7)
                g, par = divmod(pr, 2)
                if l == 0:
                    return
                pe.wait_ge(s_x1[par], 6 * g + l)
                take("d4y", i)
                for m in range(4):
                    o = slice(128 * m, 128 * m + 128)
                    if l < 6:
                        mm(M[1][:, o], tinvt[:, par, m, :], ofx[:, par, m, :], start=True, stop=True)
                    ins = mm(M[2][:, o], ofx[:, par, m, :], tinvt[:, par, m, :], start=True, stop=True)
                ins.then_inc(s_x2p[par], 1)

            def inverse(h, t):
                return ofx[:, (h % 4) // 2, 2 * (h % 2) + t, :]

            def do_d5a(h):
                pe.wait_ge(s_tks, h + 1)
                pe.wait_ge(s_t[(h % 4) // 2], 7 * (h // 4) + 7)
                take("d5a", h)
                mm(M[0][:, 0:128], inverse(h, 0), tok[:, h % 4, 1, :], start=True, stop=True).then_inc(s_5ap, 1)

            def do_d5b(h):
                pe.wait_ge(s_5a, h + 1)
                take("d5b", h)
                mm(M[1][:, 0:128], tok[:, h % 4, 0, :], dw[:, 0, :], start=True, stop=True)
                mm(M[1][:, 128:256], aq[:, 2 * (h % 4), 1, :], dw[:, 0, :], start=True, stop=True).then_inc(s_5bp, 1)

            def do_d5c(h):
                pe.wait_ge(s_5b, h + 1)
                take("d5c", h)
                mm(M[2][:, 0:128], ykqv[:, h % 4, 0, 128:256], dw[:, 1, :], start=True, stop=True)
                mm(M[2][:, 128:256], ykqv[:, h % 4, 1, 128:256], dw[:, 1, :], start=True, stop=True).then_inc(s_5cp, 1)

            def do_d5d(h):
                pe.wait_ge(s_5c, h + 1)
                take("d5d", h)
                mm(M[0][:, 0:128], inverse(h, 1), tok[:, h % 4, 2, :], start=True, stop=True).then_inc(s_5dp, 1)

            def do_d5e(h):
                pe.wait_ge(s_5d, h + 1)
                take("d5e", h)
                mm(M[1][:, 0:128], aq[:, 2 * (h % 4) + 1, 1, :], dw[:, 2, :], start=True, stop=True).then_inc(s_5ep, 1)

            def do_d7(h):
                pe.wait_ge(s_ow, 2 * h + 2)
                take("d7", h)
                for t in range(T):
                    ins = turn(M[2][:, 128 * t:128 * t + 128], tok[:, h % 4, t, :])
                ins.then_inc(s_owp, 1)

            def do_gT(ct):
                i = ct // 4
                pe.wait_ge(s_glu, i + 1)
                take("gT", ct)
                for t in range(T):
                    ins = turn(M[3][:, 128 * t:128 * t + 128], proj[:, 2 * i, t, 128 * (ct % 4):128 * (ct % 4) + 128])
                ins.then_inc(s_gtp, 1)

            def do_lnm(_):
                pe.wait_ge(s_cv, 2 * TAPS * 8 // 2)
                take("lnm", 0)
                for ct in range(8):
                    ins = mm(M[0][:, 0:S], ones[:, :], cvr[:, ct, :], start=(ct == 0), stop=(ct == 7))
                ins.then_inc(s_mup, 1)

            def do_lnv(ct):
                pe.wait_ge(s_lsq, ct + 1)
                take("lnv", ct)
                mm(M[1][:, 0:S], ones[:, :], cvr[:, 8 + ct % 2, :], start=(ct == 0), stop=(ct == 7)).then_inc(s_lvp, 1)

            def do_zT(n):
                j, slot, col, _ = zsource(n)
                pe.wait_ge(*evac_done(j))
                take("zT", n)
                for t in range(T):
                    ins = turn(M[3][:, 128 * t:128 * t + 128], proj[:, slot, t, 128 * col:128 * col + 128])
                ins.then_inc(s_zp, 1)

            def do_mqT(dt):
                i = dt // 4
                pe.wait_ge(*evac_done(MQJOB[i]))
                take("mqT", dt)
                for t in range(T):
                    ins = turn(M[dt % 2][:, 128 * t:128 * t + 128],
                               proj[:, MQSLOT[i], t, 128 * (dt % 4):128 * (dt % 4) + 128])
                ins.then_inc(s_mqp, 1)

            def do_mkT(dt):
                i = dt // 4
                pe.wait_ge(s_mks, i + 1)
                take("mkT", dt)
                for t in range(T):
                    ins = turn(M[dt % 2][:, 128 * t:128 * t + 128],
                               proj[:, MQSLOT[4 + i], t, 128 * (dt % 4):128 * (dt % 4) + 128])
                ins.then_inc(s_mkp, 1)

            def do_mas(n):
                hd = n % 4
                pe.wait_ge(s_mqT, 8 * (n // 4) + 2 * hd + 2)
                pe.wait_ge(s_mkT, 2 * hd + 2)
                take("mas", n)
                for t in range(T):
                    for dt in range(2):
                        ins = mm(M[0][:, 256 * t:256 * t + 256], qmt[:, 2 * hd + dt, 128 * t:128 * t + 128],
                                 kmt[:, 2 * hd + dt, :], start=(dt == 0), stop=(dt == 1))
                ins.then_inc(s_scp, 1)

            def do_mat(n):
                pe.wait_ge(s_pr, n + 1)
                take("mat", n)
                for m in range(2):
                    for t in range(T):
                        ins = turn(M[1][:, 256 * m + 128 * t:256 * m + 128 * t + 128], prob[:, t, 128 * m:128 * m + 128])
                ins.then_inc(s_ptp, 1)

            def do_mao(m):
                n, dt = divmod(m, 2)
                hd = n % 4
                pe.wait_ge(s_pt, n + 1)
                pe.wait_ge(*evac_done(20 + hd // 2))
                take("mao", m)
                for mt in range(2):
                    ins = mm(M[2][:, 0:S], vm[:, mt, 256 * hd + 128 * dt:256 * hd + 128 * dt + 128], probt[:, mt, :],
                             start=(mt == 0), stop=(mt == 1))
                ins.then_inc(s_maop, 1)

            def do_sbT(h):
                pe.wait_ge(s_sbn, 2 * (h // 4) + 2)
                take("sbT", h)
                for c in range(2):
                    for t in range(T):
                        o = 256 * c + 128 * t
                        ins = turn(M[0][:, o:o + 128], proj[:, c, t, 128 * (h % 4):128 * (h % 4) + 128])
                ins.then_inc(s_sbtp, 1)

            def do_sbz(h):
                pe.wait_ge(s_sbT, h + 1)
                take("sbz", h)
                q, k = qk[:, h % 4, 0, :], qk[:, h % 4, 1, :]
                mm(M[1][:, 0:S], k[:, 0:128], q[:, 0:S], start=True, stop=False, skip_group_check=True)
                mm(M[1][:, S:384], k[:, 128:S], q[:, 128:S], start=False, stop=False, skip_group_check=True
                   ).then_inc(s_sbzp, 1)

            def do_sbc(h):
                pe.wait_ge(s_sbmk, h + 1)
                for a, b, lhs, rhs in ((0, 256, negfrom, spz[:, 0:256]), (256, 384, negfrom, spz[:, 256:384]),
                                       (128, 256, negones, spz[:, 256:384]), (0, 128, ident, shut[:, 0, :]),
                                       (256, 384, ident, shut[:, 0, :])):
                    ins = mm(M[1][:, a:b], lhs[:, :], rhs, start=False, stop=(a == 256), skip_group_check=True)
                ins.then_inc(s_sbcp, 1)

            def do_sbo(h):
                pe.wait_ge(s_sbW, h + 1)
                pe.wait_ge(*evac_done(J_ODIN + 4 * (h // 4) + 2))
                take("sbo", h)
                v = proj[:, 2, :, 128 * (h % 4):128 * (h % 4) + 128]
                mm(M[2][:, 0:S], v[:, 0, :], wts[:, 0:256], start=True, stop=False, skip_group_check=True)
                mm(M[2][:, 128:S], v[:, 1, :], wts[:, 256:384], start=False, stop=True, skip_group_check=True
                   ).then_inc(s_sbop, 1)

            steps = {"chunk": do_chunk, "xt": do_xt, "ba": do_ba, "dnT": do_dnT, "dnB": do_dnB, "dnV": do_dnV,
                     "dnG": do_dnG, "d4x": do_d4x, "d4y": do_d4y, "d5a": do_d5a, "d5b": do_d5b, "d5c": do_d5c,
                     "d5d": do_d5d, "d5e": do_d5e, "d7": do_d7, "gT": do_gT, "lnm": do_lnm, "lnv": do_lnv,
                     "zT": do_zT, "mqT": do_mqT, "mkT": do_mkT, "mas": do_mas, "mat": do_mat, "mao": do_mao,
                     "sbT": do_sbT, "sbz": do_sbz, "sbc": do_sbc, "sbo": do_sbo}
            pe.wait_ge(s_const, 1)
            pe.wait_ge(s_vrow, 16 * 15)
            for a, n in enumerate((NVEC, 96, 128, 120)):
                ins = nc.tensor.transpose(M[0][:, 128 * a:128 * a + n], vrow[0:n, a, :], ident[0:n, 0:n])
            ins.then_inc(s_vp, 1)
            for st, i in plan:
                if st in steps:
                    steps[st](i)


INS = ["x", "mem", "mem_norm_g", "w_mem_kv", "mem_k_norm_g", "ev_norm_g", "ev_w_in", "ev_conv_qkv", "ev_a_log",
       "ev_dt_bias", "ev_dn_norm_g", "ev_dw_w", "ev_dw_b", "ev_ln_g", "ev_ln_b", "ev_q_norm_m", "ev_w_out",
       "od_norm_g", "od_w_in", "od_q_norm_c", "od_k_norm_c", "od_q_norm_m", "od_w_out"]
LAST = len(JOBS)


def kernel(**inputs):
    import numpy as np
    import concourse.bacc as bacc
    from concourse.bass_utils import run_bass_kernel_spmd

    nc = bacc.Bacc("TRN2", target_bir_lowering=False, num_devices=1)
    arrays, d = {}, {}
    for name in INS:
        a = np.ascontiguousarray(inputs[name])
        arrays[f"in_{name}_dram"] = a
        d[name] = nc.dram_tensor(f"in_{name}_dram", a.shape, mybir.dt.from_np(a.dtype), kind="ExternalInput").ap()
    out = nc.dram_tensor("out_dram", (1, S, D), F32, kind="ExternalOutput").ap()

    def vecs(vrow):
        for name, n in VEC:
            v = d[name]
            v = v[0, :] if len(v.shape) == 2 else v
            yield vrow[VCOL[name]:VCOL[name] + n, 0, :], v.rearrange("(k p) -> k p", p=128)
        yield vrow[0:96, 1, :], d["ev_conv_qkv"][0, :, :].rearrange("k (c p) -> (k c) p", p=128)
        dw = d["ev_dw_w"][0, :, :].rearrange("k (c p) -> (k c) p", p=128)
        yield vrow[0:128, 2, :], dw[0:128, :]
        yield vrow[0:120, 3, :], dw[128:248, :]

    w = {"ev_in": d["ev_w_in"][0, :, :], "mem": d["w_mem_kv"], "ev_out": d["ev_w_out"][0, :, :],
         "od_in": d["od_w_in"][0, :, :], "od_out": d["od_w_out"][0, :, :]}
    prog(nc, d["x"][0, :, :], d["mem"][0, :, :], vecs, w, d["ev_a_log"][0, :], d["ev_dt_bias"][0, :],
         out[0, :, :], LAST)
    r = run_bass_kernel_spmd(nc, [arrays], core_ids=[0])
    return r.results[0]["out_dram"]
```

```python
import math

import concourse.bass as bass
from concourse import mybir
from contextlib import ExitStack

F32 = mybir.dt.float32
F32R = mybir.dt.float32r
BF16 = mybir.dt.bfloat16
ALU = mybir.AluOpType
ACT = mybir.ActivationFunctionType
AX = mybir.AxisListType

D = 2048
S = 256
T = 2
KT = D // 128
DNW, CVW, MW, SBW = 1024, 1024, 1024, 2048
H_DN, H_MEM, H_SB = 8, 4, 16
EPS = 1e-6
NEG = -1.0e30
CONV, TAPS = 4, 31

Q0, K0, V0, ZA0, BA0 = 0, DNW, 2 * DNW, 3 * DNW, 4 * DNW
GA0 = BA0 + 2 * H_DN
GB0 = GA0 + CVW
ZB0 = GB0 + CVW
QM0 = ZB0 + CVW
ZM0 = QM0 + MW
JOBS = []


def _jobs():
    for g in range(2):
        for base in (GA0, GB0, Q0, K0, V0, ZA0):
            JOBS.append(("ev_in", 0, base + 512 * g, KT, 0))
    for c0 in (ZB0, ZB0 + 512, QM0, QM0 + 512, ZM0, ZM0 + 512):
        JOBS.append(("ev_in", 0, c0, KT, 0))
    for b in range(4):
        JOBS.append(("ev_out", 0, 512 * b, 8, F_OA))
    for b in range(4):
        JOBS.append(("mem", 0, 512 * b, KT, F_MEM))
    for part in (1, 2):
        for b in range(4):
            JOBS.append(("ev_out", 1024 * part, 512 * b, 8, F_OB + 8 * (part - 1)))
    for g in range(4):
        for base in (0, SBW, 2 * SBW, 3 * SBW):
            JOBS.append(("od_in", 0, base + 512 * g, KT, F_H))
    for b in range(4):
        JOBS.append(("od_in", 0, 4 * SBW + 512 * b, KT, F_H))
    for part in range(3):
        for b in range(4):
            JOBS.append(("od_out", 1024 * part, 512 * b, 8, F_ODD + 8 * part))


F_OA, F_MEM, F_OB, F_OM, F_H, F_ODD = 16, 24, 40, 48, 56, 72
_jobs()
J_ZB, J_QM, J_ZM, J_OA, J_MEM, J_OB, J_OM, J_ODIN, J_ODOUT = 12, 14, 16, 18, 22, 26, 30, 34, 54
ADDED = [j for j in range(len(JOBS)) if JOBS[j][0] in ("ev_out", "od_out")]
COPIED = [j for j in range(len(JOBS)) if j not in ADDED]
CH0 = []
_n = 0
for _j in JOBS:
    CH0.append(_n)
    _n += _j[3] // 2
CH0.append(_n)
NCH = _n
JOB_OF = [j for j in range(len(JOBS)) for _ in range(JOBS[j][3] // 2)]

LOW, HIGH = list(range(8)), list(range(8, 16))
SLOT = LOW + HIGH + LOW + HIGH + LOW + HIGH + LOW + HIGH + LOW + HIGH + LOW + HIGH
NFILL = len(SLOT)


def fills_of(j):
    return range(JOBS[j][4], JOBS[j][4] + JOBS[j][3])


LAST_CHUNK = {}
for _j in range(len(JOBS)):
    for _i, _f in enumerate(fills_of(_j)):
        LAST_CHUNK[_f] = CH0[_j] + _i // 2 + 1


def chunks_before_fill(n):
    before = [m for m in range(n) if SLOT[m] == SLOT[n]]
    return LAST_CHUNK[before[-1]] if before else 0


VEC = [("mem_norm_g", 16), ("ev_norm_g", 16), ("od_norm_g", 16), ("mem_k_norm_g", 2), ("ev_q_norm_m", 2),
       ("od_q_norm_m", 2), ("ev_dn_norm_g", 1), ("od_q_norm_c", 1), ("od_k_norm_c", 1), ("ev_dw_b", 8),
       ("ev_ln_g", 8), ("ev_ln_b", 8)]
VCOL = {}
_n = 0
for _name, _c in VEC:
    VCOL[_name] = _n
    _n += _c
NVEC = _n
V_CONV = 128
V_DW = 256
NV = 512

RAWS, RING, AHEAD = 4, 8, 6


PSLOT = dict(zip(range(J_OA), (0, 1, 2, 3, 0, 1, 2, 3, 0, 1, 2, 3, 0, 1, 2, 3, 0, 1)))
PSLOT.update({J_MEM: 0, J_MEM + 1: 1})
PSLOT.update({j: (j - J_ODIN) % 4 for j in range(J_ODIN, J_ODOUT)})
J_GLU, J_Q, J_K, J_V, J_ZA = (0, 6), (2, 8), (3, 9), (4, 10), (5, 11)


def make_plan(last_job):
    placed = []

    def stream(k, pos, items):
        for step, cost in items:
            if step == "at":
                pos = max(pos, cost)
                continue
            placed.append((int(pos), k, len(placed), step))
            pos += cost
        return pos

    def after(j):
        return CH0[j + 1] + 3

    def deltanet(g):
        t = ("dnT", "dnC", "dnB")
        h0 = 4 * g
        s = [((t[0], h0), .2), ((t[1], h0), 3.0)]
        for h in range(h0 + 1, h0 + 4):
            s += [((t[0], h), .2), ((t[1], h), 2.8), ((t[2], h - 1), .2)]
        s += [((t[2], h0 + 3), .5), ("at", after(J_ZA[g]) - 1), (("za", g), .5), (("dnV", g), 1.5)]
        s += [(("dnG", h), .6) for h in range(h0, h0 + 4)]
        a, b = 2 * g, 2 * g + 1
        s += [(("d4x", 7 * a), .5)]
        for l in range(7):
            s += [(("d4y", 7 * a + l), 0), (("d4x", 7 * b + l), 1)]
            s += [(("d4y", 7 * b + l), 0 if l < 6 else 1)] + ([(("d4x", 7 * a + l + 1), 1)] if l < 6 else [])
        for h in range(h0, h0 + 4):
            s += [(("d5" + c, h), .6) for c in "abcde"]
        return s + [(("d6", g), 1.5)] + [(("d7", h), .4) for h in range(h0, h0 + 4)]

    stream(0, -1, [(("xt", n), 0) for n in range(4)])
    for i in range(6):
        stream(0, i, [(("xt", 4 + 2 * i), 0), (("xt", 5 + 2 * i), 0)])
    stream(0, 6, [(("rstd", 0), 0)])
    stream(0, RING + 1, [(("ba", 0), 0)])
    p = stream(1, after(J_V[0]), deltanet(0))
    p = stream(1, max(p, after(J_V[1])), deltanet(1))
    oa = int(p)
    stream(1, oa, [(("mload", 0), 0), (("xload", 0), 0)])
    conv = [(("glu", 0), .3)] + [(("gT", ct), .4) for ct in range(4)]
    conv += [(("conv", q), 1.75) for q in range(12)] + [(("conv", q), 3.6) for q in range(12, 16)]
    conv += [("at", after(J_GLU[1] + 1)), (("glu", 1), .3)] + [(("gT", ct), .4) for ct in range(4, 8)]
    conv += [(("conv", q), 3.6) for q in range(16, 32)]
    p = stream(2, after(J_GLU[0] + 1), conv)
    zt = max(after(J_ZB + 1), oa - 12)
    stream(3, zt, [(("zT", n), .8) for n in range(8)])
    stream(3, max(after(J_ZM), oa + 1), [(("zT", n), .5) for n in range(8, 12)])
    stream(3, max(after(J_ZM + 1), oa + 3), [(("zT", n), .5) for n in range(12, 16)])
    p = max(p, after(J_ZM + 1) + 8)
    p = stream(2, p, [(("lnm", 0), 2)])
    p = int(p) + 1
    stream(2, p, [(("lnv", ct), 0) for ct in range(8)])
    p = stream(2, p, [(("lnr", 0), 4)])
    p = stream(2, p, [(("lno", ct), .7) for ct in range(8)])
    p = stream(4, after(J_MEM), [(("mks", 0), 1)] + [(("mkT", dt), .4) for dt in range(4)])
    p = stream(4, after(J_MEM + 1), [(("mks", 1), 1)] + [(("mkT", dt), .4) for dt in range(4, 8)])
    p = stream(4, p, [(("mqs", i), 1) for i in range(2)] + [(("mqT", dt), .3) for dt in range(8)])
    att = [(("mas", 0), 1)]
    for n in range(4):
        att += [(("mat", n), .8)] + ([(("mas", n + 1), .8)] if n < 3 else []) + [(("mao", 2 * n), .4), (("mao", 2 * n + 1), .4)]
    stream(4, max(p, after(J_MEM + 3) - 2), att)
    for k in range(8):
        stream(5, CH0[J_OA] + k // 2 - 2, [(("mf", F_OA + k), 0)])
        stream(5, CH0[J_OB] + k // 2 - 3, [(("mf", F_OB + k), 0)])
        stream(5, CH0[J_OM] + k // 2 - 1, [(("mf", F_OM + k), 0)])
        stream(5, CH0[J_MEM] + k - 2, [(("xt", F_MEM + 2 * k), 0), (("xt", F_MEM + 2 * k + 1), 0)])
        stream(5, CH0[J_ODOUT] + k // 2 - 2, [(("mf", F_ODD + k), 0)])
        stream(5, CH0[J_ODOUT] + k // 2 + 4, [(("mf", F_ODD + 8 + k), 0)])
        stream(5, CH0[J_ODOUT + 8] + k // 2 - 1, [(("mf", F_ODD + 16 + k), 0)])
    stream(5, CH0[J_MEM] + 6, [(("rstd", 1), 0)])
    for k in range(KT):
        b = k // 4
        stream(5, max(CH0[J_OM + 1 + b] + (1 if b < 3 else 0), CH0[J_ODIN - 1] + (k - 8) // 2 + 1),
               [(("xt", F_H + k), 0)])
    stream(5, CH0[J_ODIN] + 1, [(("rstd", 2), 0)])
    p = 0
    for g in range(4):
        s = [(("sbn", g), 1.5)] + [(("sbT", h), .5) for h in range(4 * g, 4 * g + 4)]
        s += [("at", after(J_ODIN + 4 * g + 3))] + [(("zT", 16 + 4 * g + q), .3) for q in range(4)] + [(("tab", g), 0)]
        slow = 1.3 if g < 3 else .9
        for h in range(4 * g, 4 * g + 4):
            s += [(("sbz", h), slow), (("sbc", h), slow), (("sbo", h), .3)]
        p = stream(6, max(p, after(J_ODIN + 4 * g + 1)), s)
    p = stream(6, max(p, after(J_ODIN + 17)), [(("mqs", 2), 1), (("mqs", 3), 1)] + [(("mqT", dt), .4) for dt in range(8, 16)])
    p = stream(6, max(p, after(J_ODIN + 19)), [(("zT", n), .4) for n in range(32, 40)])
    att = [(("mas", 4), 1)]
    for n in range(4, 8):
        att += [(("mat", n), 1)] + ([(("mas", n + 1), 1)] if n < 7 else []) + [(("mao", 2 * n), .5), (("mao", 2 * n + 1), .5)]
    p = stream(6, p, att)
    for j in range(len(JOBS)):
        stream(-1, CH0[j + 1] + (0 if j in (J_ODIN - 1, len(JOBS) - 1) else 1), [(("evac", j), 0)])

    plan = []
    placed.sort(key=lambda q: q[:3])
    at = 0
    for c in range(NCH):
        while at < len(placed) and placed[at][0] <= c:
            plan.append(placed[at][3])
            at += 1
        plan.append(("chunk", c))
    plan += [q[3] for q in placed[at:]]
    if last_job < len(JOBS):
        stop = plan.index(("evac", last_job - 1)) + 1
        plan = [q for q in plan[:stop] if not (q[0] == "chunk" and q[1] >= CH0[last_job])
                and not (q[0] == "xt" and q[1] >= F_H)]
    return plan


def prog(nc, x, mem, vecs, w, a_log, dt_bias, out, last_job=len(JOBS)):
    plan = make_plan(last_job)
    jobs = JOBS[:last_job]
    nch = CH0[last_job]
    ctx = ExitStack()
    with ctx:
        def sb(name, shape, dt=F32):
            return ctx.enter_context(nc.sbuf_tensor(name, shape, dt))

        def sem(name):
            return ctx.enter_context(nc.semaphore(name))

        raw = sb("raw", [128, RAWS, 2, 512])
        whi = sb("whi", [128, RING, 2, 512], F32R)
        wlo = sb("wlo", [128, RING, 2, 512], F32R)
        xhi = sb("xhi", [128, 16, S], F32R)
        xlo = sb("xlo", [128, 16, S], F32R)
        hid = sb("hid", [128, T, D])
        proj = sb("proj", [128, 4, T, 512])
        reg = sb("reg", [128, 4096])
        cvr = sb("cvr", [128, 10, S])
        mix = sb("mix", [128, 24, S])
        scr = sb("scr", [128, 1024])
        ident = sb("ident", [128, 128])
        ones = sb("ones", [128, 128])
        negones = sb("negones", [128, 128])
        upto = sb("upto", [128, 128])
        negfrom = sb("negfrom", [128, 128])
        after01 = sb("after01", [128, 128])
        shut = sb("shut", [128, 2, 128], BF16)
        identb = sb("identb", [128, 128], BF16)
        vt = sb("vt", [128, NV])
        qgain = sb("qgain", [128, 1])
        rows = sb("rows", [24, 2, 128])
        ssq = sb("ssq", [128, 3, T])
        rstd = sb("rstd", [128, 3, T])
        mhalf = sb("mhalf", [128, 16])
        ba = sb("ba", [128, T, 2 * H_DN])
        alog = sb("alog", [128, H_DN])
        dtb = sb("dtb", [128, H_DN])
        beta = sb("beta", [128, T, H_DN])
        halfb = sb("halfb", [128, T, H_DN])
        lnb = sb("lnb", [128, T, H_DN])
        gu = sb("gu", [128, T, H_DN])
        ge = sb("ge", [128, T, H_DN])
        gl_in = sb("gl_in", [128, T, H_DN])
        gcl = sb("gcl", [128, 2, T, H_DN])
        nrm = sb("nrm", [128, H_DN, 4])
        hln = sb("hln", [128, 2, 4, 4])
        cc = sb("cc", [128, 2, 4, T])
        ei = sb("ei", [128, 2, 4, 8])
        ex = sb("ex", [128, 2, 4, 8])
        nks = sb("nks", [128, 2, 8])
        oss = sb("oss", [128, 2, 8])
        oms = sb("oms", [128, 2, 8])
        ofac = sb("ofac", [128, 2, 8])
        qss = sb("qss", [128, 6, 4])
        qrs = sb("qrs", [128, 6, 4])
        smx = sb("smx", [128, 8, T])
        snb = sb("snb", [128, 8, T])
        ssm = sb("ssm", [128, 8, T])
        srs = sb("srs", [128, 8, T])
        bss = sb("bss", [128, 4, 16])
        brs = sb("brs", [128, 4, 16])

        flat = hid[:, :, :].rearrange("p t d -> p (t d)")
        pflat = proj[:, :, :, :].rearrange("p a t n -> p (a t n)")
        cflat = cvr[:, :, :].rearrange("p a s -> p (a s)")
        mflat = mix[:, :, :].rearrange("p a s -> p (a s)")
        ykqv = reg[:, 0:3072].rearrange("p (h c s) -> p h c s", h=4, c=3)
        ofx = reg[:, 3072:4096].rearrange("p (a m n) -> p a m n", a=2, m=4)
        tok = flat[:, 0:1536].rearrange("p (h c n) -> p h c n", h=4, c=3)
        aq = flat[:, 1536:3584].rearrange("p (m c n) -> p m c n", m=8, c=2)
        dw = flat[:, 3584:4096].rearrange("p (c n) -> p c n", c=4)
        tinv = mflat[:, 12 * S:16 * S].rearrange("p (a m n) -> p a m n", a=2, m=4)
        tinvt = mflat[:, 4 * S:8 * S].rearrange("p (a m n) -> p a m n", a=2, m=4)
        za = mflat[:, 16 * S:24 * S].rearrange("p (t n) -> p t n", t=T)
        level = mflat[:, 8 * S:8 * S + 896].rearrange("p (l n) -> p l n", l=7)
        memx = reg[:, :].rearrange("p (t d) -> p t d", t=T)
        kmt = reg[:, 0:2048].rearrange("p (a s) -> p a s", a=8)
        vm = reg[:, 2048:4096].rearrange("p (t n) -> p t n", t=T)
        qmt = [v[:, 0:2048].rearrange("p (a s) -> p a s", a=8) for v in (pflat, cflat)]
        prob = scr[:, 0:512].rearrange("p (t m) -> p t m", t=T)
        probt = scr[:, 512:1024].rearrange("p (m s) -> p m s", m=2)
        qk = cflat[:, 0:2048].rearrange("p (a c s) -> p a c s", a=4, c=2)
        wts = cflat[:, 2048:2432]
        absz = scr[:, 0:384]
        spz = scr[:, 512:896]
        vrow = pflat[:, 0:512].rearrange("p (a n) -> p a n", a=4)
        wba = reg[:, 0:256].rearrange("p (k n) -> p k n", k=16)
        bah = whi[:, RING - 1, 0, 0:256].rearrange("p (k n) -> p k n", k=16)
        bal = wlo[:, RING - 1, 0, 0:256].rearrange("p (k n) -> p k n", k=16)

        def psum(name):
            return ctx.enter_context(nc.psum_tensor(name, [128, 512], F32))

        pj = [[psum(f"job{a}{t}") for t in range(T)] for a in range(2)]
        M = [psum(f"mixer{i}") for i in range(4)]

        s_vrow = sem("vector_rows_loaded")
        s_small = sem("small_inputs_loaded")
        s_xin = [sem(f"x_columns_loaded{b}") for b in range(4)]
        s_min = sem("mem_loaded")
        s_xre = sem("x_loaded_again")
        s_raw = [sem(f"raw_chunk_loaded{i}") for i in range(RAWS)]
        s_out = sem("output_stored")
        s_hi = sem("chunk_high_parts")
        s_lo = sem("chunk_remainders")
        s_pe = sem("chunks_multiplied")
        s_evA = sem("job_results_copied")
        s_evD = sem("job_results_added")
        s_xp = sem("rows_transposed")
        s_xh = sem("fill_high_parts")
        s_xl = sem("fill_remainders")
        s_const = sem("constants_made")
        s_vp = sem("vectors_transposed")
        s_vt = sem("vectors_copied")
        s_ss = sem("row_squares_summed")
        s_ms = sem("row_mean_squares")
        s_rstd = sem("row_rstd")
        s_wbh = sem("ba_weights_high")
        s_wbl = sem("ba_weights_low")
        s_bap = sem("ba_multiplied")
        s_ba = sem("ba_copied")
        s_baA = sem("ba_scalar_steps")
        s_baD = sem("ba_vector_steps")
        s_gcp = sem("decays_summed")
        s_gc = sem("decays_copied")
        s_zat = sem("za_tanh")
        s_za = sem("za_gates")
        s_dnT = sem("dn_qkv_transposed")
        s_cv4 = sem("dn_conv_ops")
        s_th = sem("dn_tanh")
        s_silu = sem("dn_silu")
        s_sq = sem("dn_squares")
        s_back = sem("dn_kv_transposed_back")
        s_tok = sem("dn_kv_by_token")
        s_np = sem("dn_norms_summed")
        s_nrm = sem("dn_norms_copied")
        s_lnq = sem("dn_log_norms")
        s_ei = sem("dn_exponents")
        s_ex = sem("dn_factors")
        s_rp = sem("dn_rows_transposed")
        s_rows = sem("dn_rows_copied")
        s_tks = sem("dn_kv_scaled")
        s_gp = sem("dn_products")
        s_eq = sem("dn_decays")
        s_aq = sem("dn_matrices")
        s_of = [sem(f"inv_masked{i}") for i in range(2)]
        s_x1p = [sem(f"inv_first_product{i}") for i in range(2)]
        s_x1 = [sem(f"inv_first_copied{i}") for i in range(2)]
        s_x2p = [sem(f"inv_second_products{i}") for i in range(2)]
        s_t = [sem(f"inv_updated{i}") for i in range(2)]
        s_5ap = sem("dn_v0_product")
        s_5a = sem("dn_v0_copied")
        s_5bp = sem("dn_state_products")
        s_5b = sem("dn_state_copied")
        s_5cp = sem("dn_state_read")
        s_5cA = sem("dn_q_state_copied")
        s_5c = sem("dn_second_rhs")
        s_5dp = sem("dn_v1_product")
        s_5d = sem("dn_v1_copied")
        s_5ep = sem("dn_o1_product")
        s_5e = sem("dn_o1_added")
        s_oss = sem("dn_out_squares")
        s_oms = sem("dn_out_mean_squares")
        s_opw = sem("dn_out_rstd")
        s_of6 = sem("dn_out_factors")
        s_ow = sem("dn_out_gated")
        s_owp = sem("dn_out_transposed")
        s_mixa = sem("dn_out_stored")
        s_glt = sem("glu_tanh")
        s_glu = sem("glu_products")
        s_gtp = sem("glu_transposed")
        s_gt = sem("glu_stored")
        s_cv = sem("conv_taps")
        s_mup = sem("ln_sum")
        s_mu = sem("ln_mean")
        s_xc = sem("ln_centred")
        s_lsq = sem("ln_squares")
        s_lvp = sem("ln_square_sums")
        s_var = sem("ln_variance")
        s_std = sem("ln_std")
        s_xn = sem("ln_normalised")
        s_ly = sem("ln_affine")
        s_lt = sem("ln_tanh")
        s_mixb = sem("conv_out_stored")
        s_zp = sem("gates_transposed")
        s_zc = sem("gates_tanh")
        s_z = sem("gates_stored")
        s_mqs = sem("mq_squares")
        s_mqm = sem("mq_mean_squares")
        s_mqr = sem("mq_rstd")
        s_mqk = sem("mq_scales")
        s_mks = sem("mk_scaled")
        s_mqp = sem("mq_transposed")
        s_mqT = sem("mq_stored")
        s_mkp = sem("mk_transposed")
        s_mkT = sem("mk_stored")
        s_scp = sem("mem_scores")
        s_nb = sem("mem_score_maxima")
        s_exp = sem("mem_exps")
        s_pr = sem("mem_probs")
        s_ptp = sem("mem_probs_transposed")
        s_pt = sem("mem_probs_stored")
        s_maop = sem("mem_out_products")
        s_mao = sem("mem_out_stored")
        s_sbs = sem("sb_squares")
        s_sbr = sem("sb_square_sums")
        s_sbm = sem("sb_mean_squares")
        s_sbw = sem("sb_rstd")
        s_sbn = sem("sb_normalised")
        s_sbtp = sem("sb_qk_transposed")
        s_sbT = sem("sb_qk_stored")
        s_sbzp = sem("sb_scores")
        s_sbA = sem("sb_log_terms")
        s_sbsp = sem("sb_softplus")
        s_sbmk = sem("sb_softplus_masked")
        s_sbcp = sem("sb_sums")
        s_sbW = sem("sb_weights")
        s_sbop = sem("sb_out_products")
        s_sbo = sem("sb_out_stored")
        s_actq = sem("scalar_own_steps")
        s_dveq = sem("vector_own_steps")
        s_poolq = sem("gpsimd_own_steps")

        def evac_done(j):
            if j in ADDED:
                return s_evD, ADDED.index(j) + 1
            return s_evA, COPIED.index(j) + 1

        def banks(step, i):
            if step == "xt":
                return [i % 4] if i < 16 else [2 + i % 2]
            if step in ("mqT", "mkT"):
                return [i % 2]
            if step == "d4y":
                return [] if i % 7 == 0 else ([1, 2] if i % 7 < 6 else [2])
            if step == "lnv":
                return [3] if i == 0 else []
            return {"vec": [0], "ba": [0, 1], "dnT": [0, 1], "dnB": [2], "dnV": [1], "dnG": [0, 1], "d4x": [0],
                    "d5a": [0], "d5b": [1], "d5c": [2], "d5d": [0], "d5e": [1], "d7": [2], "gT": [3], "zT": [3],
                    "lnm": [3], "mas": [0], "mat": [1], "mao": [2], "sbT": [0], "sbz": [1], "sbo": [2]}.get(step, [])

        def inv_count(i):
            return 7 * (i // 14) + i % 7 + 1

        def read(step, i):
            par = (i // 7) % 2
            return {"vec": (s_vt, 1), "xt": (s_xl, i + 1), "ba": (s_gc, 1), "dnT": (s_silu, 2 * i + 2),
                    "dnB": (s_nrm, i + 1), "dnV": (s_rows, i + 1), "dnG": (s_aq, i + 1),
                    "d4x": (s_t[par], inv_count(i)) if i % 7 == 0 else (s_x1[par], 6 * (i // 14) + i % 7),
                    "d4y": (s_t[par], inv_count(i)), "d5a": (s_5a, i + 1), "d5b": (s_5b, i + 1),
                    "d5c": (s_5c, i + 1), "d5d": (s_5d, i + 1), "d5e": (s_5e, i + 1), "d7": (s_mixa, i + 1),
                    "gT": (s_gt, i + 1), "zT": (s_z, i + 1), "lnm": (s_mu, 1), "lnv": (s_var, 1),
                    "mqT": (s_mqT, i + 1), "mkT": (s_mkT, i + 1), "mas": (s_exp, i + 1), "mat": (s_pt, i + 1),
                    "mao": (s_mao, i + 1), "sbT": (s_sbT, i + 1), "sbz": (s_sbW, i + 1),
                    "sbo": (s_sbo, i + 1)}[step]

        last_user, bank_free = {}, {}
        for st, i in [("vec", 0)] + plan:
            bank_free[st, i] = [read(*last_user[b]) for b in banks(st, i) if b in last_user]
            for b in banks(st, i):
                last_user[b] = (st, i)

        def slot_jobs(j):
            before = [q for q in PSLOT if q < j and PSLOT[q] == PSLOT[j]]
            if not before:
                return [(s_ss, 1), (s_vp, 1)]
            q = max(before)
            for g in range(2):
                if q == J_GLU[g]:
                    return [(s_gtp, 4 * g + 4)]
                if q == J_GLU[g] + 1:
                    return [(s_glu, g + 1)]
                if q in (J_Q[g], J_K[g], J_V[g]):
                    return [(s_dnT, 4 * g + 4)]
                if q == J_ZA[g]:
                    return [(s_za, g + 1)]
            if q < J_QM:
                return [(s_zp, 4 * (q - J_ZB) + 4)]
            if q < J_ZM:
                return [(s_mqp, 4 * (q - J_QM) + 4), (s_ss, 3)]
            if q < J_OA:
                return [(s_zp, 8 + 4 * (q - J_ZM) + 4), (s_ss, 2)]
            if q < J_ODIN:
                return [(s_mkp, 4 * (q - J_MEM) + 4), (s_scp, 4), (s_ss, 3)]
            g, c = divmod(q - J_ODIN, 4)
            if q >= J_ODIN + 16:
                return []
            return [[(s_sbtp, 4 * g + 4)], [(s_sbtp, 4 * g + 4)], [(s_sbop, 4 * g + 4)], [(s_zp, 16 + 4 * g + 4)]][c]

        def zsource(n):
            if n < 8:
                return J_ZB + n // 4, n // 4, n % 4, 8 + n
            if n < 16:
                return J_ZM + (n - 8) // 4, (n - 8) // 4, n % 4, 16 + n - 8
            if n < 32:
                return J_ODIN + 4 * ((n - 16) // 4) + 3, 3, n % 4, n - 16
            return J_ODIN + 18 + (n - 32) // 4, 2 + (n - 32) // 4, n % 4, 16 + n - 32

        def gain(name, c):
            return vt[:, VCOL[name] + c:VCOL[name] + c + 1]

        def xt_gain(n):
            return (gain("ev_norm_g", n) if n < F_OA else gain("mem_norm_g", n - F_MEM) if n < F_OB
                    else gain("od_norm_g", n - F_H))

        def turned(n):
            return n + 1 if n < F_OA else n - F_MEM + 17 if n < F_OB else n - F_H + 33

        def mix_tile(n):
            return n - F_OA if n < F_MEM else n - F_OB + 8 if n < F_H else n - F_ODD


        def mix_ready(n):
            kt, odd = mix_tile(n), n >= F_H
            if odd and kt < 16:
                return s_sbo, kt + 1
            if kt < 8:
                return s_mixa, kt + 1
            if kt < 16:
                return s_mixb, kt - 7
            return s_mao, 8 * odd + kt - 15

        def halves(m, par, l):
            return m[:, par, :, :].rearrange("p m n -> p (m n)").rearrange("p (b c r) -> p b c r", c=2, r=1 << l)

        mm = nc.tensor.matmul
        act = nc.scalar.activation
        vec = nc.vector
        MQJOB = [J_QM, J_QM + 1, J_ODIN + 16, J_ODIN + 17, J_MEM, J_MEM + 1]
        MQSLOT = [2, 3, 0, 1, 0, 1]
        order = {4: 1, 5: 2, 0: 3, 1: 4, 2: 5, 3: 6}

        block = ctx.enter_context(nc.Block())

        @block.sync
        def _(sp):
            for b in range(4):
                sp.dma_start(hid[:, :, 512 * b:512 * b + 512],
                             x[:, 512 * b:512 * b + 512].rearrange("(t p) d -> p t d", p=128)).then_inc(s_xin[b], 16)
            for c in range(nch):
                j = JOB_OF[c]
                name, r0, c0, _, _ = JOBS[j]
                r = r0 + 256 * (c - CH0[j])
                if c >= RAWS:
                    sp.wait_ge(s_lo, c - RAWS + 1)
                sp.dma_start(raw[:, c % RAWS, :, :], w[name][r:r + 256, c0:c0 + 512].rearrange("(k p) n -> p k n", p=128)
                             ).then_inc(s_raw[c % RAWS], 16)
            stores = 0
            for b in range(4):
                j = last_job - 4 + b
                sp.wait_ge(*evac_done(j))
                sp.dma_start(out[:, 512 * b:512 * b + 512].rearrange("(t p) d -> p t d", p=128),
                             hid[:, :, 512 * b:512 * b + 512]).then_inc(s_out, 16)
                stores += 16
            sp.wait_ge(s_out, stores)

        @block.gpsimd
        def _(gp):
            own = [0]

            def link(ins):
                own[0] += 1
                ins.then_inc(s_poolq, 1)
                gp.wait_ge(s_poolq, own[0])

            def keep(t, pattern, base, mult, op, fill):
                link(nc.gpsimd.affine_select(out=t, in_=t, compare_op=op, fill=fill, base=base,
                                             pattern=pattern, channel_multiplier=mult))

            link(nc.gpsimd.memset(ident[:, :], 0.0))
            nc.gpsimd.affine_select(out=ident[:, :], in_=ident[:, :], compare_op=ALU.not_equal, fill=1.0, base=0,
                                    pattern=[[-1, 128]], channel_multiplier=1).then_inc(s_const, 1)
            for t, v in ((identb, 0.0), (ones, 1.0), (negones, -1.0), (upto, 1.0), (negfrom, -1.0), (after01, 1.0),
                         (mhalf, -0.5)):
                link(nc.gpsimd.memset(t[:, :], v))
            link(nc.gpsimd.memset(shut[:, :, :], 0.0))
            link(nc.gpsimd.memset(level, 0.0))
            keep(identb[:, :], [[-1, 128]], 0, 1, ALU.not_equal, 1.0)
            keep(upto[:, :], [[1, 128]], 0, -1, ALU.is_ge, 0.0)
            keep(negfrom[:, :], [[-1, 128]], 0, 1, ALU.is_ge, 0.0)
            keep(shut[:, 0, :], [[1, 128]], 0, -1, ALU.is_gt, NEG)
            keep(shut[:, 1, :], [[1, 128]], 0, -1, ALU.is_ge, NEG)
            for l in range(7):
                h = 1 << l
                nb = 64 // h
                v = level[:, l, :].rearrange("p (b c r) -> p b c r", b=nb, c=2)[:, :, 1, :]
                link(nc.gpsimd.memset(v, 1.0))
                keep(v, [[-2 * h, nb], [0, h]], 0, 1, ALU.is_ge, 0.0)
                keep(v, [[2 * h, nb], [0, h]], h - 1, -1, ALU.is_ge, 0.0)
            nc.gpsimd.affine_select(out=after01[:, :], in_=after01[:, :], compare_op=ALU.is_gt, fill=0.0, base=0,
                                    pattern=[[1, 128]], channel_multiplier=-1).then_inc(s_const, 1)
            gp.wait_ge(s_const, 2)

            def power(out_, in_, n, done):
                nc.gpsimd.tensor_tensor(out_, in_, mhalf[:, 0:n], ALU.pow).then_inc(done, 1)

            def do_rstd(src):
                gp.wait_ge(s_ms, src + 1)
                power(rstd[:, src, :], ssq[:, src, :], T, s_rstd)

            def do_dnB(h):
                gp.wait_ge(s_silu, 2 * h + 2)
                if h:
                    gp.wait_ge(s_np, h)
                k = ykqv[:, h % 4, 0:2, :]
                nc.gpsimd.tensor_tensor(scr[:, 0:512].rearrange("p (c s) -> p c s", c=2), k, k, ALU.mult).then_inc(s_sq, 1)

            def do_dnG(h):
                g, hl = h // 4, h % 4
                gp.wait_ge(s_tok, h + 1)
                gp.wait_ge(s_ex, g + 1)
                gp.wait_ge(s_baD, 2)
                for c, f in ((0, ex[:, g, 1, 2 * hl:2 * hl + 1]), (1, halfb[:, 0, h:h + 1]), (2, halfb[:, 1, h:h + 1])):
                    ins = nc.gpsimd.tensor_scalar(tok[:, hl, c, :], tok[:, hl, c, :], f, 1.0, ALU.mult, ALU.mult)
                ins.then_inc(s_tks, 1)

            def do_d4x(i):
                pr, l = divmod(i, 7)
                g, par = divmod(pr, 2)
                if l == 0:
                    gp.wait_ge(s_aq, 4 * g + 2 * par + 2)
                    if g:
                        gp.wait_ge(s_5dp, 4 * (g - 1) + 2 * par + 2)
                else:
                    gp.wait_ge(s_t[par], 7 * g + l)
                nc.gpsimd.tensor_tensor(ofx[:, par, :, :], aq[:, 4 * par:4 * par + 4, 0, :],
                                        level[:, l, :].unsqueeze(1).broadcast_to([128, 4, 128]), ALU.mult
                                        ).then_inc(s_of[par], 1)

            def do_d6(g):
                gp.wait_ge(s_oms, g + 1)
                power(oms[:, g, :], oms[:, g, :], 8, s_opw)

            def mq_power(i, n):
                gp.wait_ge(s_mqm, n)
                power(qss[:, i, :], qss[:, i, :], 4, s_mqr)

            def do_sbn(g):
                gp.wait_ge(s_sbm, g + 1)
                power(brs[:, g, :], bss[:, g, :], 16, s_sbw)
                gp.wait_ge(s_sbw, g + 1)
                for c in range(2):
                    v = pflat[:, 1024 * c:1024 * c + 1024].rearrange("p (a n) -> p a n", n=128)
                    nc.gpsimd.tensor_tensor(v, v, brs[:, g, 8 * c:8 * c + 8].unsqueeze(2).broadcast_to([128, 8, 128]),
                                            ALU.mult).then_inc(s_sbn, 1)

            def do_sbz(h):
                gp.wait_ge(s_sbsp, h + 1)
                v = spz.rearrange("p (a n) -> p a n", a=3)[:, 0:3:2, :]
                nc.gpsimd.tensor_tensor(v, v, after01[:, :].unsqueeze(1).broadcast_to([128, 2, 128]), ALU.mult
                                        ).then_inc(s_sbmk, 1)

            steps = {"rstd": do_rstd, "dnB": do_dnB, "dnG": do_dnG, "d4x": do_d4x, "d6": do_d6, "sbn": do_sbn,
                     "sbz": do_sbz, "mqs": lambda i: mq_power(i, order[i]), "mks": lambda i: mq_power(4 + i, order[4 + i])}
            for st, i in plan:
                if st in steps:
                    steps[st](i)

        @block.scalar
        def _(sc):
            own = [0]

            def link(ins):
                own[0] += 1
                ins.then_inc(s_actq, 1)
                sc.wait_ge(s_actq, own[0])

            def split(c):
                sc.wait_ge(s_raw[c % RAWS], 16 * (c // RAWS + 1))
                if c >= RING:
                    sc.wait_ge(s_pe, c - RING + 1)
                if c == 2 * RING - 1:
                    sc.wait_ge(s_bap, 1)
                act(whi[:, c % RING, :, :], raw[:, c % RAWS, :, :], ACT.Copy).then_inc(s_hi, 1)

            def do_chunk(c):
                if c + AHEAD < nch:
                    split(c + AHEAD)

            def do_evac(j):
                if j in ADDED:
                    return
                src = 0 if j < J_OA else 1 if j < J_OB else 2
                sc.wait_ge(s_rstd, src + 1)
                sc.wait_ge(s_pe, CH0[j + 1])
                if j in PSLOT:
                    for q in slot_jobs(j):
                        sc.wait_ge(*q)
                else:
                    sc.wait_ge(s_ss, 2)
                for t in range(T):
                    if j in PSLOT:
                        dst = proj[:, PSLOT[j], t, :]
                    else:
                        dst = vm[:, t, 512 * (j - J_MEM - 2):512 * (j - J_MEM - 2) + 512]
                    ins = act(dst, pj[j % 2][t][:, :], ACT.Copy, scale=rstd[:, src, t:t + 1])
                ins.then_inc(evac_done(j)[0], 1)

            def fill_wait(n):
                if chunks_before_fill(n):
                    sc.wait_ge(s_pe, chunks_before_fill(n))

            def do_xt(n):
                sc.wait_ge(s_xp, turned(n))
                fill_wait(n)
                act(xhi[:, SLOT[n], :], M[banks("xt", n)[0]][:, 0:S], ACT.Copy, scale=xt_gain(n)).then_inc(s_xh, 1)

            def do_mf(n):
                sc.wait_ge(*mix_ready(n))
                fill_wait(n)
                act(xhi[:, SLOT[n], :], mix[:, mix_tile(n), :], ACT.Copy).then_inc(s_xh, 1)

            def do_rstd(src):
                if src == 0:
                    for b in range(4):
                        sc.wait_ge(s_xin[b], 16)
                elif src == 1:
                    sc.wait_ge(s_min, 16)
                    sc.wait_ge(s_zp, 16)
                else:
                    sc.wait_ge(*evac_done(J_ODIN - 1))
                    sc.wait_ge(s_scp, 4)
                o = 0 if src == 1 else 2048
                link(act(pflat[:, 0:2048], (memx if src == 1 else hid)[:, 0, :], ACT.Square, accum_out=ssq[:, src, 0:1]))
                ins = act(pflat[:, o:o + 2048], (memx if src == 1 else hid)[:, 1, :], ACT.Square, accum_out=ssq[:, src, 1:2])
                ins.then_inc(s_ss, 1)

            def do_ba(_):
                sc.wait_ge(s_small, 48)
                sc.wait_ge(s_pe, RING)
                act(bah, wba, ACT.Copy).then_inc(s_wbh, 1)
                sc.wait_ge(s_bap, 1)
                sc.wait_ge(s_rstd, 1)
                for t in range(T):
                    ins = act(ba[:, t, :], M[0][:, 16 * t:16 * t + 16], ACT.Copy, scale=rstd[:, 0, t:t + 1])
                ins.then_inc(s_ba, 1)
                sc.wait_ge(s_ba, 1)
                act(beta[:, :, :], ba[:, :, 0:H_DN], ACT.Tanh, scale=0.5).then_inc(s_baA, 1)
                link(act(alog[:, :], alog[:, :], ACT.Exp))
                sc.wait_ge(s_baD, 1)
                link(act(ge[:, :, :], gu[:, :, :], ACT.Abs))
                link(act(ge[:, :, :], ge[:, :, :], ACT.Exp, scale=-1.0))
                sc.wait_ge(s_baD, 2)
                act(ge[:, :, :], ge[:, :, :], ACT.Ln, bias=1.0)
                act(lnb[:, :, :], beta[:, :, :], ACT.Ln).then_inc(s_baA, 1)

            def do_za(g):
                sc.wait_ge(*evac_done(J_ZA[g]))
                act(za[:, :, 512 * g:512 * g + 512], proj[:, PSLOT[J_ZA[g]], :, :], ACT.Tanh, scale=0.5).then_inc(s_zat, 1)

            def do_dnC(h):
                sc.wait_ge(s_cv4, 12 * h + 12)
                y = ykqv[:, h % 4, :, :]
                act(M[0][:, :].rearrange("p (c s) -> p c s", c=2), y[:, 0:2, :], ACT.Tanh, scale=0.5)
                act(M[1][:, 0:S], y[:, 2, :], ACT.Tanh, scale=0.5).then_inc(s_th, 1)

            def do_dnB(h):
                sc.wait_ge(s_back, h + 1)
                if h >= 4:
                    sc.wait_ge(s_owp, h - 3)
                sc.wait_ge(s_ss, 1)
                act(tok[:, h % 4, :, :], M[2][:, 0:384].rearrange("p (c n) -> p c n", c=3), ACT.Copy).then_inc(s_tok, 1)

            def do_dnV(g):
                sc.wait_ge(s_lnq, 2 * g + 1)
                act(hln[:, g, :, :], hln[:, g, :, :], ACT.Ln).then_inc(s_lnq, 1)
                sc.wait_ge(s_ei, g + 1)
                act(ex[:, g, :, :], ei[:, g, :, :], ACT.Exp).then_inc(s_ex, 1)

            def do_dnG(h):
                g, hl = h // 4, h % 4
                sc.wait_ge(s_gp, h + 1)
                if h >= 4:
                    sc.wait_ge(s_5ep, h - 3)
                for t in range(T):
                    ins = act(aq[:, 2 * hl + t, :, :], M[1][:, 256 * t:256 * t + 256].rearrange("p (c n) -> p c n", c=2),
                              ACT.Exp, bias=cc[:, g, hl, t:t + 1])
                ins.then_inc(s_eq, 1)

            def do_d4x(i):
                pr, l = divmod(i, 7)
                g, par = divmod(pr, 2)
                if l:
                    sc.wait_ge(s_x1p[par], 7 * g + l + 1)
                    act(ofx[:, par, :, :], M[0][:, :].rearrange("p (m n) -> p m n", m=4), ACT.Copy).then_inc(s_x1[par], 1)

            def do_d5a(h):
                sc.wait_ge(s_5ap, h + 1)
                act(dw[:, 0, :], M[0][:, 0:128], ACT.Copy).then_inc(s_5a, 1)

            def do_d5b(h):
                sc.wait_ge(s_5bp, h + 1)
                if h:
                    sc.wait_ge(s_oss, h)
                act(dw[:, 1, :], M[1][:, 0:128], ACT.Copy)
                act(tok[:, h % 4, 0, :], M[1][:, 128:256], ACT.Copy).then_inc(s_5b, 1)

            def do_d5c(h):
                g, hl = h // 4, h % 4
                sc.wait_ge(s_5cp, h + 1)
                if h:
                    sc.wait_ge(s_5e, h)
                act(dw[:, 3, :], M[2][:, 128:256], ACT.Copy, scale=ex[:, g, 2, 2 * hl + 1:2 * hl + 2]).then_inc(s_5cA, 1)

            def do_d5d(h):
                sc.wait_ge(s_5dp, h + 1)
                act(dw[:, 2, :], M[0][:, 0:128], ACT.Copy).then_inc(s_5d, 1)

            def do_d5e(h):
                g, hl = h // 4, h % 4
                sc.wait_ge(s_5e, h + 1)
                for t in range(T):
                    ins = act(dw[:, 1 + t, :], tok[:, hl, t, :], ACT.Square, accum_out=oss[:, g, 2 * hl + t:2 * hl + t + 1])
                ins.then_inc(s_oss, 1)

            def do_d7(h):
                sc.wait_ge(s_owp, h + 1)
                act(mix[:, h, :], M[2][:, 0:S], ACT.Copy, scale=gain("ev_dn_norm_g", 0)).then_inc(s_mixa, 1)

            def do_glu(i):
                sc.wait_ge(*evac_done(J_GLU[i] + 1))
                act(proj[:, 2 * i + 1, :, :], proj[:, 2 * i + 1, :, :], ACT.Tanh, scale=0.5).then_inc(s_glt, 1)

            def do_gT(ct):
                sc.wait_ge(s_gtp, ct + 1)
                act(cvr[:, ct + 2, :], M[3][:, 0:S], ACT.Copy, scale=0.5).then_inc(s_gt, 1)

            def do_lnm(_):
                sc.wait_ge(s_mup, 1)
                act(scr[:, 0:S], M[3][:, 0:S], ACT.Copy, scale=1.0 / CVW).then_inc(s_mu, 1)

            def do_lnv(ct):
                sc.wait_ge(s_xc, 1)
                if ct >= 2:
                    sc.wait_ge(s_lvp, ct - 1)
                act(cvr[:, 8 + ct % 2, :], cvr[:, ct, :], ACT.Square).then_inc(s_lsq, 1)

            def do_lnr(_):
                sc.wait_ge(s_var, 1)
                act(scr[:, S:2 * S], scr[:, S:2 * S], ACT.Sqrt).then_inc(s_std, 1)

            def do_lno(ct):
                sc.wait_ge(s_ly, ct + 1)
                if ct >= 2:
                    sc.wait_ge(s_mixb, ct - 1)
                act(cvr[:, 8 + ct % 2, :], cvr[:, ct, :], ACT.Tanh, scale=0.5).then_inc(s_lt, 1)

            def do_zT(n):
                kt = zsource(n)[3]
                sc.wait_ge(s_zp, n + 1)
                if n < 8:
                    sc.wait_ge(s_t[0], 14)
                    sc.wait_ge(s_t[1], 14)
                elif n < 16:
                    sc.wait_ge(s_ow, 16)
                elif n == 16:
                    sc.wait_ge(s_xl, F_OM)
                elif n == 32:
                    sc.wait_ge(s_xl, F_H)
                act(mix[:, kt, :], M[3][:, 0:S], ACT.Copy)
                act(M[3][:, S:2 * S], M[3][:, 0:S], ACT.Tanh, scale=0.5).then_inc(s_zc, 1)

            def squares(i):
                sc.wait_ge(*evac_done(MQJOB[i]))
                if i == 2:
                    sc.wait_ge(s_sbcp, 16)
                if order[i] == 1:
                    sc.wait_ge(s_xn, 1)
                else:
                    sc.wait_ge(s_mqs, order[i] - 1)
                for t in range(T):
                    for hd in range(2):
                        ins = act(scr[:, 256 * (2 * t + hd):256 * (2 * t + hd) + 256],
                                  proj[:, MQSLOT[i], t, 256 * hd:256 * hd + 256], ACT.Square,
                                  accum_out=qss[:, i, 2 * t + hd:2 * t + hd + 1])
                ins.then_inc(s_mqs, 1)

            def do_mqT(dt):
                sc.wait_ge(s_mqp, dt + 1)
                sc.wait_ge(*((s_mkp, 8) if dt < 8 else (s_sbzp, 16)))
                act(qmt[dt // 8][:, dt % 8, :], M[dt % 2][:, 0:S], ACT.Copy,
                    scale=gain("ev_q_norm_m" if dt < 8 else "od_q_norm_m", dt % 2)).then_inc(s_mqT, 1)

            def do_mkT(dt):
                sc.wait_ge(s_mkp, dt + 1)
                sc.wait_ge(s_ss, 2)
                act(kmt[:, dt, :], M[dt % 2][:, 0:S], ACT.Copy, scale=gain("mem_k_norm_g", dt % 2)).then_inc(s_mkT, 1)

            def do_mas(n):
                i, hd2 = 2 * (n // 4) + (n % 4) // 2, n % 2
                sc.wait_ge(s_nb, n + 1)
                if n:
                    sc.wait_ge(s_ptp, n)
                for t in range(T):
                    ins = act(prob[:, t, :], M[0][:, 256 * t:256 * t + 256], ACT.Exp, bias=snb[:, n, t:t + 1],
                              scale=qrs[:, i, 2 * t + hd2:2 * t + hd2 + 1], accum_out=ssm[:, n, t:t + 1])
                ins.then_inc(s_exp, 1)

            def do_mat(n):
                sc.wait_ge(s_ptp, n + 1)
                if n:
                    sc.wait_ge(s_maop, 2 * n)
                act(probt, M[1][:, :].rearrange("p (m s) -> p m s", m=2), ACT.Copy).then_inc(s_pt, 1)

            def do_sbn(g):
                for c in range(2):
                    sc.wait_ge(*evac_done(J_ODIN + 4 * g + c))
                    if 2 * g + c:
                        sc.wait_ge(s_sbr, 2 * g + c)
                    else:
                        sc.wait_ge(s_maop, 8)
                    if g:
                        sc.wait_ge(s_sbcp, 4 * g)
                    act(scr[:, :], pflat[:, 1024 * c:1024 * c + 1024], ACT.Square).then_inc(s_sbs, 1)

            def do_tab(_):
                sc.preload_act_table_set("natural_log_exp_and_others")

            def do_sbT(h):
                sc.wait_ge(s_sbtp, h + 1)
                if h >= 4:
                    sc.wait_ge(s_sbzp, h - 3)
                else:
                    sc.wait_ge(s_mixb, 8)
                act(qk[:, h % 4, 0, :], M[0][:, 0:S], ACT.Copy, scale=qgain[:, 0:1])
                act(qk[:, h % 4, 1, :], M[0][:, S:2 * S], ACT.Copy, scale=gain("od_k_norm_c", 0)).then_inc(s_sbT, 1)

            def do_sbz(h):
                sc.wait_ge(s_sbzp, h + 1)
                sc.wait_ge(s_sbr, 2 * (h // 4) + 2)
                if h:
                    sc.wait_ge(s_sbsp, h)
                link(act(absz, M[1][:, 0:384], ACT.Abs))
                link(act(absz, absz, ACT.Exp, scale=-1.0))
                act(absz, absz, ACT.Ln, bias=1.0).then_inc(s_sbA, 1)

            def do_sbc(h):
                sc.wait_ge(s_sbcp, h + 1)
                if h:
                    sc.wait_ge(s_sbop, h)
                act(wts, M[1][:, 0:384], ACT.Exp).then_inc(s_sbW, 1)

            def do_mload(_):
                sc.wait_ge(s_5cp, 8)
                sc.wait_ge(s_5dp, 8)
                sc.dma_start(memx, mem.rearrange("(t p) d -> p t d", p=128)).then_inc(s_min, 16)

            def do_xload(_):
                sc.wait_ge(s_mixa, 8)
                sc.dma_start(hid[:, :, :], x.rearrange("(t p) d -> p t d", p=128)).then_inc(s_xre, 16)

            steps = {"chunk": do_chunk, "evac": do_evac, "xt": do_xt, "mf": do_mf, "rstd": do_rstd, "ba": do_ba,
                     "za": do_za, "dnC": do_dnC, "dnB": do_dnB, "dnV": do_dnV, "dnG": do_dnG, "d4x": do_d4x,
                     "d5a": do_d5a, "d5b": do_d5b, "d5c": do_d5c, "d5d": do_d5d, "d5e": do_d5e, "d7": do_d7,
                     "glu": do_glu, "gT": do_gT, "lnm": do_lnm, "lnv": do_lnv, "lnr": do_lnr, "lno": do_lno,
                     "zT": do_zT, "mqs": squares, "mks": lambda i: squares(4 + i), "mqT": do_mqT, "mkT": do_mkT,
                     "mas": do_mas, "mat": do_mat, "sbn": do_sbn, "tab": do_tab, "sbT": do_sbT, "sbz": do_sbz,
                     "sbc": do_sbc, "mload": do_mload, "xload": do_xload}
            for dst, src in vecs(vrow):
                sc.dma_start(dst, src).then_inc(s_vrow, 16)
            sc.dma_start(wba, w["ev_in"][:, BA0:BA0 + 16].rearrange("(k p) n -> p k n", p=128),
                         allow_slow_non_contiguous=True).then_inc(s_small, 16)
            sc.dma_start(alog[:, :], a_log.partition_broadcast(128)).then_inc(s_small, 16)
            sc.dma_start(dtb[:, :], dt_bias.partition_broadcast(128)).then_inc(s_small, 16)
            sc.wait_ge(s_vp, 1)
            for a, n in enumerate((NVEC, 96, 128, 120)):
                ins = act(vt[:, 128 * a:128 * a + n], M[0][:, 128 * a:128 * a + n], ACT.Copy)
            ins.then_inc(s_vt, 1)
            sc.wait_ge(s_vt, 1)
            act(qgain[:, :], gain("od_q_norm_c", 0), ACT.Copy, scale=128.0 ** -0.5)
            for c in range(AHEAD):
                split(c)
            for st, i in plan:
                if st in steps:
                    steps[st](i)

        @block.vector
        def _(ve):
            own = [0]

            def link(ins):
                own[0] += 1
                ins.then_inc(s_dveq, 1)
                ve.wait_ge(s_dveq, own[0])

            def split(c):
                ve.wait_ge(s_hi, c + 1)
                vec.tensor_tensor(wlo[:, c % RING, :, :], raw[:, c % RAWS, :, :], whi[:, c % RING, :, :].bitcast(F32),
                                  ALU.subtract).then_inc(s_lo, 1)

            def do_chunk(c):
                if c + AHEAD < nch:
                    split(c + AHEAD)

            def do_evac(j):
                if j in COPIED:
                    return
                b = JOBS[j][2] // 512
                ve.wait_ge(s_pe, CH0[j + 1])
                ve.wait_ge(s_xre, 16)
                if evac_done(j)[1] > 1:
                    ve.wait_ge(s_evD, evac_done(j)[1] - 1)
                if j == J_ODOUT:
                    ve.wait_ge(s_xp, turned(F_H + KT - 1))
                    ve.wait_ge(s_ss, 3)
                for t in range(T):
                    v = hid[:, t, 512 * b:512 * b + 512]
                    ins = vec.tensor_tensor(v, v, pj[j % 2][t][:, :], ALU.add)
                ins.then_inc(s_evD, 1)

            def do_xt(n):
                ve.wait_ge(s_xh, n + 1)
                vec.scalar_tensor_tensor(out=xlo[:, SLOT[n], :], in0=M[banks("xt", n)[0]][:, 0:S], scalar=xt_gain(n),
                                         in1=xhi[:, SLOT[n], :].bitcast(F32), op0=ALU.mult, op1=ALU.subtract
                                         ).then_inc(s_xl, 1)

            def do_mf(n):
                ve.wait_ge(s_xh, n + 1)
                vec.tensor_tensor(xlo[:, SLOT[n], :], mix[:, mix_tile(n), :],
                                  xhi[:, SLOT[n], :].bitcast(F32), ALU.subtract).then_inc(s_xl, 1)

            def do_rstd(src):
                ve.wait_ge(s_ss, src + 1)
                vec.tensor_scalar(ssq[:, src, :], ssq[:, src, :], 1.0 / D, EPS, ALU.mult, ALU.add).then_inc(s_ms, 1)

            def do_ba(_):
                ve.wait_ge(s_wbh, 1)
                vec.tensor_tensor(bal, wba, bah.bitcast(F32), ALU.subtract).then_inc(s_wbl, 1)
                ve.wait_ge(s_ba, 1)
                ve.wait_ge(s_small, 48)
                vec.tensor_tensor(gu[:, :, :], ba[:, :, H_DN:2 * H_DN],
                                  dtb[:, :].unsqueeze(1).broadcast_to([128, T, H_DN]), ALU.add).then_inc(s_baD, 1)
                ve.wait_ge(s_baA, 1)
                link(vec.tensor_scalar(beta[:, :, :], beta[:, :, :], 0.5, 0.5, ALU.mult, ALU.add))
                link(vec.tensor_scalar(beta[:, :, :], beta[:, :, :], 1e-18, None, ALU.max))
                vec.tensor_scalar(halfb[:, :, :], beta[:, :, :], 0.5, None, ALU.mult).then_inc(s_baD, 1)
                ve.wait_ge(s_baA, 2)
                link(vec.scalar_tensor_tensor(out=ge[:, :, :], in0=gu[:, :, :], scalar=0.0, in1=ge[:, :, :],
                                              op0=ALU.max, op1=ALU.add))
                vec.scalar_tensor_tensor(out=gl_in[:, :, :], in0=ge[:, :, :], scalar=-1.0,
                                         in1=alog[:, :].unsqueeze(1).broadcast_to([128, T, H_DN]),
                                         op0=ALU.mult, op1=ALU.mult).then_inc(s_baD, 1)
                ve.wait_ge(s_gcp, 1)
                vec.tensor_copy(gcl[:, :, :, :].rearrange("p a t h -> p (a t h)"), M[1][:, 0:32]).then_inc(s_gc, 1)

            def do_za(g):
                ve.wait_ge(s_zat, g + 1)
                v = za[:, :, 512 * g:512 * g + 512]
                vec.scalar_tensor_tensor(out=v, in0=v, scalar=1.0, in1=proj[:, PSLOT[J_ZA[g]], :, :], op0=ALU.add, op1=ALU.mult
                                         ).then_inc(s_za, 1)

            def do_dnC(h):
                ve.wait_ge(s_dnT, h + 1)
                if h >= 4:
                    ve.wait_ge(s_5cp, h - 3)
                src = [M[0][:, S:2 * S], M[0][:, 0:S], M[1][:, 0:S]]
                tile = [8 + h, h, 16 + h]
                n = 12 * h
                for r in range(CONV):
                    for c in range(3):
                        y = ykqv[:, h % 4, c, :]
                        col = V_CONV + 24 * (CONV - 1 - r) + tile[c]
                        wc = vt[:, col:col + 1]
                        if r == 0:
                            ins = vec.tensor_scalar(y, src[c], wc, None, ALU.mult)
                        else:
                            ve.wait_ge(s_cv4, n + 1 - 3)
                            ins = vec.scalar_tensor_tensor(out=y[:, r:], in0=src[c][:, 0:S - r], scalar=wc,
                                                           in1=y[:, r:], op0=ALU.mult, op1=ALU.add)
                        ins.then_inc(s_cv4, 1)
                        n += 1
                ve.wait_ge(s_th, h + 1)
                y = ykqv[:, h % 4, :, :]
                vec.scalar_tensor_tensor(out=y[:, 0:2, :], in0=M[0][:, :].rearrange("p (c s) -> p c s", c=2), scalar=1.0,
                                         in1=y[:, 0:2, :], op0=ALU.add, op1=ALU.mult).then_inc(s_silu, 1)
                vec.scalar_tensor_tensor(out=y[:, 2, :], in0=M[1][:, 0:S], scalar=1.0, in1=y[:, 2, :],
                                         op0=ALU.add, op1=ALU.mult).then_inc(s_silu, 1)

            def do_dnB(h):
                ve.wait_ge(s_np, h + 1)
                ve.wait_ge(s_tok, h + 1)
                vec.tensor_copy(nrm[:, h, :], M[2][:, 384:388]).then_inc(s_nrm, 1)

            def do_dnV(g):
                hs = slice(4 * g, 4 * g + 4)
                ve.wait_ge(s_nrm, 4 * g + 4)
                vec.tensor_scalar(hln[:, g, :, :], nrm[:, hs, :], 4 * EPS, None, ALU.add).then_inc(s_lnq, 1)
                ve.wait_ge(s_lnq, 2 * g + 2)
                ve.wait_ge(s_gc, 1)
                ve.wait_ge(s_baA, 2)
                link(vec.tensor_scalar(hln[:, g, :, :], hln[:, g, :, :], -0.5, None, ALU.mult))
                lk, lq = hln[:, g, :, 0:2], hln[:, g, :, 2:4]
                gc = gcl[:, 0, :, hs].rearrange("p t h -> p h t")
                gl = gcl[:, 1, :, hs].rearrange("p t h -> p h t")
                lb = lnb[:, :, hs].rearrange("p t h -> p h t")

                def e(a):
                    return ei[:, g, a, :].rearrange("p (h t) -> p h t", h=4)
                vec.tensor_tensor(cc[:, g, :, :], lk, gc, ALU.subtract)
                link(vec.tensor_tensor(e(0), lk, gc, ALU.add))
                vec.tensor_tensor(e(0), e(0), lb, ALU.add)
                vec.tensor_tensor(e(1), cc[:, g, :, :], gl, ALU.add)
                vec.tensor_copy(e(2), gc)
                vec.tensor_scalar(e(3), lq, -0.5 * math.log(128.0), None, ALU.add).then_inc(s_ei, 1)
                ve.wait_ge(s_rp, g + 1)
                vec.tensor_copy(rows[:, g, :], M[1][0:24, 0:128]).then_inc(s_rows, 1)
                ve.wait_ge(s_ex, g + 1)
                link(vec.tensor_scalar(nks[:, g, :], ex[:, g, 0, :], -1.0, None, ALU.mult))

            def do_dnG(h):
                ve.wait_ge(s_eq, h + 1)
                v = aq[:, 2 * (h % 4):2 * (h % 4) + 2, :, :].rearrange("p m c n -> p (m c n)")
                vec.tensor_tensor(v, M[0][:, :], v, ALU.mult).then_inc(s_aq, 1)

            def do_d4x(i):
                pr, l = divmod(i, 7)
                g, par = divmod(pr, 2)
                if l == 0:
                    ve.wait_ge(s_x1p[par], 7 * g + 1)
                    eye = ident[:, :].unsqueeze(1).broadcast_to([128, 4, 128])
                    vec.tensor_tensor(tinv[:, par, :, :], eye, M[0][:, :].rearrange("p (m n) -> p m n", m=4), ALU.subtract)
                    vec.tensor_tensor(tinvt[:, par, :, :], eye, ofx[:, par, :, :], ALU.subtract).then_inc(s_t[par], 1)

            def do_d4y(i):
                pr, l = divmod(i, 7)
                g, par = divmod(pr, 2)
                if l == 0:
                    return
                ve.wait_ge(s_x2p[par], 6 * g + l)
                ve.wait_ge(s_t[par], 7 * g + l)
                t0, t1 = halves(tinv, par, l)[:, :, 0, :], halves(tinvt, par, l)[:, :, 1, :]
                m1, m2 = (M[b][:, 0:256].rearrange("p (b r) -> p b r", r=1 << l) for b in (1, 2))
                if l < 6:
                    vec.tensor_tensor(t0, t0, m1, ALU.subtract)
                vec.tensor_tensor(t1, t1, m2, ALU.subtract).then_inc(s_t[par], 1)

            def do_d5c(h):
                g, hl = h // 4, h % 4
                ve.wait_ge(s_5cA, h + 1)
                ve.wait_ge(s_tks, h + 1)
                vec.scalar_tensor_tensor(out=tok[:, hl, 2, :], in0=M[2][:, 0:128], scalar=nks[:, g, 2 * hl + 1:2 * hl + 2],
                                         in1=tok[:, hl, 2, :], op0=ALU.mult, op1=ALU.add).then_inc(s_5c, 1)

            def do_d5e(h):
                ve.wait_ge(s_5ep, h + 1)
                vec.tensor_tensor(tok[:, h % 4, 1, :], dw[:, 3, :], M[1][:, 0:128], ALU.add).then_inc(s_5e, 1)

            def do_d6(g):
                ve.wait_ge(s_oss, 4 * g + 4)
                sq = ex[:, g, 3, :]
                link(vec.tensor_tensor(oms[:, g, :], oss[:, g, :], sq, ALU.mult))
                link(vec.tensor_tensor(oms[:, g, :], oms[:, g, :], sq, ALU.mult))
                vec.tensor_scalar(oms[:, g, :], oms[:, g, :], 1.0 / 128, EPS, ALU.mult, ALU.add).then_inc(s_oms, 1)
                ve.wait_ge(s_opw, g + 1)
                vec.scalar_tensor_tensor(out=ofac[:, g, :], in0=oms[:, g, :], scalar=0.5, in1=sq, op0=ALU.mult,
                                         op1=ALU.mult).then_inc(s_of6, 1)

            def do_d7(h):
                g, hl = h // 4, h % 4
                ve.wait_ge(s_of6, g + 1)
                ve.wait_ge(s_za, g + 1)
                for t in range(T):
                    v = tok[:, hl, t, :]
                    vec.scalar_tensor_tensor(out=v, in0=v, scalar=ofac[:, g, 2 * hl + t:2 * hl + t + 1],
                                             in1=za[:, t, 128 * h:128 * h + 128], op0=ALU.mult, op1=ALU.mult
                                             ).then_inc(s_ow, 1)

            def do_glu(i):
                ve.wait_ge(s_glt, i + 1)
                a = proj[:, 2 * i, :, :]
                vec.scalar_tensor_tensor(out=a, in0=proj[:, 2 * i + 1, :, :], scalar=1.0, in1=a, op0=ALU.add,
                                         op1=ALU.mult).then_inc(s_glu, 1)

            def do_conv(i):
                pr, q = divmod(i, 8)
                for k in range(8 * q, min(8 * q + 8, 2 * TAPS)):
                    d, which = divmod(k, 2)
                    ct = 2 * pr + which
                    n = 2 * TAPS * pr + k
                    c, gsrc = cvr[:, ct, :], cvr[:, ct + 2, :]
                    col = V_DW + 8 * (TAPS - 1 - d) + ct
                    if d == 0:
                        if pr:
                            ve.wait_ge(s_cv, 2 * TAPS * pr)
                        ve.wait_ge(s_gt, ct + 1)
                        ins = vec.tensor_scalar(c, gsrc, vt[:, col:col + 1], gain("ev_dw_b", ct), ALU.mult, ALU.add)
                    else:
                        ve.wait_ge(s_cv, n - 1)
                        ins = vec.scalar_tensor_tensor(out=c[:, d:], in0=gsrc[:, 0:S - d], scalar=vt[:, col:col + 1],
                                                       in1=c[:, d:], op0=ALU.mult, op1=ALU.add)
                    ins.then_inc(s_cv, 1)

            def do_lnm(_):
                ve.wait_ge(s_mu, 1)
                v = cvr[:, 0:8, :]
                vec.tensor_tensor(v, v, scr[:, 0:S].unsqueeze(1).broadcast_to([128, 8, S]), ALU.subtract).then_inc(s_xc, 1)

            def do_lnr(_):
                ve.wait_ge(s_lvp, 8)
                r = scr[:, S:2 * S]
                vec.tensor_scalar(r, M[3][:, 0:S], 1.0 / CVW, EPS, ALU.mult, ALU.add).then_inc(s_var, 1)
                ve.wait_ge(s_std, 1)
                link(vec.reciprocal(r, r))
                v = cvr[:, 0:8, :]
                vec.tensor_tensor(v, v, r.unsqueeze(1).broadcast_to([128, 8, S]), ALU.mult).then_inc(s_xn, 1)

            def do_lno(ct):
                ve.wait_ge(s_xn, 1)
                c = cvr[:, ct, :]
                vec.tensor_scalar(c, c, gain("ev_ln_g", ct), gain("ev_ln_b", ct), ALU.mult, ALU.add).then_inc(s_ly, 1)
                ve.wait_ge(s_lt, ct + 1)
                ve.wait_ge(s_z, ct + 1)
                link(vec.scalar_tensor_tensor(out=c, in0=cvr[:, 8 + ct % 2, :], scalar=1.0, in1=c, op0=ALU.add, op1=ALU.mult))
                v = mix[:, 8 + ct, :]
                vec.scalar_tensor_tensor(out=v, in0=c, scalar=0.25, in1=v, op0=ALU.mult, op1=ALU.mult).then_inc(s_mixb, 1)

            def do_zT(n):
                ve.wait_ge(s_zc, n + 1)
                v = mix[:, zsource(n)[3], :]
                vec.scalar_tensor_tensor(out=v, in0=M[3][:, S:2 * S], scalar=1.0, in1=v, op0=ALU.add, op1=ALU.mult
                                         ).then_inc(s_z, 1)

            mq_n = [0]

            def mean_squares(i):
                mq_n[0] += 1
                n = mq_n[0]
                ve.wait_ge(s_mqs, n)
                vec.tensor_scalar(qss[:, i, :], qss[:, i, :], 1.0 / 256, EPS, ALU.mult, ALU.add).then_inc(s_mqm, 1)
                ve.wait_ge(s_mqr, n)

            def do_mqs(i):
                mean_squares(i)
                vec.tensor_scalar(qrs[:, i, :], qss[:, i, :], 1.0 / 16, None, ALU.mult).then_inc(s_mqk, 1)

            def do_mks(i):
                mean_squares(4 + i)
                for t in range(T):
                    for hd in range(2):
                        v = proj[:, MQSLOT[4 + i], t, 256 * hd:256 * hd + 256]
                        ins = vec.tensor_scalar(v, v, qss[:, 4 + i, 2 * t + hd:2 * t + hd + 1], None, ALU.mult)
                ins.then_inc(s_mks, 1)

            def do_mas(n):
                i, hd2 = 2 * (n // 4) + (n % 4) // 2, n % 2
                ve.wait_ge(s_scp, n + 1)
                ve.wait_ge(s_mqk, i + 1)
                link(vec.tensor_reduce(smx[:, n, :], M[0][:, :].rearrange("p (t m) -> p t m", t=T), AX.X, ALU.max))
                vec.scalar_tensor_tensor(out=snb[:, n, :], in0=smx[:, n, :], scalar=-1.0, in1=qrs[:, i, hd2:4:2],
                                         op0=ALU.mult, op1=ALU.mult).then_inc(s_nb, 1)
                ve.wait_ge(s_exp, n + 1)
                link(vec.reciprocal(srs[:, n, :], ssm[:, n, :]))
                for t in range(T):
                    ins = vec.tensor_scalar(prob[:, t, :], prob[:, t, :], srs[:, n, t:t + 1], None, ALU.mult)
                ins.then_inc(s_pr, 1)

            def do_mao(m):
                ve.wait_ge(s_maop, m + 1)
                ve.wait_ge(s_z, (8 if m < 8 else 32) + m % 8 + 1)
                v = mix[:, 16 + m % 8, :]
                vec.scalar_tensor_tensor(out=v, in0=M[2][:, 0:S], scalar=0.5, in1=v, op0=ALU.mult, op1=ALU.mult
                                         ).then_inc(s_mao, 1)

            def do_sbn(g):
                for c in range(2):
                    ve.wait_ge(s_sbs, 2 * g + c + 1)
                    vec.tensor_reduce(bss[:, g, 8 * c:8 * c + 8], scr[:, :].rearrange("p (a n) -> p a n", n=128),
                                      AX.X, ALU.add).then_inc(s_sbr, 1)
                ve.wait_ge(s_sbr, 2 * g + 2)
                vec.tensor_scalar(bss[:, g, :], bss[:, g, :], 1.0 / 128, EPS, ALU.mult, ALU.add).then_inc(s_sbm, 1)

            def do_sbz(h):
                ve.wait_ge(s_sbA, h + 1)
                if h:
                    ve.wait_ge(s_sbcp, h)
                vec.scalar_tensor_tensor(out=spz, in0=M[1][:, 0:384], scalar=0.0, in1=absz, op0=ALU.max, op1=ALU.add
                                         ).then_inc(s_sbsp, 1)

            def do_sbo(h):
                ve.wait_ge(s_sbop, h + 1)
                ve.wait_ge(s_z, 16 + h + 1)
                v = mix[:, h, :]
                vec.scalar_tensor_tensor(out=v, in0=M[2][:, 0:S], scalar=0.5, in1=v, op0=ALU.mult, op1=ALU.mult
                                         ).then_inc(s_sbo, 1)

            steps = {"chunk": do_chunk, "evac": do_evac, "xt": do_xt, "mf": do_mf, "rstd": do_rstd, "ba": do_ba,
                     "za": do_za, "dnC": do_dnC, "dnB": do_dnB, "dnV": do_dnV, "dnG": do_dnG, "d4x": do_d4x,
                     "d4y": do_d4y, "d5c": do_d5c, "d5e": do_d5e, "d6": do_d6, "d7": do_d7, "glu": do_glu,
                     "conv": do_conv, "lnm": do_lnm, "lnr": do_lnr, "lno": do_lno, "zT": do_zT, "mqs": do_mqs,
                     "mks": do_mks, "mas": do_mas, "mao": do_mao, "sbn": do_sbn, "sbz": do_sbz, "sbo": do_sbo}
            ve.wait_ge(s_vt, 1)
            for c in range(AHEAD):
                split(c)
            for st, i in plan:
                if st in steps:
                    steps[st](i)

        @block.tensor
        def _(pe):
            def take(st, i):
                for q in bank_free[st, i]:
                    pe.wait_ge(*q)

            def three(out_, k, t, hi, lo, first, last):
                xh, xl = xhi[:, k, 128 * t:128 * t + 128], xlo[:, k, 128 * t:128 * t + 128]
                mm(out_, xh, hi, start=first, stop=False)
                mm(out_, xh, lo, start=False, stop=False)
                return mm(out_, xl, hi, start=False, stop=last)

            def do_chunk(c):
                j = JOB_OF[c]
                kts, fill = JOBS[j][3], JOBS[j][4]
                i = c - CH0[j]
                if i == 0 and j >= 2:
                    pe.wait_ge(*evac_done(j - 2))
                pe.wait_ge(s_xl, fill + 2 * i + 2)
                pe.wait_ge(s_lo, c + 1)
                for k in (2 * i, 2 * i + 1):
                    for t in range(T):
                        ins = three(pj[j % 2][t][:, :], SLOT[fill + k], t, whi[:, c % RING, k % 2, :],
                                    wlo[:, c % RING, k % 2, :], k == 0, k == kts - 1)
                ins.then_inc(s_pe, 1)

            def turn(dst, src):
                return nc.tensor.transpose(dst, src, ident[:, :])

            def do_xt(n):
                if n < F_OA:
                    src, k = hid, n
                    pe.wait_ge(s_xin[k // 4], 16)
                elif n < F_OB:
                    src, k = memx, n - F_MEM
                    pe.wait_ge(s_min, 16)
                else:
                    src, k = hid, n - F_H
                    pe.wait_ge(*evac_done(J_OM + k // 4))
                take("xt", n)
                for t in range(T):
                    ins = turn(M[banks("xt", n)[0]][:, 128 * t:128 * t + 128], src[:, t, 128 * k:128 * k + 128])
                ins.then_inc(s_xp, 1)

            def do_ba(_):
                pe.wait_ge(s_wbl, 1)
                pe.wait_ge(s_xl, 16)
                take("ba", 0)
                for t in range(T):
                    for k in range(KT):
                        ins = three(M[0][:, 16 * t:16 * t + 16], k, t, bah[:, k, :], bal[:, k, :], k == 0, k == KT - 1)
                ins.then_inc(s_bap, 1)
                pe.wait_ge(s_const, 2)
                pe.wait_ge(s_baD, 3)
                g = gl_in[:, :, :].rearrange("p t h -> p (t h)")
                mm(M[1][:, 0:16], upto[:, :], g, start=True, stop=True)
                mm(M[1][:, 16:32], ones[:, :], g, start=True, stop=True).then_inc(s_gcp, 1)

            def do_dnT(h):
                g = h // 4
                pe.wait_ge(*evac_done(J_V[g]))
                take("dnT", h)
                for c, slot in enumerate((PSLOT[J_Q[g]], PSLOT[J_K[g]], PSLOT[J_V[g]])):
                    for t in range(T):
                        o = 256 * (c % 2) + 128 * t
                        ins = turn(M[c // 2][:, o:o + 128], proj[:, slot, t, 128 * (h % 4):128 * (h % 4) + 128])
                ins.then_inc(s_dnT, 1)

            def do_dnB(h):
                pe.wait_ge(s_silu, 2 * h + 2)
                take("dnB", h)
                pe.wait_ge(s_sq, h + 1)
                for a in range(4):
                    ins = mm(M[2][:, 384 + a:385 + a], scr[:, 128 * a:128 * a + 128], ones[:, 0:1], start=True, stop=True)
                ins.then_inc(s_np, 1)
                y = ykqv[:, h % 4, :, :]
                turn(M[2][:, 0:128], y[:, 0, 0:128])
                turn(M[2][:, 128:256], y[:, 2, 0:128])
                turn(M[2][:, 256:384], y[:, 2, 128:256]).then_inc(s_back, 1)

            def do_dnV(g):
                pe.wait_ge(s_ei, g + 1)
                take("dnV", g)
                turn(M[1][0:24, 0:128], ei[:, g, 0:3, :].rearrange("p a m -> p (a m)")).then_inc(s_rp, 1)

            def do_dnG(h):
                g, hl = h // 4, h % 4
                pe.wait_ge(s_rows, g + 1)
                take("dnG", h)
                for t in range(T):
                    tc = slice(128 * t, 128 * t + 128)
                    mm(M[0][:, 256 * t:256 * t + 256].rearrange("p (c n) -> p c n", c=2), ykqv[:, hl, 0, tc],
                       ykqv[:, hl, 0:2, tc], start=True, stop=True)
                for t in range(T):
                    mm(M[1][:, 256 * t:256 * t + 256], identb[:, :], shut[:, :, :].rearrange("p c n -> p (c n)"),
                       start=(t == 0), stop=False, skip_group_check=True)
                    for c in range(2):
                        o = 256 * t + 128 * c
                        r = 16 * c + 2 * hl + t
                        ins = mm(M[1][:, o:o + 128], ident[0:24, r:r + 1].broadcast_to([24, 128]), rows[:, g, :],
                                 start=False, stop=True, skip_group_check=True)
                ins.then_inc(s_gp, 1)

            def do_d4x(i):
                pr, l = divmod(i, 7)
                g, par = divmod(pr, 2)
                pe.wait_ge(s_of[par], 7 * g + l + 1)
                if l:
                    pe.wait_ge(s_t[par], 7 * g + l)
                take("d4x", i)
                for m in range(4):
                    ins = mm(M[0][:, 128 * m:128 * m + 128], ofx[:, par, m, :], tinv[:, par, m, :] if l else ident[:, :],
                             start=True, stop=True)
                ins.then_inc(s_x1p[par], 1)

            def do_d4y(i):
                pr, l = divmod(i, 7)
                g, par = divmod(pr, 2)
                if l == 0:
                    return
                pe.wait_ge(s_x1[par], 6 * g + l)
                take("d4y", i)
                for m in range(4):
                    m1, m2 = (M[b][:, 64 * m:64 * m + 64].rearrange("p (b r) -> p b r", r=1 << l) for b in (1, 2))
                    x0, t1 = (v[:, par, m, :].rearrange("p (b c r) -> p b c r", c=2, r=1 << l) for v in (ofx, tinvt))
                    if l < 6:
                        mm(m1, tinvt[:, par, m, :], x0[:, :, 0, :], start=True, stop=True)
                    ins = mm(m2, ofx[:, par, m, :], t1[:, :, 1, :], start=True, stop=True)
                ins.then_inc(s_x2p[par], 1)

            def inverse(h, t):
                return tinvt[:, (h % 4) // 2, 2 * (h % 2) + t, :]

            def do_d5a(h):
                pe.wait_ge(s_tks, h + 1)
                pe.wait_ge(s_t[(h % 4) // 2], 7 * (h // 4) + 7)
                take("d5a", h)
                mm(M[0][:, 0:128], inverse(h, 0), tok[:, h % 4, 1, :], start=True, stop=True).then_inc(s_5ap, 1)

            def do_d5b(h):
                pe.wait_ge(s_5a, h + 1)
                take("d5b", h)
                mm(M[1][:, 0:128], tok[:, h % 4, 0, :], dw[:, 0, :], start=True, stop=True)
                mm(M[1][:, 128:256], aq[:, 2 * (h % 4), 1, :], dw[:, 0, :], start=True, stop=True).then_inc(s_5bp, 1)

            def do_d5c(h):
                pe.wait_ge(s_5b, h + 1)
                take("d5c", h)
                mm(M[2][:, 0:128], ykqv[:, h % 4, 0, 128:256], dw[:, 1, :], start=True, stop=True)
                mm(M[2][:, 128:256], ykqv[:, h % 4, 1, 128:256], dw[:, 1, :], start=True, stop=True).then_inc(s_5cp, 1)

            def do_d5d(h):
                pe.wait_ge(s_5c, h + 1)
                take("d5d", h)
                mm(M[0][:, 0:128], inverse(h, 1), tok[:, h % 4, 2, :], start=True, stop=True).then_inc(s_5dp, 1)

            def do_d5e(h):
                pe.wait_ge(s_5d, h + 1)
                take("d5e", h)
                mm(M[1][:, 0:128], aq[:, 2 * (h % 4) + 1, 1, :], dw[:, 2, :], start=True, stop=True).then_inc(s_5ep, 1)

            def do_d7(h):
                pe.wait_ge(s_ow, 2 * h + 2)
                take("d7", h)
                for t in range(T):
                    ins = turn(M[2][:, 128 * t:128 * t + 128], tok[:, h % 4, t, :])
                ins.then_inc(s_owp, 1)

            def do_gT(ct):
                i = ct // 4
                pe.wait_ge(s_glu, i + 1)
                take("gT", ct)
                for t in range(T):
                    ins = turn(M[3][:, 128 * t:128 * t + 128], proj[:, 2 * i, t, 128 * (ct % 4):128 * (ct % 4) + 128])
                ins.then_inc(s_gtp, 1)

            def do_lnm(_):
                pe.wait_ge(s_cv, 2 * TAPS * 8 // 2)
                take("lnm", 0)
                for ct in range(8):
                    ins = mm(M[3][:, 0:S], ones[:, :], cvr[:, ct, :], start=(ct == 0), stop=(ct == 7))
                ins.then_inc(s_mup, 1)

            def do_lnv(ct):
                pe.wait_ge(s_lsq, ct + 1)
                take("lnv", ct)
                mm(M[3][:, 0:S], ones[:, :], cvr[:, 8 + ct % 2, :], start=(ct == 0), stop=(ct == 7)).then_inc(s_lvp, 1)

            def do_zT(n):
                j, slot, col, _ = zsource(n)
                pe.wait_ge(*evac_done(j))
                take("zT", n)
                for t in range(T):
                    ins = turn(M[3][:, 128 * t:128 * t + 128], proj[:, slot, t, 128 * col:128 * col + 128])
                ins.then_inc(s_zp, 1)

            def do_mqT(dt):
                i = dt // 4
                pe.wait_ge(*evac_done(MQJOB[i]))
                take("mqT", dt)
                for t in range(T):
                    ins = turn(M[dt % 2][:, 128 * t:128 * t + 128],
                               proj[:, MQSLOT[i], t, 128 * (dt % 4):128 * (dt % 4) + 128])
                ins.then_inc(s_mqp, 1)

            def do_mkT(dt):
                i = dt // 4
                pe.wait_ge(s_mks, i + 1)
                take("mkT", dt)
                for t in range(T):
                    ins = turn(M[dt % 2][:, 128 * t:128 * t + 128],
                               proj[:, MQSLOT[4 + i], t, 128 * (dt % 4):128 * (dt % 4) + 128])
                ins.then_inc(s_mkp, 1)

            def do_mas(n):
                hd = n % 4
                pe.wait_ge(s_mqT, 8 * (n // 4) + 2 * hd + 2)
                pe.wait_ge(s_mkT, 2 * hd + 2)
                take("mas", n)
                for t in range(T):
                    for dt in range(2):
                        ins = mm(M[0][:, 256 * t:256 * t + 256], qmt[n // 4][:, 2 * hd + dt, 128 * t:128 * t + 128],
                                 kmt[:, 2 * hd + dt, :], start=(dt == 0), stop=(dt == 1))
                ins.then_inc(s_scp, 1)

            def do_mat(n):
                pe.wait_ge(s_pr, n + 1)
                take("mat", n)
                for m in range(2):
                    for t in range(T):
                        ins = turn(M[1][:, 256 * m + 128 * t:256 * m + 128 * t + 128], prob[:, t, 128 * m:128 * m + 128])
                ins.then_inc(s_ptp, 1)

            def do_mao(m):
                n, dt = divmod(m, 2)
                hd = n % 4
                pe.wait_ge(s_pt, n + 1)
                pe.wait_ge(*evac_done(J_MEM + 2 + hd // 2))
                take("mao", m)
                for mt in range(2):
                    ins = mm(M[2][:, 0:S], vm[:, mt, 256 * hd + 128 * dt:256 * hd + 128 * dt + 128], probt[:, mt, :],
                             start=(mt == 0), stop=(mt == 1))
                ins.then_inc(s_maop, 1)

            def do_sbT(h):
                pe.wait_ge(s_sbn, 2 * (h // 4) + 2)
                take("sbT", h)
                for c in range(2):
                    for t in range(T):
                        o = 256 * c + 128 * t
                        ins = turn(M[0][:, o:o + 128], proj[:, c, t, 128 * (h % 4):128 * (h % 4) + 128])
                ins.then_inc(s_sbtp, 1)

            def do_sbz(h):
                pe.wait_ge(s_sbT, h + 1)
                take("sbz", h)
                q, k = qk[:, h % 4, 0, :], qk[:, h % 4, 1, :]
                mm(M[1][:, 0:S], k[:, 0:128], q[:, 0:S], start=True, stop=False, skip_group_check=True)
                mm(M[1][:, S:384], k[:, 128:S], q[:, 128:S], start=False, stop=False, skip_group_check=True
                   ).then_inc(s_sbzp, 1)

            def do_sbc(h):
                pe.wait_ge(s_sbmk, h + 1)
                for a, b, lhs, rhs in ((0, 256, negfrom, spz[:, 0:256]), (256, 384, negfrom, spz[:, 256:384]),
                                       (128, 256, negones, spz[:, 256:384]), (0, 128, identb, shut[:, 0, :]),
                                       (256, 384, identb, shut[:, 0, :])):
                    ins = mm(M[1][:, a:b], lhs[:, :], rhs, start=False, stop=(a == 256), skip_group_check=True)
                ins.then_inc(s_sbcp, 1)

            def do_sbo(h):
                pe.wait_ge(s_sbW, h + 1)
                pe.wait_ge(*evac_done(J_ODIN + 4 * (h // 4) + 2))
                take("sbo", h)
                v = proj[:, 2, :, 128 * (h % 4):128 * (h % 4) + 128]
                mm(M[2][:, 0:S], v[:, 0, :], wts[:, 0:256], start=True, stop=False, skip_group_check=True)
                mm(M[2][:, 128:S], v[:, 1, :], wts[:, 256:384], start=False, stop=True, skip_group_check=True
                   ).then_inc(s_sbop, 1)

            steps = {"chunk": do_chunk, "xt": do_xt, "ba": do_ba, "dnT": do_dnT, "dnB": do_dnB, "dnV": do_dnV,
                     "dnG": do_dnG, "d4x": do_d4x, "d4y": do_d4y, "d5a": do_d5a, "d5b": do_d5b, "d5c": do_d5c,
                     "d5d": do_d5d, "d5e": do_d5e, "d7": do_d7, "gT": do_gT, "lnm": do_lnm, "lnv": do_lnv,
                     "zT": do_zT, "mqT": do_mqT, "mkT": do_mkT, "mas": do_mas, "mat": do_mat, "mao": do_mao,
                     "sbT": do_sbT, "sbz": do_sbz, "sbc": do_sbc, "sbo": do_sbo}
            pe.wait_ge(s_const, 1)
            pe.wait_ge(s_vrow, 16 * 15)
            for a, n in enumerate((NVEC, 96, 128, 120)):
                ins = nc.tensor.transpose(M[0][:, 128 * a:128 * a + n], vrow[0:n, a, :], ident[0:n, 0:n])
            ins.then_inc(s_vp, 1)
            for st, i in plan:
                if st in steps:
                    steps[st](i)


INS = ["x", "mem", "mem_norm_g", "w_mem_kv", "mem_k_norm_g", "ev_norm_g", "ev_w_in", "ev_conv_qkv", "ev_a_log",
       "ev_dt_bias", "ev_dn_norm_g", "ev_dw_w", "ev_dw_b", "ev_ln_g", "ev_ln_b", "ev_q_norm_m", "ev_w_out",
       "od_norm_g", "od_w_in", "od_q_norm_c", "od_k_norm_c", "od_q_norm_m", "od_w_out"]
LAST = len(JOBS)


def kernel(**inputs):
    import numpy as np
    import concourse.bacc as bacc
    from concourse.bass_utils import run_bass_kernel_spmd

    nc = bacc.Bacc("TRN2", target_bir_lowering=False, num_devices=1)
    arrays, d = {}, {}
    for name in INS:
        a = np.ascontiguousarray(inputs[name])
        arrays[f"in_{name}_dram"] = a
        d[name] = nc.dram_tensor(f"in_{name}_dram", a.shape, mybir.dt.from_np(a.dtype), kind="ExternalInput").ap()
    out = nc.dram_tensor("out_dram", (1, S, D), F32, kind="ExternalOutput").ap()

    def vecs(vrow):
        for name, n in VEC:
            v = d[name]
            v = v[0, :] if len(v.shape) == 2 else v
            yield vrow[VCOL[name]:VCOL[name] + n, 0, :], v.rearrange("(k p) -> k p", p=128)
        yield vrow[0:96, 1, :], d["ev_conv_qkv"][0, :, :].rearrange("k (c p) -> (k c) p", p=128)
        dw = d["ev_dw_w"][0, :, :].rearrange("k (c p) -> (k c) p", p=128)
        yield vrow[0:128, 2, :], dw[0:128, :]
        yield vrow[0:120, 3, :], dw[128:248, :]

    w = {"ev_in": d["ev_w_in"][0, :, :], "mem": d["w_mem_kv"], "ev_out": d["ev_w_out"][0, :, :],
         "od_in": d["od_w_in"][0, :, :], "od_out": d["od_w_out"][0, :, :]}
    prog(nc, d["x"][0, :, :], d["mem"][0, :, :], vecs, w, d["ev_a_log"][0, :], d["ev_dt_bias"][0, :],
         out[0, :, :], LAST)
    r = run_bass_kernel_spmd(nc, [arrays], core_ids=[0])
    return r.results[0]["out_dram"]
```

```python
import math

import concourse.bass as bass
from concourse import mybir
from contextlib import ExitStack

F32 = mybir.dt.float32
F32R = mybir.dt.float32r
BF16 = mybir.dt.bfloat16
ALU = mybir.AluOpType
ACT = mybir.ActivationFunctionType
AX = mybir.AxisListType

D = 2048
S = 256
T = 2
KT = D // 128
DNW, CVW, MW, SBW = 1024, 1024, 1024, 2048
H_DN, H_MEM, H_SB = 8, 4, 16
EPS = 1e-6
NEG = -1.0e30
CONV, TAPS = 4, 31

Q0, K0, V0, ZA0, BA0 = 0, DNW, 2 * DNW, 3 * DNW, 4 * DNW
GA0 = BA0 + 2 * H_DN
GB0 = GA0 + CVW
ZB0 = GB0 + CVW
QM0 = ZB0 + CVW
ZM0 = QM0 + MW
JOBS = []


def _jobs():
    for g in range(2):
        for base in (Q0, K0, V0, GA0, GB0, ZA0):
            JOBS.append(("ev_in", 0, base + 512 * g, KT, 0))
    for c0 in (ZB0, ZB0 + 512, QM0, QM0 + 512, ZM0, ZM0 + 512):
        JOBS.append(("ev_in", 0, c0, KT, 0))
    for b in range(4):
        JOBS.append(("ev_out", 0, 512 * b, 8, F_OA))
    for b in range(4):
        JOBS.append(("mem", 0, 512 * b, KT, F_MEM))
    for part in (1, 2):
        for b in range(4):
            JOBS.append(("ev_out", 1024 * part, 512 * b, 8, F_OB + 8 * (part - 1)))
    for g in range(4):
        for base in (0, SBW, 2 * SBW, 3 * SBW):
            JOBS.append(("od_in", 0, base + 512 * g, KT, F_H))
    for b in range(4):
        JOBS.append(("od_in", 0, 4 * SBW + 512 * b, KT, F_H))
    for part in range(3):
        for b in range(4):
            JOBS.append(("od_out", 1024 * part, 512 * b, 8, F_ODD + 8 * part))


F_OA, F_MEM, F_OB, F_OM, F_H, F_ODD = 16, 24, 40, 48, 56, 72
_jobs()
J_ZB, J_QM, J_ZM, J_OA, J_MEM, J_OB, J_OM, J_ODIN, J_ODOUT = 12, 14, 16, 18, 22, 26, 30, 34, 54
ADDED = [j for j in range(len(JOBS)) if JOBS[j][0] in ("ev_out", "od_out")]
COPIED = [j for j in range(len(JOBS)) if j not in ADDED]
CH0 = []
_n = 0
for _j in JOBS:
    CH0.append(_n)
    _n += _j[3] // 2
CH0.append(_n)
NCH = _n
JOB_OF = [j for j in range(len(JOBS)) for _ in range(JOBS[j][3] // 2)]

LOW, HIGH = list(range(8)), list(range(8, 16))
SLOT = 6 * (LOW + HIGH)


def fills_of(j):
    return range(JOBS[j][4], JOBS[j][4] + JOBS[j][3])


LAST_CHUNK = {}
for _j in range(len(JOBS)):
    for _i, _f in enumerate(fills_of(_j)):
        LAST_CHUNK[_f] = CH0[_j] + _i // 2 + 1


def chunks_before_fill(n):
    before = [m for m in range(n) if SLOT[m] == SLOT[n]]
    return LAST_CHUNK[before[-1]] if before else 0


VEC = [("ev_norm_g", 16), ("mem_norm_g", 16), ("od_norm_g", 16), ("mem_k_norm_g", 2), ("ev_q_norm_m", 2),
       ("od_q_norm_m", 2), ("ev_dn_norm_g", 1), ("od_q_norm_c", 1), ("od_k_norm_c", 1), ("ev_dw_b", 8),
       ("ev_ln_g", 8), ("ev_ln_b", 8)]
VCOL = {}
_n = 0
for _name, _c in VEC:
    VCOL[_name] = _n
    _n += _c
NVEC = _n
V_CONV = 128
V_DW = 256
NV = 512

RAWS, RING, AHEAD = 6, 7, 4
FIRST = 4
DN_STEP = 3.5
CONV_STEP = (1.15, 1.0, 1.35)


PSLOT = dict(zip(range(J_OA), (0, 1, 2, 3, 0, 1, 2, 3, 0, 1, 2, 3, 0, 1, 2, 3, 0, 1)))
PSLOT.update({J_MEM: 0, J_MEM + 1: 1})
PSLOT.update({j: (j - J_ODIN) % 4 for j in range(J_ODIN, J_ODOUT)})
J_Q, J_K, J_V, J_GLU, J_ZA = (0, 6), (1, 7), (2, 8), (3, 9), (5, 11)


def make_plan(last_job):
    placed = []

    def stream(k, pos, items):
        for step, cost in items:
            if step == "at":
                pos = max(pos, cost)
                continue
            if step == "wait":
                pos += cost
                continue
            placed.append((int(pos), k, len(placed), step))
            pos += cost
        return pos

    def after(j):
        return CH0[j + 1] + 3

    def deltanet(g):
        h0 = 4 * g
        s = []
        for h in range(h0, h0 + 4):
            s += [(("dnT", h), .2), (("dnC", h), 1.2), (("dnS", h), .9), (("dnU", h), DN_STEP - 2.1)]
            s += [(("dnB", h - 1), .1)] if h > h0 else []
        s += [("wait", 1), (("dnB", h0 + 3), 1), (("dnV", g), 2), (("dnR", g), 2.2)]
        s += [(("dnG", h), 1) for h in range(h0, h0 + 4)]
        a, b = 2 * g, 2 * g + 1
        s += [("wait", .5), (("d4x", 7 * a), 1)]
        for l in range(7):
            s += [(("d4y", 7 * a + l), 0), (("d4x", 7 * b + l), 1 if l else 1.6)]
            s += [(("d4y", 7 * b + l), 0 if l < 6 else 1)] + ([(("d4x", 7 * a + l + 1), 1)] if l < 6 else [])
        for n in range(11):
            now = [("d5" + "abcde"[n - 2 * q], h0 + q) for q in range(4) if 0 <= n - 2 * q < 5]
            s += [(st, 0) for st in now[:-1]] + [(now[-1], 1)]
        last = [(("d6", g), 1)] + [(("gate", h), .25) for h in range(h0, h0 + 4)]
        return s, last + [("wait", 1)] + [(("d7", h), 2 - 1.2 * g) for h in range(h0, h0 + 4)]

    for c in range(NCH):
        stream(7 if c < 16 else 0, max(-1, c - min(AHEAD, 2 + c // 4)), [(("split", c), 0)])
    stream(0, -1, [(("xt", n), 0) for n in range(2)])
    for n in range(2, KT):
        stream(0, n // 2 - 2, [(("xt", n), 0)])
    stream(0, 4, [(("vec", 0), 0)])
    stream(0, 6, [(("rstd", 0), 0)])
    stream(0, RING + 1, [(("baw", 0), 1), (("ba", 0), 2), (("bat", 0), 4), (("bas", 0), 0)])
    work, last = deltanet(0)
    p = stream(1, after(J_V[0]), work)
    stream(1, p, last)
    work, last = deltanet(1)
    start = max(int(p) + 2, after(J_V[1]))
    p = stream(1, start, work)
    for g in range(2):
        stream(1, after(J_ZA[g]) - 1, [(("za", g), 0)])
    inverted = p - 11
    stream(3, p, [(("mload", b), 1.5) for b in range(4)])
    oa = stream(1, p, last)
    stream(3, oa, [(("xload", b), 1.5) for b in range(4)])
    conv = [(("glu", 0), 1)] + [(("gT", ct), 1) for ct in range(4)]
    conv += [(("conv", q), CONV_STEP[0]) for q in range(26)] + [("at", start + 15)]
    conv += [(("conv", q), CONV_STEP[1]) for q in range(26, 32)]
    conv += [("at", after(J_GLU[1] + 1)), (("glu", 1), 1)] + [(("gT", ct), 1) for ct in range(4, 8)]
    conv += [(("conv", q), CONV_STEP[2]) for q in range(32, 64)]
    p = stream(2, after(J_GLU[0] + 1), conv)
    stream(3, max(after(J_ZB + 1), int(inverted) + 1), [(("zT", n), 1) for n in range(8)])
    p = stream(2, p, [(("lnm", 0), 2)])
    p = int(p) + 1
    stream(2, p, [(("lnv", ct), 0) for ct in range(8)])
    p = stream(2, p, [(("lnr", 0), 4)])
    q = stream(3, max(after(J_ZM), oa, p), [(("zT", n), 1) for n in range(8, 12)])
    q = stream(3, max(after(J_ZM + 1), q), [(("zT", n), 1) for n in range(12, 16)])
    p = stream(2, q, [(("lno", ct), .8) for ct in range(8)])
    stream(4, oa + 1, [(("mqs", i), 1) for i in range(2)])
    p = stream(4, after(J_MEM) + 1, [(("mks", 0), 4.5)] + [(("mkT", dt), .5) for dt in range(4)])
    p = stream(4, after(J_MEM + 1), [(("mks", 1), 2.5)] + [(("mkT", dt), .5) for dt in range(4, 8)])
    p = stream(4, p, [(("mqT", dt), .5) for dt in range(8)])

    def attend(n0):
        s = [(("mas", n0), 2)]
        for n in range(n0, n0 + 4):
            s += [(("mat", n), 0)] + ([(("mas", n + 1), 1 if n > n0 else 1.6)] if n < n0 + 3 else [("wait", 1)])
            s += [(("mao", 2 * n), 0), (("mao", 2 * n + 1), 1)]
        return s

    stream(4, max(p, after(J_MEM + 3) - 2), attend(0))
    for k in range(8):
        stream(5, CH0[J_OA] + k // 2 - 2, [(("mf", F_OA + k), 0)])
        stream(5, CH0[J_OB] + k // 2 - 3, [(("mf", F_OB + k), 0)])
        stream(5, CH0[J_OM] + k // 2 - 1, [(("mf", F_OM + k), 0)])
        stream(5, CH0[J_MEM] + k - 2, [(("xt", F_MEM + 2 * k), 0), (("xt", F_MEM + 2 * k + 1), 0)])
        stream(5, CH0[J_ODOUT] + k // 2 - 2, [(("mf", F_ODD + k), 0)])
        stream(5, CH0[J_ODOUT] + k // 2 + 4, [(("mf", F_ODD + 8 + k), 0)])
        stream(5, CH0[J_ODOUT + 8] + k // 2 - 1, [(("mf", F_ODD + 16 + k), 0)])
    stream(5, CH0[J_MEM] + 6, [(("rstd", 1), 0)])
    for k in range(KT):
        b = k // 4
        stream(5, max(CH0[J_OM + 1 + b] + (1 if b < 3 else 0), CH0[J_ODIN - 1] + (k - 8) // 2 + 1),
               [(("xt", F_H + k), 0)])
    stream(5, CH0[J_ODIN] + 1, [(("rstd", 2), 0)])
    p = 0
    for g in range(4):
        s = [(("sbn", g), 4)] + [(("sbT", h), 1) for h in range(4 * g, 4 * g + 4)]
        s += [("at", after(J_ODIN + 4 * g + 3)), (("tab", g), 0)]
        for h in range(4 * g, 4 * g + 4):
            s += [(("sbz", h), 0), (("zT", 16 + h), 2), (("sbc", h), 1), (("sbo", h), 0)]
        p = stream(6, max(p, after(J_ODIN + 4 * g + 1)), s)
    p = stream(6, max(p + 1, after(J_ODIN + 17)), [(("mqs", 2), 1.5), (("mqs", 3), 1.5)]
               + [(("mqT", dt), .5) for dt in range(8, 16)])
    stream(4, after(J_ODIN + 18), [(("zT", n), 1) for n in range(32, 36)])
    stream(4, after(J_ODIN + 19), [(("zT", n), 1) for n in range(36, 40)])
    p = stream(6, max(p, after(J_ODIN + 19)), attend(4))
    for j in range(len(JOBS)):
        late = 5 if j == J_GLU[1] + 1 else 0 if j in (J_ODIN - 1, len(JOBS) - 1) else 1
        stream(-1, CH0[j + 1] + late, [(("evac", j), 0)])

    plan = []
    placed.sort(key=lambda q: q[:3])
    at = 0
    for c in range(NCH):
        while at < len(placed) and placed[at][0] <= c:
            plan.append(placed[at][3])
            at += 1
        plan.append(("chunk", c))
    plan += [q[3] for q in placed[at:]]
    if last_job < len(JOBS):
        stop = plan.index(("evac", last_job - 1)) + 1
        plan = [q for q in plan[:stop] if not (q[0] in ("chunk", "split") and q[1] >= CH0[last_job])
                and not (q[0] == "xt" and q[1] >= F_H)]
    return plan


def prog(nc, x, mem, vecs, w, a_log, dt_bias, out, last_job=len(JOBS)):
    plan = make_plan(last_job)
    jobs = JOBS[:last_job]
    nch = CH0[last_job]
    ctx = ExitStack()
    with ctx:
        def sb(name, shape, dt=F32):
            return ctx.enter_context(nc.sbuf_tensor(name, shape, dt))

        def sem(name):
            return ctx.enter_context(nc.semaphore(name))

        raw = sb("raw", [128, RAWS, 2, 512])
        whi = sb("whi", [128, RING, 2, 512], F32R)
        wlo = sb("wlo", [128, RING, 2, 512], F32R)
        xhi = sb("xhi", [128, 16, S], F32R)
        xlo = sb("xlo", [128, 16, S], F32R)
        hid = sb("hid", [128, T, D])
        proj = sb("proj", [128, 4, T, 512])
        reg = sb("reg", [128, 4096])
        cvr = sb("cvr", [128, 10, S])
        mix = sb("mix", [128, 24, S])
        scr = sb("scr", [128, 1024])
        ident = sb("ident", [128, 128])
        ones = sb("ones", [128, 128])
        negones = sb("negones", [128, 128])
        upto = sb("upto", [128, 128])
        negfrom = sb("negfrom", [128, 128])
        after01 = sb("after01", [128, 128])
        shut = sb("shut", [128, 2, 128], BF16)
        identb = sb("identb", [128, 128], BF16)
        vt = sb("vt", [128, NV])
        qgain = sb("qgain", [128, 1])
        rows = sb("rows", [24, 2, 128])
        ssq = sb("ssq", [128, 3, T])
        rstd = sb("rstd", [128, 3, T])
        mhalf = sb("mhalf", [128, 16])
        ba = sb("ba", [128, T, 2 * H_DN])
        alog = sb("alog", [128, H_DN])
        dtb = sb("dtb", [128, H_DN])
        beta = sb("beta", [128, T, H_DN])
        halfb = sb("halfb", [128, T, H_DN])
        lnb = sb("lnb", [128, T, H_DN])
        gu = sb("gu", [128, T, H_DN])
        ge = sb("ge", [128, T, H_DN])
        gl_in = sb("gl_in", [128, T, H_DN])
        gcl = sb("gcl", [128, 2, T, H_DN])
        nrm = sb("nrm", [128, H_DN, 4])
        hln = sb("hln", [128, 2, 4, 4])
        cc = sb("cc", [128, 2, 4, T])
        ei = sb("ei", [128, 2, 4, 8])
        ex = sb("ex", [128, 2, 4, 8])
        nks = sb("nks", [128, 2, 8])
        oss = sb("oss", [128, 2, 8])
        oms = sb("oms", [128, 2, 8])
        ofac = sb("ofac", [128, 2, 8])
        qss = sb("qss", [128, 6, 4])
        qrs = sb("qrs", [128, 6, 4])
        smx = sb("smx", [128, 8, T])
        snb = sb("snb", [128, 8, T])
        ssm = sb("ssm", [128, 8, T])
        srs = sb("srs", [128, 8, T])
        bss = sb("bss", [128, 4, 16])
        brs = sb("brs", [128, 4, 16])

        flat = hid[:, :, :].rearrange("p t d -> p (t d)")
        pflat = proj[:, :, :, :].rearrange("p a t n -> p (a t n)")
        cflat = cvr[:, :, :].rearrange("p a s -> p (a s)")
        mflat = mix[:, :, :].rearrange("p a s -> p (a s)")
        ykqv = reg[:, 0:3072].rearrange("p (h c s) -> p h c s", h=4, c=3)
        ofx = reg[:, 3072:4096].rearrange("p (a m n) -> p a m n", a=2, m=4)
        tok = flat[:, 0:1536].rearrange("p (h c n) -> p h c n", h=4, c=3)
        aq = flat[:, 1536:3584].rearrange("p (m c n) -> p m c n", m=8, c=2)
        dw = [v.rearrange("p (c n) -> p c n", c=4) for v in (flat[:, 3584:4096], scr[:, 512:1024])]
        tinv = mflat[:, 12 * S:16 * S].rearrange("p (a m n) -> p a m n", a=2, m=4)
        tinvt = mflat[:, 4 * S:8 * S].rearrange("p (a m n) -> p a m n", a=2, m=4)
        za = mflat[:, 16 * S:24 * S].rearrange("p (t n) -> p t n", t=T)
        level = mflat[:, 8 * S:8 * S + 896].rearrange("p (l n) -> p l n", l=7)
        memx = reg[:, :].rearrange("p (t d) -> p t d", t=T)
        kmt = reg[:, 0:2048].rearrange("p (a s) -> p a s", a=8)
        vm = reg[:, 2048:4096].rearrange("p (t n) -> p t n", t=T)
        qmt = [v[:, 0:2048].rearrange("p (a s) -> p a s", a=8) for v in (pflat, cflat)]
        prob = scr[:, 0:512].rearrange("p (t m) -> p t m", t=T)
        probt = scr[:, 512:1024].rearrange("p (m s) -> p m s", m=2)
        qk = cflat[:, 0:2048].rearrange("p (a c s) -> p a c s", a=4, c=2)
        wts = cflat[:, 2048:2432]
        absz = scr[:, 0:384]
        spz = scr[:, 512:896]
        vrow = pflat[:, 0:512].rearrange("p (a n) -> p a n", a=4)
        wba = reg[:, 0:256].rearrange("p (k n) -> p k n", k=16)
        bar = reg[0:2 * H_DN, 256:512]
        bah = whi[:, RING - 1, 0, 0:256].rearrange("p (k n) -> p k n", k=16)
        bal = wlo[:, RING - 1, 0, 0:256].rearrange("p (k n) -> p k n", k=16)

        def psum(name):
            return ctx.enter_context(nc.psum_tensor(name, [128, 512], F32))

        pj = [[psum(f"job{a}{t}") for t in range(T)] for a in range(2)]
        M = [psum(f"mixer{i}") for i in range(4)]

        s_gain = sem("x_gain_loaded")
        s_vrow = sem("vector_rows_loaded")
        s_small = sem("small_inputs_loaded")
        s_xin = [sem(f"x_columns_loaded{b}") for b in range(4)]
        s_min = sem("mem_loaded")
        s_xre = sem("x_loaded_again")
        s_raw = [sem(f"raw_chunk_loaded{i}") for i in range(RAWS)]
        s_out = sem("output_stored")
        s_hi = sem("chunk_high_parts")
        s_lo = sem("chunk_remainders")
        s_pe = sem("chunks_multiplied")
        s_evA = sem("job_results_copied")
        s_evD = sem("job_results_added")
        s_xp = sem("rows_transposed")
        s_xh = sem("fill_high_parts")
        s_xl = sem("fill_remainders")
        s_const = sem("constants_made")
        s_vp = sem("vectors_transposed")
        s_vt = sem("vectors_copied")
        s_ss = sem("row_squares_summed")
        s_ms = sem("row_mean_squares")
        s_rstd = sem("row_rstd")
        s_wbh = sem("ba_weights_high")
        s_wbl = sem("ba_weights_low")
        s_bap = sem("ba_multiplied")
        s_bac = sem("ba_rows_copied")
        s_batp = sem("ba_transposed")
        s_ba = sem("ba_copied")
        s_baA = sem("ba_scalar_steps")
        s_baD = sem("ba_vector_steps")
        s_gcp = sem("decays_summed")
        s_gc = sem("decays_copied")
        s_zat = sem("za_tanh")
        s_za = sem("za_gates")
        s_dnT = sem("dn_qkv_transposed")
        s_tap = sem("dn_last_tap")
        s_cv4 = sem("dn_other_taps")
        s_th = sem("dn_tanh")
        s_silu = sem("dn_silu")
        s_sq = sem("dn_squares")
        s_back = sem("dn_kv_transposed_back")
        s_tok = sem("dn_kv_by_token")
        s_np = sem("dn_norms_summed")
        s_nrm = sem("dn_norms_copied")
        s_lnq = sem("dn_log_norms")
        s_ei = sem("dn_exponents")
        s_ex = sem("dn_factors")
        s_rp = sem("dn_rows_transposed")
        s_rows = sem("dn_rows_copied")
        s_tks = sem("dn_kv_scaled")
        s_gp = sem("dn_products")
        s_eq = sem("dn_decays")
        s_aq = sem("dn_matrices")
        s_of = [sem(f"inv_masked{i}") for i in range(2)]
        s_x1p = [sem(f"inv_first_product{i}") for i in range(2)]
        s_x1 = [sem(f"inv_first_copied{i}") for i in range(2)]
        s_x2p = [sem(f"inv_second_products{i}") for i in range(2)]
        s_t = [sem(f"inv_updated{i}") for i in range(2)]
        s_5ap = sem("dn_v0_product")
        s_5a = sem("dn_v0_copied")
        s_5bp = sem("dn_state_products")
        s_5b = sem("dn_state_copied")
        s_5cp = sem("dn_state_read")
        s_5cA = sem("dn_q_state_copied")
        s_5c = sem("dn_second_rhs")
        s_5dp = sem("dn_v1_product")
        s_5d = sem("dn_v1_copied")
        s_5ep = sem("dn_o1_product")
        s_5e = sem("dn_o1_added")
        s_oss = sem("dn_out_squares")
        s_oms = sem("dn_out_mean_squares")
        s_opw = sem("dn_out_rstd")
        s_of6 = sem("dn_out_factors")
        s_ow = sem("dn_out_gated")
        s_owp = sem("dn_out_transposed")
        s_mixa = sem("dn_out_stored")
        s_glt = sem("glu_tanh")
        s_glu = sem("glu_products")
        s_gtp = sem("glu_transposed")
        s_gt = sem("glu_stored")
        s_cv = sem("conv_taps")
        s_mup = sem("ln_sum")
        s_mu = sem("ln_mean")
        s_xc = sem("ln_centred")
        s_lsq = sem("ln_squares")
        s_lvp = sem("ln_square_sums")
        s_var = sem("ln_variance")
        s_std = sem("ln_std")
        s_xn = sem("ln_normalised")
        s_ly = sem("ln_affine")
        s_lt = sem("ln_tanh")
        s_mixb = sem("conv_out_stored")
        s_zp = sem("gates_transposed")
        s_zc = sem("gates_tanh")
        s_z = sem("gates_stored")
        s_mqs = sem("mq_squares")
        s_mqm = sem("mq_mean_squares")
        s_mqr = sem("mq_rstd")
        s_mqk = sem("mq_scales")
        s_mks = sem("mk_scaled")
        s_mqp = sem("mq_transposed")
        s_mqT = sem("mq_stored")
        s_mkp = sem("mk_transposed")
        s_mkT = sem("mk_stored")
        s_scp = sem("mem_scores")
        s_nb = sem("mem_score_maxima")
        s_exp = sem("mem_exps")
        s_pr = sem("mem_probs")
        s_ptp = sem("mem_probs_transposed")
        s_pt = sem("mem_probs_stored")
        s_maop = sem("mem_out_products")
        s_mao = sem("mem_out_stored")
        s_sbs = sem("sb_squares")
        s_sbr = sem("sb_square_sums")
        s_sbm = sem("sb_mean_squares")
        s_sbw = sem("sb_rstd")
        s_sbn = sem("sb_normalised")
        s_sbtp = sem("sb_qk_transposed")
        s_sbT = sem("sb_qk_stored")
        s_sbzp = sem("sb_scores")
        s_sbA = sem("sb_log_terms")
        s_sbsp = sem("sb_softplus")
        s_sbmk = sem("sb_softplus_masked")
        s_sbcp = sem("sb_sums")
        s_sbW = sem("sb_weights")
        s_sbop = sem("sb_out_products")
        s_sbo = sem("sb_out_stored")
        s_actq = sem("scalar_own_steps")
        s_dveq = sem("vector_own_steps")
        s_poolq = sem("gpsimd_own_steps")

        def evac_done(j):
            if j in ADDED:
                return s_evD, ADDED.index(j) + 1
            return s_evA, COPIED.index(j) + 1

        def banks(step, i):
            if step == "xt":
                return [i % 3 if F_MEM <= i < F_OB else i % 4]
            if step in ("mqT", "mkT"):
                return [i % 2]
            if step == "mao":
                return [2 + i % 2]
            if step == "d4y":
                return [] if i % 7 == 0 else ([1, 2] if i % 7 < 6 else [2])
            if step == "lnv":
                return [3] if i == 0 else []
            return {"first": [0], "vec": [0], "ba": [0], "bat": [1], "bas": [2], "dnT": [0, 1], "dnB": [2], "dnR": [1], "dnG": [0, 1],
                    "d4x": [0],
                    "d5a": [0], "d5b": [1], "d5c": [2], "d5d": [0], "d5e": [1], "d7": [2], "gT": [3], "zT": [3],
                    "lnm": [3], "mas": [0], "mat": [1], "sbT": [0], "sbz": [1], "sbo": [2]}.get(step, [])

        def inv_count(i):
            return 7 * (i // 14) + i % 7 + 1

        def read(step, i):
            par = (i // 7) % 2
            return {"first": (s_vt, 1), "vec": (s_vt, 2), "xt": (s_xl, i + 1), "ba": (s_bac, 1), "bat": (s_ba, 1), "bas": (s_gc, 1),
                    "dnT": (s_silu, 2 * i + 2),
                    "dnB": (s_nrm, i + 1), "dnR": (s_rows, i + 1), "dnG": (s_aq, i + 1),
                    "d4x": (s_t[par], inv_count(i)) if i % 7 == 0 else (s_x1[par], 6 * (i // 14) + i % 7),
                    "d4y": (s_t[par], inv_count(i)), "d5a": (s_5a, i + 1), "d5b": (s_5b, i + 1),
                    "d5c": (s_5c, i + 1), "d5d": (s_5d, i + 1), "d5e": (s_5e, i + 1), "d7": (s_mixa, i + 1),
                    "gT": (s_gt, i + 1), "zT": (s_z, i + 1), "lnm": (s_mu, 1), "lnv": (s_var, 1),
                    "mqT": (s_mqT, i + 1), "mkT": (s_mkT, i + 1), "mas": (s_exp, i + 1), "mat": (s_pt, i + 1),
                    "mao": (s_mao, i + 1), "sbT": (s_sbT, i + 1), "sbz": (s_sbW, i + 1),
                    "sbo": (s_sbo, i + 1)}[step]

        last_user, bank_free = {}, {}
        for st, i in [("first", 0)] + plan:
            bank_free[st, i] = [read(*last_user[b]) for b in banks(st, i) if b in last_user]
            for b in banks(st, i):
                last_user[b] = (st, i)

        def slot_jobs(j):
            before = [q for q in PSLOT if q < j and PSLOT[q] == PSLOT[j]]
            if not before:
                return [(s_ss, 1)]
            q = max(before)
            for g in range(2):
                if q == J_GLU[g]:
                    return [(s_gtp, 4 * g + 4)]
                if q == J_GLU[g] + 1:
                    return [(s_glu, g + 1)]
                if q in (J_Q[g], J_K[g], J_V[g]):
                    return [(s_dnT, 4 * g + 4)]
                if q == J_ZA[g]:
                    return [(s_za, g + 1)]
            if q < J_QM:
                return [(s_zp, 4 * (q - J_ZB) + 4)]
            if q < J_ZM:
                return [(s_mqp, 4 * (q - J_QM) + 4), (s_ss, 3)]
            if q < J_OA:
                return [(s_zp, 8 + 4 * (q - J_ZM) + 4), (s_ss, 2)]
            if q < J_ODIN:
                return [(s_mkp, 4 * (q - J_MEM) + 4), (s_scp, 4), (s_ss, 3)]
            g, c = divmod(q - J_ODIN, 4)
            if q >= J_ODIN + 16:
                return []
            return [[(s_sbtp, 4 * g + 4)], [(s_sbtp, 4 * g + 4)], [(s_sbop, 4 * g + 4)], [(s_zp, 16 + 4 * g + 4)]][c]

        def zsource(n):
            if n < 8:
                return J_ZB + n // 4, n // 4, n % 4, 8 + n
            if n < 16:
                return J_ZM + (n - 8) // 4, (n - 8) // 4, n % 4, 16 + n - 8
            if n < 32:
                return J_ODIN + 4 * ((n - 16) // 4) + 3, 3, n % 4, n - 16
            return J_ODIN + 18 + (n - 32) // 4, 2 + (n - 32) // 4, n % 4, 16 + n - 32

        def gain(name, c):
            return vt[:, VCOL[name] + c:VCOL[name] + c + 1]

        def xt_gain(n):
            return (gain("ev_norm_g", n) if n < F_OA else gain("mem_norm_g", n - F_MEM) if n < F_OB
                    else gain("od_norm_g", n - F_H))

        def turned(n):
            return n + 1 if n < F_OA else n - F_MEM + 17 if n < F_OB else n - F_H + 33

        def mix_tile(n):
            return n - F_OA if n < F_MEM else n - F_OB + 8 if n < F_H else n - F_ODD


        def mix_ready(n):
            kt, odd = mix_tile(n), n >= F_H
            if odd and kt < 16:
                return s_sbo, kt + 1
            if kt < 8:
                return s_mixa, kt + 1
            if kt < 16:
                return s_mixb, kt - 7
            return s_mao, 8 * odd + kt - 15

        def halves(m, par, l):
            return m[:, par, :, :].rearrange("p m n -> p (m n)").rearrange("p (b c r) -> p b c r", c=2, r=1 << l)

        def dn_source(c):
            return (M[0][:, S:2 * S], M[0][:, 0:S], M[1][:, 0:S])[c]

        def dn_tile(h, c):
            return (8 + h, h, 16 + h)[c]

        mm = nc.tensor.matmul
        act = nc.scalar.activation
        vec = nc.vector
        MQJOB = [J_QM, J_QM + 1, J_ODIN + 16, J_ODIN + 17, J_MEM, J_MEM + 1]
        MQSLOT = [2, 3, 0, 1, 0, 1]
        order = {0: 1, 1: 2, 4: 3, 5: 4, 2: 5, 3: 6}

        block = ctx.enter_context(nc.Block())

        @block.sync
        def _(sp):
            def load_chunk(c):
                j = JOB_OF[c]
                name, r0, c0, _, _ = JOBS[j]
                r = r0 + 256 * (c - CH0[j])
                if c >= RAWS:
                    sp.wait_ge(s_lo, c - RAWS + 1)
                sp.dma_start(raw[:, c % RAWS, :, :], w[name][r:r + 256, c0:c0 + 512].rearrange("(k p) n -> p k n", p=128)
                             ).then_inc(s_raw[c % RAWS], 16)

            sources = vecs(vrow)
            sp.dma_start(sources[0][0], sources[0][1]).then_inc(s_gain, 16)
            for b in range(FIRST):
                sp.dma_start(hid[:, :, 512 * b:512 * b + 512],
                             x[:, 512 * b:512 * b + 512].rearrange("(t p) d -> p t d", p=128)).then_inc(s_xin[b], 16)
                load_chunk(b)
            for dst, src in sources[1:]:
                sp.dma_start(dst, src).then_inc(s_vrow, 16)
            sp.dma_start(wba, w["ev_in"][:, BA0:BA0 + 16].rearrange("(k p) n -> p k n", p=128),
                         allow_slow_non_contiguous=True).then_inc(s_small, 16)
            sp.dma_start(alog[:, :], a_log.partition_broadcast(128)).then_inc(s_small, 16)
            sp.dma_start(dtb[:, :], dt_bias.partition_broadcast(128)).then_inc(s_small, 16)
            for c in range(FIRST, nch):
                load_chunk(c)
            stores = 0
            for b in range(4):
                j = last_job - 4 + b
                sp.wait_ge(*evac_done(j))
                sp.dma_start(out[:, 512 * b:512 * b + 512].rearrange("(t p) d -> p t d", p=128),
                             hid[:, :, 512 * b:512 * b + 512]).then_inc(s_out, 16)
                stores += 16
            sp.wait_ge(s_out, stores)

        @block.gpsimd
        def _(gp):
            own = [0]

            def link(ins):
                own[0] += 1
                ins.then_inc(s_poolq, 1)
                gp.wait_ge(s_poolq, own[0])

            def keep(t, pattern, base, mult, op, fill):
                link(nc.gpsimd.affine_select(out=t, in_=t, compare_op=op, fill=fill, base=base,
                                             pattern=pattern, channel_multiplier=mult))

            link(nc.gpsimd.memset(ident[:, :], 0.0))
            nc.gpsimd.affine_select(out=ident[:, :], in_=ident[:, :], compare_op=ALU.not_equal, fill=1.0, base=0,
                                    pattern=[[-1, 128]], channel_multiplier=1).then_inc(s_const, 1)
            for t, v in ((identb, 0.0), (ones, 1.0), (negones, -1.0), (upto, 1.0), (negfrom, -1.0), (after01, 1.0),
                         (mhalf, -0.5)):
                link(nc.gpsimd.memset(t[:, :], v))
            link(nc.gpsimd.memset(shut[:, :, :], 0.0))
            link(nc.gpsimd.memset(level, 0.0))
            keep(identb[:, :], [[-1, 128]], 0, 1, ALU.not_equal, 1.0)
            keep(upto[:, :], [[1, 128]], 0, -1, ALU.is_ge, 0.0)
            keep(negfrom[:, :], [[-1, 128]], 0, 1, ALU.is_ge, 0.0)
            keep(shut[:, 0, :], [[1, 128]], 0, -1, ALU.is_gt, NEG)
            keep(shut[:, 1, :], [[1, 128]], 0, -1, ALU.is_ge, NEG)
            for l in range(7):
                h = 1 << l
                nb = 64 // h
                v = level[:, l, :].rearrange("p (b c r) -> p b c r", b=nb, c=2)[:, :, 1, :]
                link(nc.gpsimd.memset(v, 1.0))
                keep(v, [[-2 * h, nb], [0, h]], 0, 1, ALU.is_ge, 0.0)
                keep(v, [[2 * h, nb], [0, h]], h - 1, -1, ALU.is_ge, 0.0)
            nc.gpsimd.affine_select(out=after01[:, :], in_=after01[:, :], compare_op=ALU.is_gt, fill=0.0, base=0,
                                    pattern=[[1, 128]], channel_multiplier=-1).then_inc(s_const, 1)
            gp.wait_ge(s_const, 2)

            def power(out_, in_, n, done):
                nc.gpsimd.tensor_tensor(out_, in_, mhalf[:, 0:n], ALU.pow).then_inc(done, 1)

            def do_rstd(src):
                gp.wait_ge(s_ms, src + 1)
                power(rstd[:, src, :], ssq[:, src, :], T, s_rstd)

            def do_dnB(h):
                gp.wait_ge(s_silu, 2 * h + 2)
                if h:
                    gp.wait_ge(s_np, h)
                k = ykqv[:, h % 4, 0:2, :]
                nc.gpsimd.tensor_tensor(scr[:, 0:512].rearrange("p (c s) -> p c s", c=2), k, k, ALU.mult).then_inc(s_sq, 1)

            def do_dnG(h):
                g, hl = h // 4, h % 4
                gp.wait_ge(s_tok, h + 1)
                gp.wait_ge(s_ex, g + 1)
                gp.wait_ge(s_baD, 2)
                for c, f in ((0, ex[:, g, 1, 2 * hl:2 * hl + 1]), (1, halfb[:, 0, h:h + 1]), (2, halfb[:, 1, h:h + 1])):
                    ins = nc.gpsimd.tensor_scalar(tok[:, hl, c, :], tok[:, hl, c, :], f, 1.0, ALU.mult, ALU.mult)
                ins.then_inc(s_tks, 1)

            def do_d4x(i):
                pr, l = divmod(i, 7)
                g, par = divmod(pr, 2)
                if l == 0:
                    gp.wait_ge(s_aq, 4 * g + 2 * par + 2)
                    if g:
                        gp.wait_ge(s_5dp, 4 * (g - 1) + 2 * par + 2)
                else:
                    gp.wait_ge(s_t[par], 7 * g + l)
                nc.gpsimd.tensor_tensor(ofx[:, par, :, :], aq[:, 4 * par:4 * par + 4, 0, :],
                                        level[:, l, :].unsqueeze(1).broadcast_to([128, 4, 128]), ALU.mult
                                        ).then_inc(s_of[par], 1)

            def do_d6(g):
                gp.wait_ge(s_oms, g + 1)
                power(oms[:, g, :], oms[:, g, :], 8, s_opw)

            def mq_power(i, n):
                gp.wait_ge(s_mqm, n)
                power(qss[:, i, :], qss[:, i, :], 4, s_mqr)

            def do_sbn(g):
                gp.wait_ge(s_sbm, g + 1)
                power(brs[:, g, :], bss[:, g, :], 16, s_sbw)
                gp.wait_ge(s_sbw, g + 1)
                for c in range(2):
                    v = pflat[:, 1024 * c:1024 * c + 1024].rearrange("p (a n) -> p a n", n=128)
                    nc.gpsimd.tensor_tensor(v, v, brs[:, g, 8 * c:8 * c + 8].unsqueeze(2).broadcast_to([128, 8, 128]),
                                            ALU.mult).then_inc(s_sbn, 1)

            def do_sbz(h):
                gp.wait_ge(s_sbsp, h + 1)
                v = spz.rearrange("p (a n) -> p a n", a=3)[:, 0:3:2, :]
                nc.gpsimd.tensor_tensor(v, v, after01[:, :].unsqueeze(1).broadcast_to([128, 2, 128]), ALU.mult
                                        ).then_inc(s_sbmk, 1)

            steps = {"rstd": do_rstd, "dnB": do_dnB, "dnG": do_dnG, "d4x": do_d4x, "d6": do_d6, "sbn": do_sbn,
                     "sbz": do_sbz, "mqs": lambda i: mq_power(i, order[i]), "mks": lambda i: mq_power(4 + i, order[4 + i])}
            for st, i in plan:
                if st in steps:
                    steps[st](i)

        @block.scalar
        def _(sc):
            own = [0]

            def link(ins):
                own[0] += 1
                ins.then_inc(s_actq, 1)
                sc.wait_ge(s_actq, own[0])

            def split(c):
                sc.wait_ge(s_raw[c % RAWS], 16 * (c // RAWS + 1))
                if c >= RING:
                    sc.wait_ge(s_pe, c - RING + 1)
                if c == 2 * RING - 1:
                    sc.wait_ge(s_bap, 1)
                act(whi[:, c % RING, :, :], raw[:, c % RAWS, :, :], ACT.Copy).then_inc(s_hi, 1)

            def do_vec(_):
                sc.wait_ge(s_vp, 2)
                act(vt[:, 16:NVEC], M[0][:, 16:NVEC], ACT.Copy)
                for a, n in ((1, 96), (2, 128), (3, 120)):
                    ins = act(vt[:, 128 * a:128 * a + n], M[0][:, 128 * a:128 * a + n], ACT.Copy)
                ins.then_inc(s_vt, 1)
                sc.wait_ge(s_vt, 2)
                act(qgain[:, :], gain("od_q_norm_c", 0), ACT.Copy, scale=128.0 ** -0.5)

            def do_evac(j):
                if j in ADDED:
                    return
                src = 0 if j < J_OA else 1 if j < J_OB else 2
                sc.wait_ge(s_rstd, src + 1)
                sc.wait_ge(s_pe, CH0[j + 1])
                if j in PSLOT:
                    for q in slot_jobs(j):
                        sc.wait_ge(*q)
                else:
                    sc.wait_ge(s_ss, 2)
                for t in range(T):
                    if j in PSLOT:
                        dst = proj[:, PSLOT[j], t, :]
                    else:
                        dst = vm[:, t, 512 * (j - J_MEM - 2):512 * (j - J_MEM - 2) + 512]
                    ins = act(dst, pj[j % 2][t][:, :], ACT.Copy, scale=rstd[:, src, t:t + 1])
                ins.then_inc(evac_done(j)[0], 1)

            def fill_wait(n):
                if chunks_before_fill(n):
                    sc.wait_ge(s_pe, chunks_before_fill(n))

            def do_xt(n):
                sc.wait_ge(s_xp, turned(n))
                fill_wait(n)
                act(xhi[:, SLOT[n], :], M[banks("xt", n)[0]][:, 0:S], ACT.Copy, scale=xt_gain(n)).then_inc(s_xh, 1)

            def do_mf(n):
                sc.wait_ge(*mix_ready(n))
                fill_wait(n)
                act(xhi[:, SLOT[n], :], mix[:, mix_tile(n), :], ACT.Copy).then_inc(s_xh, 1)

            def do_rstd(src):
                if src == 0:
                    for b in range(4):
                        sc.wait_ge(s_xin[b], 16)
                elif src == 1:
                    sc.wait_ge(s_min, 64)
                    sc.wait_ge(s_zp, 16)
                else:
                    sc.wait_ge(*evac_done(J_ODIN - 1))
                    sc.wait_ge(s_scp, 4)
                o = 0 if src == 1 else 2048
                link(act(pflat[:, 0:2048], (memx if src == 1 else hid)[:, 0, :], ACT.Square, accum_out=ssq[:, src, 0:1]))
                ins = act(pflat[:, o:o + 2048], (memx if src == 1 else hid)[:, 1, :], ACT.Square, accum_out=ssq[:, src, 1:2])
                ins.then_inc(s_ss, 1)

            def do_baw(_):
                sc.wait_ge(s_small, 48)
                sc.wait_ge(s_pe, RING)
                act(bah, wba, ACT.Copy).then_inc(s_wbh, 1)

            def do_ba(_):
                sc.wait_ge(s_bap, 1)
                act(bar, M[0][0:16, 0:S], ACT.Copy).then_inc(s_bac, 1)

            def do_bat(_):
                sc.wait_ge(s_batp, 1)
                sc.wait_ge(s_rstd, 1)
                for t in range(T):
                    ins = act(ba[:, t, :], M[1][:, 16 * t:16 * t + 16], ACT.Copy, scale=rstd[:, 0, t:t + 1])
                ins.then_inc(s_ba, 1)
                sc.wait_ge(s_ba, 1)
                act(beta[:, :, :], ba[:, :, 0:H_DN], ACT.Tanh, scale=0.5).then_inc(s_baA, 1)
                link(act(alog[:, :], alog[:, :], ACT.Exp))
                sc.wait_ge(s_baD, 1)
                link(act(ge[:, :, :], gu[:, :, :], ACT.Abs))
                link(act(ge[:, :, :], ge[:, :, :], ACT.Exp, scale=-1.0))
                sc.wait_ge(s_baD, 2)
                act(ge[:, :, :], ge[:, :, :], ACT.Ln, bias=1.0)
                act(lnb[:, :, :], beta[:, :, :], ACT.Ln).then_inc(s_baA, 1)

            def do_za(g):
                sc.wait_ge(*evac_done(J_ZA[g]))
                act(za[:, :, 512 * g:512 * g + 512], proj[:, PSLOT[J_ZA[g]], :, :], ACT.Tanh, scale=0.5).then_inc(s_zat, 1)

            def do_dnC(h):
                sc.wait_ge(s_dnT, h + 1)
                if h >= 4:
                    sc.wait_ge(s_5cp, h - 3)
                for c in range(3):
                    col = V_CONV + 24 * (CONV - 1) + dn_tile(h, c)
                    ins = act(ykqv[:, h % 4, c, :], dn_source(c), ACT.Copy, scale=vt[:, col:col + 1])
                ins.then_inc(s_tap, 1)

            def do_dnS(h):
                sc.wait_ge(s_cv4, 9 * h + 9)
                y = ykqv[:, h % 4, :, :]
                act(M[0][:, :].rearrange("p (c s) -> p c s", c=2), y[:, 0:2, :], ACT.Tanh, scale=0.5)
                act(M[1][:, 0:S], y[:, 2, :], ACT.Tanh, scale=0.5).then_inc(s_th, 1)

            def do_dnB(h):
                sc.wait_ge(s_back, h + 1)
                if h >= 4:
                    sc.wait_ge(s_owp, h - 3)
                sc.wait_ge(s_ss, 1)
                act(tok[:, h % 4, :, :], M[2][:, 0:384].rearrange("p (c n) -> p c n", c=3), ACT.Copy).then_inc(s_tok, 1)

            def do_dnV(g):
                sc.wait_ge(s_lnq, 2 * g + 1)
                act(hln[:, g, :, :], hln[:, g, :, :], ACT.Ln).then_inc(s_lnq, 1)
                sc.wait_ge(s_ei, g + 1)
                act(ex[:, g, :, :], ei[:, g, :, :], ACT.Exp).then_inc(s_ex, 1)

            def do_dnG(h):
                g, hl = h // 4, h % 4
                sc.wait_ge(s_gp, h + 1)
                if h >= 4:
                    sc.wait_ge(s_5ep, h - 3)
                for t in range(T):
                    ins = act(aq[:, 2 * hl + t, :, :], M[1][:, 256 * t:256 * t + 256].rearrange("p (c n) -> p c n", c=2),
                              ACT.Exp, bias=cc[:, g, hl, t:t + 1])
                ins.then_inc(s_eq, 1)

            def do_d4x(i):
                pr, l = divmod(i, 7)
                g, par = divmod(pr, 2)
                if l:
                    sc.wait_ge(s_x1p[par], 7 * g + l + 1)
                    act(ofx[:, par, :, :], M[0][:, :].rearrange("p (m n) -> p m n", m=4), ACT.Copy).then_inc(s_x1[par], 1)

            def do_d5a(h):
                sc.wait_ge(s_5ap, h + 1)
                act(dw[h % 2][:, 0, :], M[0][:, 0:128], ACT.Copy).then_inc(s_5a, 1)

            def do_d5b(h):
                sc.wait_ge(s_5bp, h + 1)
                if h > 1:
                    sc.wait_ge(s_oss, h - 1)
                act(dw[h % 2][:, 1, :], M[1][:, 0:128], ACT.Copy)
                act(tok[:, h % 4, 0, :], M[1][:, 128:256], ACT.Copy).then_inc(s_5b, 1)

            def do_d5c(h):
                g, hl = h // 4, h % 4
                sc.wait_ge(s_5cp, h + 1)
                if h > 1:
                    sc.wait_ge(s_5e, h - 1)
                act(dw[h % 2][:, 3, :], M[2][:, 128:256], ACT.Copy, scale=ex[:, g, 2, 2 * hl + 1:2 * hl + 2]).then_inc(s_5cA, 1)

            def do_d5d(h):
                sc.wait_ge(s_5dp, h + 1)
                act(dw[h % 2][:, 2, :], M[0][:, 0:128], ACT.Copy).then_inc(s_5d, 1)

            def do_d5e(h):
                g, hl = h // 4, h % 4
                sc.wait_ge(s_5e, h + 1)
                for t in range(T):
                    ins = act(dw[h % 2][:, 1 + t, :], tok[:, hl, t, :], ACT.Square, accum_out=oss[:, g, 2 * hl + t:2 * hl + t + 1])
                ins.then_inc(s_oss, 1)

            def do_d7(h):
                sc.wait_ge(s_owp, h + 1)
                act(mix[:, h, :], M[2][:, 0:S], ACT.Copy, scale=gain("ev_dn_norm_g", 0)).then_inc(s_mixa, 1)

            def do_glu(i):
                sc.wait_ge(*evac_done(J_GLU[i] + 1))
                b = proj[:, PSLOT[J_GLU[i] + 1], :, :]
                act(b, b, ACT.Tanh, scale=0.5).then_inc(s_glt, 1)

            def do_gT(ct):
                sc.wait_ge(s_gtp, ct + 1)
                act(cvr[:, ct + 2, :], M[3][:, 0:S], ACT.Copy, scale=0.5).then_inc(s_gt, 1)

            def do_lnm(_):
                sc.wait_ge(s_mup, 1)
                sc.wait_ge(s_mqs, 2)
                act(scr[:, 0:S], M[3][:, 0:S], ACT.Copy, scale=1.0 / CVW).then_inc(s_mu, 1)

            def do_lnv(ct):
                sc.wait_ge(s_xc, 1)
                if ct >= 2:
                    sc.wait_ge(s_lvp, ct - 1)
                act(cvr[:, 8 + ct % 2, :], cvr[:, ct, :], ACT.Square).then_inc(s_lsq, 1)

            def do_lnr(_):
                sc.wait_ge(s_var, 1)
                act(scr[:, S:2 * S], scr[:, S:2 * S], ACT.Sqrt).then_inc(s_std, 1)

            def do_lno(ct):
                sc.wait_ge(s_ly, ct + 1)
                if ct >= 2:
                    sc.wait_ge(s_mixb, ct - 1)
                act(cvr[:, 8 + ct % 2, :], cvr[:, ct, :], ACT.Tanh, scale=0.5).then_inc(s_lt, 1)

            def do_zT(n):
                kt = zsource(n)[3]
                sc.wait_ge(s_zp, n + 1)
                if n < 8:
                    sc.wait_ge(s_t[0], 14)
                    sc.wait_ge(s_t[1], 14)
                elif n < 16:
                    sc.wait_ge(s_ow, 16)
                elif n == 16:
                    sc.wait_ge(s_xl, F_OM)
                elif n == 32:
                    sc.wait_ge(s_xl, F_H)
                act(mix[:, kt, :], M[3][:, 0:S], ACT.Copy)
                act(M[3][:, S:2 * S], M[3][:, 0:S], ACT.Tanh, scale=0.5).then_inc(s_zc, 1)

            def squares(i):
                sc.wait_ge(*evac_done(MQJOB[i]))
                if i == 2:
                    sc.wait_ge(s_sbcp, 16)
                if i == 4:
                    sc.wait_ge(s_xn, 1)
                if order[i] > 1:
                    sc.wait_ge(s_mqs, order[i] - 1)
                for t in range(T):
                    for hd in range(2):
                        ins = act(scr[:, 256 * (2 * t + hd):256 * (2 * t + hd) + 256],
                                  proj[:, MQSLOT[i], t, 256 * hd:256 * hd + 256], ACT.Square,
                                  accum_out=qss[:, i, 2 * t + hd:2 * t + hd + 1])
                ins.then_inc(s_mqs, 1)

            def do_mqT(dt):
                sc.wait_ge(s_mqp, dt + 1)
                sc.wait_ge(*((s_mkp, 8) if dt < 8 else (s_sbzp, 16)))
                act(qmt[dt // 8][:, dt % 8, :], M[dt % 2][:, 0:S], ACT.Copy,
                    scale=gain("ev_q_norm_m" if dt < 8 else "od_q_norm_m", dt % 2)).then_inc(s_mqT, 1)

            def do_mkT(dt):
                sc.wait_ge(s_mkp, dt + 1)
                sc.wait_ge(s_ss, 2)
                act(kmt[:, dt, :], M[dt % 2][:, 0:S], ACT.Copy, scale=gain("mem_k_norm_g", dt % 2)).then_inc(s_mkT, 1)

            def do_mas(n):
                i, hd2 = 2 * (n // 4) + (n % 4) // 2, n % 2
                sc.wait_ge(s_nb, n + 1)
                if n:
                    sc.wait_ge(s_ptp, n)
                for t in range(T):
                    ins = act(prob[:, t, :], M[0][:, 256 * t:256 * t + 256], ACT.Exp, bias=snb[:, n, t:t + 1],
                              scale=qrs[:, i, 2 * t + hd2:2 * t + hd2 + 1], accum_out=ssm[:, n, t:t + 1])
                ins.then_inc(s_exp, 1)

            def do_mat(n):
                sc.wait_ge(s_ptp, n + 1)
                if n:
                    sc.wait_ge(s_maop, 2 * n)
                act(probt, M[1][:, :].rearrange("p (m s) -> p m s", m=2), ACT.Copy).then_inc(s_pt, 1)

            def do_sbn(g):
                for c in range(2):
                    sc.wait_ge(*evac_done(J_ODIN + 4 * g + c))
                    if 2 * g + c:
                        sc.wait_ge(s_sbr, 2 * g + c)
                    else:
                        sc.wait_ge(s_maop, 8)
                    if g:
                        sc.wait_ge(s_sbcp, 4 * g)
                    act(scr[:, :], pflat[:, 1024 * c:1024 * c + 1024], ACT.Square).then_inc(s_sbs, 1)

            def do_tab(_):
                sc.preload_act_table_set("natural_log_exp_and_others")

            def do_sbT(h):
                sc.wait_ge(s_sbtp, h + 1)
                if h >= 4:
                    sc.wait_ge(s_sbzp, h - 3)
                else:
                    sc.wait_ge(s_mixb, 8)
                act(qk[:, h % 4, 0, :], M[0][:, 0:S], ACT.Copy, scale=qgain[:, 0:1])
                act(qk[:, h % 4, 1, :], M[0][:, S:2 * S], ACT.Copy, scale=gain("od_k_norm_c", 0)).then_inc(s_sbT, 1)

            def do_sbz(h):
                sc.wait_ge(s_sbzp, h + 1)
                sc.wait_ge(s_sbr, 2 * (h // 4) + 2)
                if h:
                    sc.wait_ge(s_sbsp, h)
                link(act(absz, M[1][:, 0:384], ACT.Abs))
                link(act(absz, absz, ACT.Exp, scale=-1.0))
                act(absz, absz, ACT.Ln, bias=1.0).then_inc(s_sbA, 1)

            def do_sbc(h):
                sc.wait_ge(s_sbcp, h + 1)
                if h:
                    sc.wait_ge(s_sbop, h)
                act(wts, M[1][:, 0:384], ACT.Exp).then_inc(s_sbW, 1)

            def do_mload(b):
                sc.wait_ge(s_5cp, 8)
                sc.wait_ge(s_5dp, 8)
                sc.dma_start(memx[:, :, 512 * b:512 * b + 512],
                             mem[:, 512 * b:512 * b + 512].rearrange("(t p) d -> p t d", p=128)).then_inc(s_min, 16)

            def do_xload(b):
                sc.wait_ge(s_mixa, 8)
                sc.dma_start(hid[:, :, 512 * b:512 * b + 512],
                             x[:, 512 * b:512 * b + 512].rearrange("(t p) d -> p t d", p=128)).then_inc(s_xre, 16)

            steps = {"split": split, "evac": do_evac, "xt": do_xt, "mf": do_mf, "rstd": do_rstd,
                     "baw": do_baw, "ba": do_ba, "bat": do_bat,
                     "za": do_za, "dnC": do_dnC, "dnS": do_dnS, "dnB": do_dnB, "dnV": do_dnV, "dnG": do_dnG, "d4x": do_d4x,
                     "d5a": do_d5a, "d5b": do_d5b, "d5c": do_d5c, "d5d": do_d5d, "d5e": do_d5e, "d7": do_d7,
                     "glu": do_glu, "gT": do_gT, "lnm": do_lnm, "lnv": do_lnv, "lnr": do_lnr, "lno": do_lno,
                     "zT": do_zT, "mqs": squares, "mks": lambda i: squares(4 + i), "mqT": do_mqT, "mkT": do_mkT,
                     "mas": do_mas, "mat": do_mat, "sbn": do_sbn, "tab": do_tab, "sbT": do_sbT, "sbz": do_sbz,
                     "sbc": do_sbc, "mload": do_mload, "xload": do_xload, "vec": do_vec}
            sc.wait_ge(s_vp, 1)
            act(vt[:, 0:16], M[0][:, 0:16], ACT.Copy).then_inc(s_vt, 1)
            sc.wait_ge(s_vt, 1)
            for st, i in plan:
                if st in steps:
                    steps[st](i)

        @block.vector
        def _(ve):
            own = [0]

            def link(ins):
                own[0] += 1
                ins.then_inc(s_dveq, 1)
                ve.wait_ge(s_dveq, own[0])

            def split(c):
                ve.wait_ge(s_hi, c + 1)
                vec.tensor_tensor(wlo[:, c % RING, :, :], raw[:, c % RAWS, :, :], whi[:, c % RING, :, :].bitcast(F32),
                                  ALU.subtract).then_inc(s_lo, 1)

            def do_evac(j):
                if j in COPIED:
                    return
                b = JOBS[j][2] // 512
                ve.wait_ge(s_pe, CH0[j + 1])
                ve.wait_ge(s_xre, 64)
                if evac_done(j)[1] > 1:
                    ve.wait_ge(s_evD, evac_done(j)[1] - 1)
                if j == J_ODOUT:
                    ve.wait_ge(s_xp, turned(F_H + KT - 1))
                    ve.wait_ge(s_ss, 3)
                for t in range(T):
                    v = hid[:, t, 512 * b:512 * b + 512]
                    ins = vec.tensor_tensor(v, v, pj[j % 2][t][:, :], ALU.add)
                ins.then_inc(s_evD, 1)

            def do_xt(n):
                ve.wait_ge(s_xh, n + 1)
                vec.scalar_tensor_tensor(out=xlo[:, SLOT[n], :], in0=M[banks("xt", n)[0]][:, 0:S], scalar=xt_gain(n),
                                         in1=xhi[:, SLOT[n], :].bitcast(F32), op0=ALU.mult, op1=ALU.subtract
                                         ).then_inc(s_xl, 1)

            def do_mf(n):
                ve.wait_ge(s_xh, n + 1)
                vec.tensor_tensor(xlo[:, SLOT[n], :], mix[:, mix_tile(n), :],
                                  xhi[:, SLOT[n], :].bitcast(F32), ALU.subtract).then_inc(s_xl, 1)

            def do_rstd(src):
                ve.wait_ge(s_ss, src + 1)
                vec.tensor_scalar(ssq[:, src, :], ssq[:, src, :], 1.0 / D, EPS, ALU.mult, ALU.add).then_inc(s_ms, 1)

            def do_baw(_):
                ve.wait_ge(s_wbh, 1)
                vec.tensor_tensor(bal, wba, bah.bitcast(F32), ALU.subtract).then_inc(s_wbl, 1)

            def do_bat(_):
                ve.wait_ge(s_ba, 1)
                ve.wait_ge(s_small, 48)
                vec.tensor_tensor(gu[:, :, :], ba[:, :, H_DN:2 * H_DN],
                                  dtb[:, :].unsqueeze(1).broadcast_to([128, T, H_DN]), ALU.add).then_inc(s_baD, 1)
                ve.wait_ge(s_baA, 1)
                link(vec.tensor_scalar(beta[:, :, :], beta[:, :, :], 0.5, 0.5, ALU.mult, ALU.add))
                link(vec.tensor_scalar(beta[:, :, :], beta[:, :, :], 1e-18, None, ALU.max))
                vec.tensor_scalar(halfb[:, :, :], beta[:, :, :], 0.5, None, ALU.mult).then_inc(s_baD, 1)
                ve.wait_ge(s_baA, 2)
                link(vec.scalar_tensor_tensor(out=ge[:, :, :], in0=gu[:, :, :], scalar=0.0, in1=ge[:, :, :],
                                              op0=ALU.max, op1=ALU.add))
                vec.scalar_tensor_tensor(out=gl_in[:, :, :], in0=ge[:, :, :], scalar=-1.0,
                                         in1=alog[:, :].unsqueeze(1).broadcast_to([128, T, H_DN]),
                                         op0=ALU.mult, op1=ALU.mult).then_inc(s_baD, 1)

            def do_bas(_):
                ve.wait_ge(s_gcp, 1)
                vec.tensor_copy(gcl[:, :, :, :].rearrange("p a t h -> p (a t h)"), M[2][:, 0:32]).then_inc(s_gc, 1)

            def do_za(g):
                ve.wait_ge(s_zat, g + 1)
                v = za[:, :, 512 * g:512 * g + 512]
                vec.scalar_tensor_tensor(out=v, in0=v, scalar=1.0, in1=proj[:, PSLOT[J_ZA[g]], :, :], op0=ALU.add, op1=ALU.mult
                                         ).then_inc(s_za, 1)

            def do_dnC(h):
                ve.wait_ge(s_tap, h + 1)
                n = 9 * h
                for r in range(1, CONV):
                    for c in range(3):
                        y = ykqv[:, h % 4, c, :]
                        col = V_CONV + 24 * (CONV - 1 - r) + dn_tile(h, c)
                        if r > 1:
                            ve.wait_ge(s_cv4, n + 1 - 3)
                        vec.scalar_tensor_tensor(out=y[:, r:], in0=dn_source(c)[:, 0:S - r], scalar=vt[:, col:col + 1],
                                                 in1=y[:, r:], op0=ALU.mult, op1=ALU.add).then_inc(s_cv4, 1)
                        n += 1

            def do_dnU(h):
                ve.wait_ge(s_th, h + 1)
                y = ykqv[:, h % 4, :, :]
                vec.scalar_tensor_tensor(out=y[:, 0:2, :], in0=M[0][:, :].rearrange("p (c s) -> p c s", c=2), scalar=1.0,
                                         in1=y[:, 0:2, :], op0=ALU.add, op1=ALU.mult).then_inc(s_silu, 1)
                vec.scalar_tensor_tensor(out=y[:, 2, :], in0=M[1][:, 0:S], scalar=1.0, in1=y[:, 2, :],
                                         op0=ALU.add, op1=ALU.mult).then_inc(s_silu, 1)

            def do_dnB(h):
                ve.wait_ge(s_np, h + 1)
                ve.wait_ge(s_tok, h + 1)
                vec.tensor_copy(nrm[:, h, :], M[2][:, 384:388]).then_inc(s_nrm, 1)

            def do_dnV(g):
                hs = slice(4 * g, 4 * g + 4)
                ve.wait_ge(s_nrm, 4 * g + 4)
                vec.tensor_scalar(hln[:, g, :, :], nrm[:, hs, :], 4 * EPS, None, ALU.add).then_inc(s_lnq, 1)
                ve.wait_ge(s_lnq, 2 * g + 2)
                ve.wait_ge(s_gc, 1)
                ve.wait_ge(s_baA, 2)
                link(vec.tensor_scalar(hln[:, g, :, :], hln[:, g, :, :], -0.5, None, ALU.mult))
                lk, lq = hln[:, g, :, 0:2], hln[:, g, :, 2:4]
                gc = gcl[:, 0, :, hs].rearrange("p t h -> p h t")
                gl = gcl[:, 1, :, hs].rearrange("p t h -> p h t")
                lb = lnb[:, :, hs].rearrange("p t h -> p h t")

                def e(a):
                    return ei[:, g, a, :].rearrange("p (h t) -> p h t", h=4)
                vec.tensor_tensor(cc[:, g, :, :], lk, gc, ALU.subtract)
                link(vec.tensor_tensor(e(0), lk, gc, ALU.add))
                vec.tensor_tensor(e(0), e(0), lb, ALU.add)
                vec.tensor_tensor(e(1), cc[:, g, :, :], gl, ALU.add)
                vec.tensor_copy(e(2), gc)
                vec.tensor_scalar(e(3), lq, -0.5 * math.log(128.0), None, ALU.add).then_inc(s_ei, 1)

            def do_dnR(g):
                ve.wait_ge(s_rp, g + 1)
                vec.tensor_copy(rows[:, g, :], M[1][0:24, 0:128]).then_inc(s_rows, 1)
                ve.wait_ge(s_ex, g + 1)
                link(vec.tensor_scalar(nks[:, g, :], ex[:, g, 0, :], -1.0, None, ALU.mult))

            def do_dnG(h):
                ve.wait_ge(s_eq, h + 1)
                v = aq[:, 2 * (h % 4):2 * (h % 4) + 2, :, :].rearrange("p m c n -> p (m c n)")
                vec.tensor_tensor(v, M[0][:, :], v, ALU.mult).then_inc(s_aq, 1)

            def do_d4x(i):
                pr, l = divmod(i, 7)
                g, par = divmod(pr, 2)
                if l == 0:
                    ve.wait_ge(s_x1p[par], 7 * g + 1)
                    eye = ident[:, :].unsqueeze(1).broadcast_to([128, 4, 128])
                    vec.tensor_tensor(tinv[:, par, :, :], eye, M[0][:, :].rearrange("p (m n) -> p m n", m=4), ALU.subtract)
                    vec.tensor_tensor(tinvt[:, par, :, :], eye, ofx[:, par, :, :], ALU.subtract).then_inc(s_t[par], 1)

            def do_d4y(i):
                pr, l = divmod(i, 7)
                g, par = divmod(pr, 2)
                if l == 0:
                    return
                ve.wait_ge(s_x2p[par], 6 * g + l)
                ve.wait_ge(s_t[par], 7 * g + l)
                t0, t1 = halves(tinv, par, l)[:, :, 0, :], halves(tinvt, par, l)[:, :, 1, :]
                m1, m2 = (M[b][:, 0:256].rearrange("p (b r) -> p b r", r=1 << l) for b in (1, 2))
                if l < 6:
                    vec.tensor_tensor(t0, t0, m1, ALU.subtract)
                vec.tensor_tensor(t1, t1, m2, ALU.subtract).then_inc(s_t[par], 1)

            def do_d5c(h):
                g, hl = h // 4, h % 4
                ve.wait_ge(s_5cA, h + 1)
                ve.wait_ge(s_tks, h + 1)
                vec.scalar_tensor_tensor(out=tok[:, hl, 2, :], in0=M[2][:, 0:128], scalar=nks[:, g, 2 * hl + 1:2 * hl + 2],
                                         in1=tok[:, hl, 2, :], op0=ALU.mult, op1=ALU.add).then_inc(s_5c, 1)

            def do_d5e(h):
                ve.wait_ge(s_5ep, h + 1)
                vec.tensor_tensor(tok[:, h % 4, 1, :], dw[h % 2][:, 3, :], M[1][:, 0:128], ALU.add).then_inc(s_5e, 1)

            def do_d6(g):
                ve.wait_ge(s_oss, 4 * g + 4)
                sq = ex[:, g, 3, :]
                link(vec.tensor_tensor(oms[:, g, :], oss[:, g, :], sq, ALU.mult))
                link(vec.tensor_tensor(oms[:, g, :], oms[:, g, :], sq, ALU.mult))
                vec.tensor_scalar(oms[:, g, :], oms[:, g, :], 1.0 / 128, EPS, ALU.mult, ALU.add).then_inc(s_oms, 1)
                ve.wait_ge(s_opw, g + 1)
                vec.scalar_tensor_tensor(out=ofac[:, g, :], in0=oms[:, g, :], scalar=0.5, in1=sq, op0=ALU.mult,
                                         op1=ALU.mult).then_inc(s_of6, 1)

            def do_gate(h):
                g, hl = h // 4, h % 4
                ve.wait_ge(s_of6, g + 1)
                ve.wait_ge(s_za, g + 1)
                for t in range(T):
                    v = tok[:, hl, t, :]
                    vec.scalar_tensor_tensor(out=v, in0=v, scalar=ofac[:, g, 2 * hl + t:2 * hl + t + 1],
                                             in1=za[:, t, 128 * h:128 * h + 128], op0=ALU.mult, op1=ALU.mult
                                             ).then_inc(s_ow, 1)

            def do_glu(i):
                ve.wait_ge(s_glt, i + 1)
                a = proj[:, PSLOT[J_GLU[i]], :, :]
                vec.scalar_tensor_tensor(out=a, in0=proj[:, PSLOT[J_GLU[i] + 1], :, :], scalar=1.0, in1=a, op0=ALU.add,
                                         op1=ALU.mult).then_inc(s_glu, 1)

            def do_conv(i):
                pr, q = divmod(i, 16)
                for k in range(4 * q, min(4 * q + 4, 2 * TAPS)):
                    d, ct = k // 2, 2 * pr + k % 2
                    n = 2 * TAPS * pr + k
                    c, gsrc = cvr[:, ct, :], cvr[:, ct + 2, :]
                    col = V_DW + 8 * (TAPS - 1 - d) + ct
                    if d == 0:
                        if pr:
                            ve.wait_ge(s_cv, 2 * TAPS * pr)
                        ve.wait_ge(s_gt, ct + 1)
                        ins = vec.tensor_scalar(c, gsrc, vt[:, col:col + 1], gain("ev_dw_b", ct), ALU.mult, ALU.add)
                    else:
                        ve.wait_ge(s_cv, n - 1)
                        ins = vec.scalar_tensor_tensor(out=c[:, d:], in0=gsrc[:, 0:S - d], scalar=vt[:, col:col + 1],
                                                       in1=c[:, d:], op0=ALU.mult, op1=ALU.add)
                    ins.then_inc(s_cv, 1)

            def do_lnm(_):
                ve.wait_ge(s_mu, 1)
                v = cvr[:, 0:8, :]
                vec.tensor_tensor(v, v, scr[:, 0:S].unsqueeze(1).broadcast_to([128, 8, S]), ALU.subtract).then_inc(s_xc, 1)

            def do_lnr(_):
                ve.wait_ge(s_lvp, 8)
                r = scr[:, S:2 * S]
                vec.tensor_scalar(r, M[3][:, 0:S], 1.0 / CVW, EPS, ALU.mult, ALU.add).then_inc(s_var, 1)
                ve.wait_ge(s_std, 1)
                link(vec.reciprocal(r, r))
                v = cvr[:, 0:8, :]
                vec.tensor_tensor(v, v, r.unsqueeze(1).broadcast_to([128, 8, S]), ALU.mult).then_inc(s_xn, 1)

            def do_lno(ct):
                ve.wait_ge(s_xn, 1)
                c = cvr[:, ct, :]
                vec.tensor_scalar(c, c, gain("ev_ln_g", ct), gain("ev_ln_b", ct), ALU.mult, ALU.add).then_inc(s_ly, 1)
                ve.wait_ge(s_lt, ct + 1)
                ve.wait_ge(s_z, ct + 1)
                link(vec.scalar_tensor_tensor(out=c, in0=cvr[:, 8 + ct % 2, :], scalar=1.0, in1=c, op0=ALU.add, op1=ALU.mult))
                v = mix[:, 8 + ct, :]
                vec.scalar_tensor_tensor(out=v, in0=c, scalar=0.25, in1=v, op0=ALU.mult, op1=ALU.mult).then_inc(s_mixb, 1)

            def do_zT(n):
                ve.wait_ge(s_zc, n + 1)
                v = mix[:, zsource(n)[3], :]
                vec.scalar_tensor_tensor(out=v, in0=M[3][:, S:2 * S], scalar=1.0, in1=v, op0=ALU.add, op1=ALU.mult
                                         ).then_inc(s_z, 1)

            mq_n = [0]

            def mean_squares(i):
                mq_n[0] += 1
                n = mq_n[0]
                ve.wait_ge(s_mqs, n)
                vec.tensor_scalar(qss[:, i, :], qss[:, i, :], 1.0 / 256, EPS, ALU.mult, ALU.add).then_inc(s_mqm, 1)
                ve.wait_ge(s_mqr, n)

            def do_mqs(i):
                mean_squares(i)
                vec.tensor_scalar(qrs[:, i, :], qss[:, i, :], 1.0 / 16, None, ALU.mult).then_inc(s_mqk, 1)

            def do_mks(i):
                mean_squares(4 + i)
                for t in range(T):
                    for hd in range(2):
                        v = proj[:, MQSLOT[4 + i], t, 256 * hd:256 * hd + 256]
                        ins = vec.tensor_scalar(v, v, qss[:, 4 + i, 2 * t + hd:2 * t + hd + 1], None, ALU.mult)
                ins.then_inc(s_mks, 1)

            def do_mas(n):
                i, hd2 = 2 * (n // 4) + (n % 4) // 2, n % 2
                ve.wait_ge(s_scp, n + 1)
                ve.wait_ge(s_mqk, i + 1)
                link(vec.tensor_reduce(smx[:, n, :], M[0][:, :].rearrange("p (t m) -> p t m", t=T), AX.X, ALU.max))
                vec.scalar_tensor_tensor(out=snb[:, n, :], in0=smx[:, n, :], scalar=-1.0, in1=qrs[:, i, hd2:4:2],
                                         op0=ALU.mult, op1=ALU.mult).then_inc(s_nb, 1)
                ve.wait_ge(s_exp, n + 1)
                link(vec.reciprocal(srs[:, n, :], ssm[:, n, :]))
                for t in range(T):
                    ins = vec.tensor_scalar(prob[:, t, :], prob[:, t, :], srs[:, n, t:t + 1], None, ALU.mult)
                ins.then_inc(s_pr, 1)

            def do_mao(m):
                ve.wait_ge(s_maop, m + 1)
                ve.wait_ge(s_z, (8 if m < 8 else 32) + m % 8 + 1)
                v = mix[:, 16 + m % 8, :]
                vec.scalar_tensor_tensor(out=v, in0=M[banks("mao", m)[0]][:, 0:S], scalar=0.5, in1=v, op0=ALU.mult,
                                         op1=ALU.mult
                                         ).then_inc(s_mao, 1)

            def do_sbn(g):
                for c in range(2):
                    ve.wait_ge(s_sbs, 2 * g + c + 1)
                    vec.tensor_reduce(bss[:, g, 8 * c:8 * c + 8], scr[:, :].rearrange("p (a n) -> p a n", n=128),
                                      AX.X, ALU.add).then_inc(s_sbr, 1)
                ve.wait_ge(s_sbr, 2 * g + 2)
                vec.tensor_scalar(bss[:, g, :], bss[:, g, :], 1.0 / 128, EPS, ALU.mult, ALU.add).then_inc(s_sbm, 1)

            def do_sbz(h):
                ve.wait_ge(s_sbA, h + 1)
                if h:
                    ve.wait_ge(s_sbcp, h)
                vec.scalar_tensor_tensor(out=spz, in0=M[1][:, 0:384], scalar=0.0, in1=absz, op0=ALU.max, op1=ALU.add
                                         ).then_inc(s_sbsp, 1)

            def do_sbo(h):
                ve.wait_ge(s_sbop, h + 1)
                ve.wait_ge(s_z, 16 + h + 1)
                v = mix[:, h, :]
                vec.scalar_tensor_tensor(out=v, in0=M[2][:, 0:S], scalar=0.5, in1=v, op0=ALU.mult, op1=ALU.mult
                                         ).then_inc(s_sbo, 1)

            steps = {"split": split, "evac": do_evac, "xt": do_xt, "mf": do_mf, "rstd": do_rstd,
                     "baw": do_baw, "bat": do_bat, "bas": do_bas,
                     "za": do_za, "dnC": do_dnC,
                     "dnU": do_dnU, "dnB": do_dnB, "dnV": do_dnV, "dnR": do_dnR, "dnG": do_dnG, "d4x": do_d4x,
                     "d4y": do_d4y, "d5c": do_d5c, "d5e": do_d5e, "d6": do_d6, "gate": do_gate, "glu": do_glu,
                     "conv": do_conv, "lnm": do_lnm, "lnr": do_lnr, "lno": do_lno, "zT": do_zT, "mqs": do_mqs,
                     "mks": do_mks, "mas": do_mas, "mao": do_mao, "sbn": do_sbn, "sbz": do_sbz, "sbo": do_sbo}
            ve.wait_ge(s_vt, 1)
            for st, i in plan:
                if st in steps:
                    steps[st](i)

        @block.tensor
        def _(pe):
            def take(st, i):
                for q in bank_free[st, i]:
                    pe.wait_ge(*q)

            def three(out_, k, t, hi, lo, first, last):
                xh, xl = xhi[:, k, 128 * t:128 * t + 128], xlo[:, k, 128 * t:128 * t + 128]
                mm(out_, xh, hi, start=first, stop=False)
                mm(out_, xh, lo, start=False, stop=False)
                return mm(out_, xl, hi, start=False, stop=last)

            def do_chunk(c):
                j = JOB_OF[c]
                kts, fill = JOBS[j][3], JOBS[j][4]
                i = c - CH0[j]
                if i == 0 and j >= 2:
                    pe.wait_ge(*evac_done(j - 2))
                if all(JOBS[q][4] != fill for q in range(j)):
                    pe.wait_ge(s_xl, fill + 2 * i + 2)
                pe.wait_ge(s_lo, c + 1)
                for k in (2 * i, 2 * i + 1):
                    for t in range(T):
                        ins = three(pj[j % 2][t][:, :], SLOT[fill + k], t, whi[:, c % RING, k % 2, :],
                                    wlo[:, c % RING, k % 2, :], k == 0, k == kts - 1)
                ins.then_inc(s_pe, 1)

            def turn(dst, src):
                return nc.tensor.transpose(dst, src, ident[:, :])

            def do_xt(n):
                if n < F_OA:
                    src, k = hid, n
                    pe.wait_ge(s_xin[k // 4], 16)
                elif n < F_OB:
                    src, k = memx, n - F_MEM
                    pe.wait_ge(s_min, 64)
                else:
                    src, k = hid, n - F_H
                    pe.wait_ge(*evac_done(J_OM + k // 4))
                take("xt", n)
                for t in range(T):
                    ins = turn(M[banks("xt", n)[0]][:, 128 * t:128 * t + 128], src[:, t, 128 * k:128 * k + 128])
                ins.then_inc(s_xp, 1)

            def do_vec(_):
                pe.wait_ge(s_vrow, 16 * 14)
                take("vec", 0)
                for a, n in enumerate((NVEC, 96, 128, 120)):
                    ins = nc.tensor.transpose(M[0][:, 128 * a:128 * a + n], vrow[0:n, a, :], ident[0:n, 0:n])
                ins.then_inc(s_vp, 1)

            def do_ba(_):
                pe.wait_ge(s_wbl, 1)
                pe.wait_ge(s_xl, 16)
                take("ba", 0)
                for k in range(KT):
                    for a, b in ((bah, xhi), (bal, xhi), (bah, xlo)):
                        ins = mm(M[0][0:16, 0:S], a[:, k, :], b[:, k, :], start=(k == 0 and a is bah and b is xhi),
                                 stop=(k == KT - 1 and b is xlo))
                ins.then_inc(s_bap, 1)

            def do_bat(_):
                pe.wait_ge(s_bac, 1)
                take("bat", 0)
                for t in range(T):
                    ins = nc.tensor.transpose(M[1][:, 16 * t:16 * t + 16], bar[:, 128 * t:128 * t + 128], ident[0:16, 0:16])
                ins.then_inc(s_batp, 1)

            def do_bas(_):
                pe.wait_ge(s_const, 2)
                pe.wait_ge(s_baD, 3)
                take("bas", 0)
                g = gl_in[:, :, :].rearrange("p t h -> p (t h)")
                mm(M[2][:, 0:16], upto[:, :], g, start=True, stop=True)
                mm(M[2][:, 16:32], ones[:, :], g, start=True, stop=True).then_inc(s_gcp, 1)

            def do_dnT(h):
                g = h // 4
                pe.wait_ge(*evac_done(J_V[g]))
                take("dnT", h)
                for c, slot in enumerate((PSLOT[J_Q[g]], PSLOT[J_K[g]], PSLOT[J_V[g]])):
                    for t in range(T):
                        o = 256 * (c % 2) + 128 * t
                        ins = turn(M[c // 2][:, o:o + 128], proj[:, slot, t, 128 * (h % 4):128 * (h % 4) + 128])
                ins.then_inc(s_dnT, 1)

            def do_dnB(h):
                pe.wait_ge(s_silu, 2 * h + 2)
                take("dnB", h)
                pe.wait_ge(s_sq, h + 1)
                for a in range(4):
                    ins = mm(M[2][:, 384 + a:385 + a], scr[:, 128 * a:128 * a + 128], ones[:, 0:1], start=True, stop=True)
                ins.then_inc(s_np, 1)
                y = ykqv[:, h % 4, :, :]
                turn(M[2][:, 0:128], y[:, 0, 0:128])
                turn(M[2][:, 128:256], y[:, 2, 0:128])
                turn(M[2][:, 256:384], y[:, 2, 128:256]).then_inc(s_back, 1)

            def do_dnR(g):
                pe.wait_ge(s_ei, g + 1)
                take("dnR", g)
                turn(M[1][0:24, 0:128], ei[:, g, 0:3, :].rearrange("p a m -> p (a m)")).then_inc(s_rp, 1)

            def do_dnG(h):
                g, hl = h // 4, h % 4
                pe.wait_ge(s_rows, g + 1)
                take("dnG", h)
                for t in range(T):
                    tc = slice(128 * t, 128 * t + 128)
                    mm(M[0][:, 256 * t:256 * t + 256].rearrange("p (c n) -> p c n", c=2), ykqv[:, hl, 0, tc],
                       ykqv[:, hl, 0:2, tc], start=True, stop=True)
                for t in range(T):
                    mm(M[1][:, 256 * t:256 * t + 256], identb[:, :], shut[:, :, :].rearrange("p c n -> p (c n)"),
                       start=(t == 0), stop=False, skip_group_check=True)
                    for c in range(2):
                        o = 256 * t + 128 * c
                        r = 16 * c + 2 * hl + t
                        ins = mm(M[1][:, o:o + 128], ident[0:24, r:r + 1].broadcast_to([24, 128]), rows[:, g, :],
                                 start=False, stop=True, skip_group_check=True)
                ins.then_inc(s_gp, 1)

            def do_d4x(i):
                pr, l = divmod(i, 7)
                g, par = divmod(pr, 2)
                pe.wait_ge(s_of[par], 7 * g + l + 1)
                if l:
                    pe.wait_ge(s_t[par], 7 * g + l)
                take("d4x", i)
                for m in range(4):
                    ins = mm(M[0][:, 128 * m:128 * m + 128], ofx[:, par, m, :], tinv[:, par, m, :] if l else ident[:, :],
                             start=True, stop=True)
                ins.then_inc(s_x1p[par], 1)

            def do_d4y(i):
                pr, l = divmod(i, 7)
                g, par = divmod(pr, 2)
                if l == 0:
                    return
                pe.wait_ge(s_x1[par], 6 * g + l)
                take("d4y", i)
                for m in range(4):
                    m1, m2 = (M[b][:, 64 * m:64 * m + 64].rearrange("p (b r) -> p b r", r=1 << l) for b in (1, 2))
                    x0, t1 = (v[:, par, m, :].rearrange("p (b c r) -> p b c r", c=2, r=1 << l) for v in (ofx, tinvt))
                    if l < 6:
                        mm(m1, tinvt[:, par, m, :], x0[:, :, 0, :], start=True, stop=True)
                    ins = mm(m2, ofx[:, par, m, :], t1[:, :, 1, :], start=True, stop=True)
                ins.then_inc(s_x2p[par], 1)

            def inverse(h, t):
                return tinvt[:, (h % 4) // 2, 2 * (h % 2) + t, :]

            def do_d5a(h):
                pe.wait_ge(s_tks, h + 1)
                pe.wait_ge(s_t[(h % 4) // 2], 7 * (h // 4) + 7)
                take("d5a", h)
                mm(M[0][:, 0:128], inverse(h, 0), tok[:, h % 4, 1, :], start=True, stop=True).then_inc(s_5ap, 1)

            def do_d5b(h):
                pe.wait_ge(s_5a, h + 1)
                take("d5b", h)
                mm(M[1][:, 0:128], tok[:, h % 4, 0, :], dw[h % 2][:, 0, :], start=True, stop=True)
                mm(M[1][:, 128:256], aq[:, 2 * (h % 4), 1, :], dw[h % 2][:, 0, :], start=True, stop=True).then_inc(s_5bp, 1)

            def do_d5c(h):
                pe.wait_ge(s_5b, h + 1)
                take("d5c", h)
                mm(M[2][:, 0:128], ykqv[:, h % 4, 0, 128:256], dw[h % 2][:, 1, :], start=True, stop=True)
                mm(M[2][:, 128:256], ykqv[:, h % 4, 1, 128:256], dw[h % 2][:, 1, :], start=True, stop=True).then_inc(s_5cp, 1)

            def do_d5d(h):
                pe.wait_ge(s_5c, h + 1)
                take("d5d", h)
                mm(M[0][:, 0:128], inverse(h, 1), tok[:, h % 4, 2, :], start=True, stop=True).then_inc(s_5dp, 1)

            def do_d5e(h):
                pe.wait_ge(s_5d, h + 1)
                take("d5e", h)
                mm(M[1][:, 0:128], aq[:, 2 * (h % 4) + 1, 1, :], dw[h % 2][:, 2, :], start=True, stop=True).then_inc(s_5ep, 1)

            def do_d7(h):
                pe.wait_ge(s_ow, 2 * h + 2)
                take("d7", h)
                for t in range(T):
                    ins = turn(M[2][:, 128 * t:128 * t + 128], tok[:, h % 4, t, :])
                ins.then_inc(s_owp, 1)

            def do_gT(ct):
                i = ct // 4
                pe.wait_ge(s_glu, i + 1)
                take("gT", ct)
                for t in range(T):
                    ins = turn(M[3][:, 128 * t:128 * t + 128], proj[:, PSLOT[J_GLU[i]], t, 128 * (ct % 4):128 * (ct % 4) + 128])
                ins.then_inc(s_gtp, 1)

            def do_lnm(_):
                pe.wait_ge(s_cv, 8 * TAPS)
                take("lnm", 0)
                for ct in range(8):
                    ins = mm(M[3][:, 0:S], ones[:, :], cvr[:, ct, :], start=(ct == 0), stop=(ct == 7))
                ins.then_inc(s_mup, 1)

            def do_lnv(ct):
                pe.wait_ge(s_lsq, ct + 1)
                take("lnv", ct)
                mm(M[3][:, 0:S], ones[:, :], cvr[:, 8 + ct % 2, :], start=(ct == 0), stop=(ct == 7)).then_inc(s_lvp, 1)

            def do_zT(n):
                j, slot, col, _ = zsource(n)
                pe.wait_ge(*evac_done(j))
                take("zT", n)
                for t in range(T):
                    ins = turn(M[3][:, 128 * t:128 * t + 128], proj[:, slot, t, 128 * col:128 * col + 128])
                ins.then_inc(s_zp, 1)

            def do_mqT(dt):
                i = dt // 4
                pe.wait_ge(*evac_done(MQJOB[i]))
                take("mqT", dt)
                for t in range(T):
                    ins = turn(M[dt % 2][:, 128 * t:128 * t + 128],
                               proj[:, MQSLOT[i], t, 128 * (dt % 4):128 * (dt % 4) + 128])
                ins.then_inc(s_mqp, 1)

            def do_mkT(dt):
                i = dt // 4
                pe.wait_ge(s_mks, i + 1)
                take("mkT", dt)
                for t in range(T):
                    ins = turn(M[dt % 2][:, 128 * t:128 * t + 128],
                               proj[:, MQSLOT[4 + i], t, 128 * (dt % 4):128 * (dt % 4) + 128])
                ins.then_inc(s_mkp, 1)

            def do_mas(n):
                hd = n % 4
                pe.wait_ge(s_mqT, 8 * (n // 4) + 2 * hd + 2)
                pe.wait_ge(s_mkT, 2 * hd + 2)
                take("mas", n)
                for t in range(T):
                    for dt in range(2):
                        ins = mm(M[0][:, 256 * t:256 * t + 256], qmt[n // 4][:, 2 * hd + dt, 128 * t:128 * t + 128],
                                 kmt[:, 2 * hd + dt, :], start=(dt == 0), stop=(dt == 1))
                ins.then_inc(s_scp, 1)

            def do_mat(n):
                pe.wait_ge(s_pr, n + 1)
                take("mat", n)
                for m in range(2):
                    for t in range(T):
                        ins = turn(M[1][:, 256 * m + 128 * t:256 * m + 128 * t + 128], prob[:, t, 128 * m:128 * m + 128])
                ins.then_inc(s_ptp, 1)

            def do_mao(m):
                n, dt = divmod(m, 2)
                hd = n % 4
                pe.wait_ge(s_pt, n + 1)
                pe.wait_ge(*evac_done(J_MEM + 2 + hd // 2))
                take("mao", m)
                for mt in range(2):
                    o = 256 * hd + 128 * dt
                    ins = mm(M[banks("mao", m)[0]][:, 0:S], vm[:, mt, o:o + 128], probt[:, mt, :],
                             start=(mt == 0), stop=(mt == 1))
                ins.then_inc(s_maop, 1)

            def do_sbT(h):
                pe.wait_ge(s_sbn, 2 * (h // 4) + 2)
                take("sbT", h)
                for c in range(2):
                    for t in range(T):
                        o = 256 * c + 128 * t
                        ins = turn(M[0][:, o:o + 128], proj[:, c, t, 128 * (h % 4):128 * (h % 4) + 128])
                ins.then_inc(s_sbtp, 1)

            def do_sbz(h):
                pe.wait_ge(s_sbT, h + 1)
                take("sbz", h)
                q, k = qk[:, h % 4, 0, :], qk[:, h % 4, 1, :]
                mm(M[1][:, 0:S], k[:, 0:128], q[:, 0:S], start=True, stop=False, skip_group_check=True)
                mm(M[1][:, S:384], k[:, 128:S], q[:, 128:S], start=False, stop=False, skip_group_check=True
                   ).then_inc(s_sbzp, 1)

            def do_sbc(h):
                pe.wait_ge(s_sbmk, h + 1)
                for a, b, lhs, rhs in ((0, 256, negfrom, spz[:, 0:256]), (256, 384, negfrom, spz[:, 256:384]),
                                       (128, 256, negones, spz[:, 256:384]), (0, 128, identb, shut[:, 0, :]),
                                       (256, 384, identb, shut[:, 0, :])):
                    ins = mm(M[1][:, a:b], lhs[:, :], rhs, start=False, stop=(a == 256), skip_group_check=True)
                ins.then_inc(s_sbcp, 1)

            def do_sbo(h):
                pe.wait_ge(s_sbW, h + 1)
                pe.wait_ge(*evac_done(J_ODIN + 4 * (h // 4) + 2))
                take("sbo", h)
                v = proj[:, 2, :, 128 * (h % 4):128 * (h % 4) + 128]
                mm(M[2][:, 0:S], v[:, 0, :], wts[:, 0:256], start=True, stop=False, skip_group_check=True)
                mm(M[2][:, 128:S], v[:, 1, :], wts[:, 256:384], start=False, stop=True, skip_group_check=True
                   ).then_inc(s_sbop, 1)

            steps = {"chunk": do_chunk, "xt": do_xt, "vec": do_vec, "ba": do_ba, "bat": do_bat, "bas": do_bas,
                     "dnT": do_dnT, "dnB": do_dnB, "dnR": do_dnR,
                     "dnG": do_dnG, "d4x": do_d4x, "d4y": do_d4y, "d5a": do_d5a, "d5b": do_d5b, "d5c": do_d5c,
                     "d5d": do_d5d, "d5e": do_d5e, "d7": do_d7, "gT": do_gT, "lnm": do_lnm, "lnv": do_lnv,
                     "zT": do_zT, "mqT": do_mqT, "mkT": do_mkT, "mas": do_mas, "mat": do_mat, "mao": do_mao,
                     "sbT": do_sbT, "sbz": do_sbz, "sbc": do_sbc, "sbo": do_sbo}
            pe.wait_ge(s_const, 1)
            pe.wait_ge(s_gain, 16)
            nc.tensor.transpose(M[0][:, 0:16], vrow[0:16, 0, :], ident[0:16, 0:16]).then_inc(s_vp, 1)
            for st, i in plan:
                if st in steps:
                    steps[st](i)


INS = ["x", "mem", "mem_norm_g", "w_mem_kv", "mem_k_norm_g", "ev_norm_g", "ev_w_in", "ev_conv_qkv", "ev_a_log",
       "ev_dt_bias", "ev_dn_norm_g", "ev_dw_w", "ev_dw_b", "ev_ln_g", "ev_ln_b", "ev_q_norm_m", "ev_w_out",
       "od_norm_g", "od_w_in", "od_q_norm_c", "od_k_norm_c", "od_q_norm_m", "od_w_out"]
LAST = len(JOBS)


def kernel(**inputs):
    import numpy as np
    import concourse.bacc as bacc
    from concourse.bass_utils import run_bass_kernel_spmd

    nc = bacc.Bacc("TRN2", target_bir_lowering=False, num_devices=1)
    arrays, d = {}, {}
    for name in INS:
        a = np.ascontiguousarray(inputs[name])
        arrays[f"in_{name}_dram"] = a
        d[name] = nc.dram_tensor(f"in_{name}_dram", a.shape, mybir.dt.from_np(a.dtype), kind="ExternalInput").ap()
    out = nc.dram_tensor("out_dram", (1, S, D), F32, kind="ExternalOutput").ap()

    def vecs(vrow):
        rows = []
        for name, n in VEC:
            v = d[name]
            v = v[0, :] if len(v.shape) == 2 else v
            rows.append((vrow[VCOL[name]:VCOL[name] + n, 0, :], v.rearrange("(k p) -> k p", p=128)))
        rows.append((vrow[0:96, 1, :], d["ev_conv_qkv"][0, :, :].rearrange("k (c p) -> (k c) p", p=128)))
        dw = d["ev_dw_w"][0, :, :].rearrange("k (c p) -> (k c) p", p=128)
        return rows + [(vrow[0:128, 2, :], dw[0:128, :]), (vrow[0:120, 3, :], dw[128:248, :])]

    w = {"ev_in": d["ev_w_in"][0, :, :], "mem": d["w_mem_kv"], "ev_out": d["ev_w_out"][0, :, :],
         "od_in": d["od_w_in"][0, :, :], "od_out": d["od_w_out"][0, :, :]}
    prog(nc, d["x"][0, :, :], d["mem"][0, :, :], vecs, w, d["ev_a_log"][0, :], d["ev_dt_bias"][0, :],
         out[0, :, :], LAST)
    r = run_bass_kernel_spmd(nc, [arrays], core_ids=[0])
    return r.results[0]["out_dram"]
```
